# Optimizing a Trainium2 kernel written in Bass

```python
import math
import jax, jax.numpy as jnp
from jax import lax
import numpy as np

D_MODEL = 1024
BATCH = 1
SEQ = 256
DEPTH = 1

HEAD_DIM = 64
NSA_HEADS = 8
NSA_KV_GROUPS = 2
NSA_Q_PER_GROUP = NSA_HEADS // NSA_KV_GROUPS
NSA_WIDTH = NSA_HEADS * HEAD_DIM
KV_WIDTH = NSA_KV_GROUPS * HEAD_DIM
CMP_BLOCK = 32
CMP_STRIDE = 16
SEL_BLOCK = 64
SEL_TOPN = 8
FORCE_BONUS = 1000.0
WINDOW = 512
Q_BLOCK = 128
SEL_Q_BLOCK = 64
POOL_WINDOWS = (2, 4, 8, 16)
POOL_GROUP = 64
POOL_WIDTH = POOL_GROUP * len(POOL_WINDOWS)
MEM_HEADS = 4
MEM_WIDTH = MEM_HEADS * HEAD_DIM
N_BRANCH = 3
IN_WIDTHS = (NSA_WIDTH, 6 * KV_WIDTH, 3 * NSA_HEADS, POOL_WIDTH, MEM_WIDTH, N_BRANCH * D_MODEL)
IN_WIDTH = NSA_WIDTH + 6 * KV_WIDTH + 3 * NSA_HEADS + POOL_WIDTH + MEM_WIDTH + N_BRANCH * D_MODEL
N_EXPERTS = 32
TOP_K = 4
D_FF = 1024
SWIGLU_LIMIT = 7.0
SWIGLU_ALPHA = 1.702
ROPE_THETA = 10000.0
EPS = 1e-5
NEG_INF = -1e30
TINY = 1e-30

kernel_name = "hybrid_nsa_pool_memxattn_moe"

def rms_norm(x, g):
    xf = x.astype(jnp.float32)
    y = xf * lax.rsqrt(jnp.mean(xf * xf, axis=-1, keepdims=True) + EPS)
    return (y * g.astype(jnp.float32)).astype(x.dtype)

def rope(x, pos):
    half = HEAD_DIM // 2
    inv = ROPE_THETA ** (-jnp.arange(half, dtype=jnp.float32) / half)
    ang = pos.astype(jnp.float32)[:, None] * inv[None, :]
    cos = jnp.cos(ang)[None, :, None, :]
    sin = jnp.sin(ang)[None, :, None, :]
    xf = x.astype(jnp.float32)
    x1, x2 = xf[..., :half], xf[..., half:]
    return jnp.concatenate([x1 * cos - x2 * sin, x2 * cos + x1 * sin], axis=-1).astype(x.dtype)

def masked_softmax(s, mask):
    s = jnp.where(mask, s.astype(jnp.float32), NEG_INF)
    m = jnp.max(s, axis=-1, keepdims=True)
    e = jnp.where(mask, jnp.exp(s - m), 0.0)
    return e / jnp.maximum(jnp.sum(e, axis=-1, keepdims=True), TINY)

def nsa_compressed(q, k, v, cmp_pos, cmp_w1, cmp_w2):
    B, S = q.shape[0], q.shape[1]
    nc = (S - CMP_BLOCK) // CMP_STRIDE + 1
    tok = jnp.arange(nc)[:, None] * CMP_STRIDE + jnp.arange(CMP_BLOCK)[None, :]

    def compress(t, i):
        blk = t[:, tok] + cmp_pos[i][None, None, :, None, :]
        hid = jax.nn.silu(jnp.einsum('bnlgd,lde->bnge', blk, cmp_w1[i]))
        return jnp.einsum('bnge,ef->bngf', hid, cmp_w2[i])

    kc = compress(k, 0)
    vc = compress(v, 1)
    qg = q.reshape(B, S, NSA_KV_GROUPS, NSA_Q_PER_GROUP, HEAD_DIM)
    s = jnp.einsum('bsghd,bngd->bghsn', qg, kc) * (HEAD_DIM ** -0.5)
    t = jnp.arange(S)
    blk_end = jnp.arange(nc) * CMP_STRIDE + CMP_BLOCK - 1
    mask = blk_end[None, :] <= t[:, None]
    p = masked_softmax(s, mask)
    o = jnp.einsum('bghsn,bngd->bsghd', p.astype(vc.dtype), vc)
    return o, jnp.sum(p, axis=2)

def nsa_select_indices(p_grp, S):
    nc = p_grp.shape[-1]
    nsb = S // SEL_BLOCK
    i = jnp.arange(nc)
    j = jnp.arange(nsb)
    overlap = ((i[:, None] * CMP_STRIDE <= j[None, :] * SEL_BLOCK + SEL_BLOCK - 1)
               & (i[:, None] * CMP_STRIDE + CMP_BLOCK - 1 >= j[None, :] * SEL_BLOCK)).astype(jnp.float32)
    score = jnp.einsum('bgsn,nj->bgsj', p_grp, overlap)
    t = jnp.arange(S)
    cur = t // SEL_BLOCK
    valid = j[None, :] * SEL_BLOCK <= t[:, None]
    forced = (j[None, :] == 0) | (j[None, :] == cur[:, None]) | (j[None, :] == cur[:, None] - 1)
    score = jnp.where(valid, score + jnp.where(forced, FORCE_BONUS, 0.0), -1.0)
    _, idx = lax.top_k(score, min(SEL_TOPN, nsb))
    return idx

def nsa_selected(q, k, v, idx):
    B, S = q.shape[0], q.shape[1]
    n = idx.shape[-1]
    nsb = S // SEL_BLOCK
    kb = k.reshape(B, nsb, SEL_BLOCK, NSA_KV_GROUPS, HEAD_DIM).transpose(0, 3, 1, 2, 4)
    vb = v.reshape(B, nsb, SEL_BLOCK, NSA_KV_GROUPS, HEAD_DIM).transpose(0, 3, 1, 2, 4)
    gather = jax.vmap(jax.vmap(lambda tbl, ids: tbl[ids]))
    m_len = n * SEL_BLOCK

    def chunk(c):
        start = c * SEL_Q_BLOCK
        qc = lax.dynamic_slice_in_dim(q, start, SEL_Q_BLOCK, axis=1).reshape(
            B, SEL_Q_BLOCK, NSA_KV_GROUPS, NSA_Q_PER_GROUP, HEAD_DIM)
        ic = lax.dynamic_slice_in_dim(idx, start, SEL_Q_BLOCK, axis=2)
        flat = ic.reshape(B, NSA_KV_GROUPS, SEL_Q_BLOCK * n)
        kg = gather(kb, flat).reshape(B, NSA_KV_GROUPS, SEL_Q_BLOCK, m_len, HEAD_DIM)
        vg = gather(vb, flat).reshape(B, NSA_KV_GROUPS, SEL_Q_BLOCK, m_len, HEAD_DIM)
        kpos = (ic[..., None] * SEL_BLOCK + jnp.arange(SEL_BLOCK)).reshape(B, NSA_KV_GROUPS, SEL_Q_BLOCK, m_len)
        qpos = start + jnp.arange(SEL_Q_BLOCK)
        mask = (kpos <= qpos[:, None])[:, :, None]
        s = jnp.einsum('bqghd,bgqmd->bghqm', qc, kg) * (HEAD_DIM ** -0.5)
        p = masked_softmax(s, mask)
        return jnp.einsum('bghqm,bgqmd->bqghd', p.astype(vg.dtype), vg)

    o = lax.map(chunk, jnp.arange(S // SEL_Q_BLOCK))
    return o.transpose(1, 0, 2, 3, 4, 5).reshape(B, S, NSA_KV_GROUPS, NSA_Q_PER_GROUP, HEAD_DIM)

def nsa_window(q, k, v):
    B, S = q.shape[0], q.shape[1]
    kp = jnp.pad(k, ((0, 0), (WINDOW, 0), (0, 0), (0, 0)))
    vp = jnp.pad(v, ((0, 0), (WINDOW, 0), (0, 0), (0, 0)))
    span = WINDOW + Q_BLOCK

    def chunk(c):
        start = c * Q_BLOCK
        qc = lax.dynamic_slice_in_dim(q, start, Q_BLOCK, axis=1).reshape(
            B, Q_BLOCK, NSA_KV_GROUPS, NSA_Q_PER_GROUP, HEAD_DIM)
        kc = lax.dynamic_slice_in_dim(kp, start, span, axis=1)
        vc = lax.dynamic_slice_in_dim(vp, start, span, axis=1)
        qpos = start + jnp.arange(Q_BLOCK)
        kpos = start - WINDOW + jnp.arange(span)
        diff = qpos[:, None] - kpos[None, :]
        mask = (diff >= 0) & (diff < WINDOW) & (kpos[None, :] >= 0)
        s = jnp.einsum('bqghd,bkgd->bghqk', qc, kc) * (HEAD_DIM ** -0.5)
        p = masked_softmax(s, mask)
        return jnp.einsum('bghqk,bkgd->bqghd', p.astype(vc.dtype), vc)

    o = lax.map(chunk, jnp.arange(S // Q_BLOCK))
    return o.transpose(1, 0, 2, 3, 4, 5).reshape(B, S, NSA_KV_GROUPS, NSA_Q_PER_GROUP, HEAD_DIM)

def pool_mixer(u, w_pool, pool_scale):
    B, S, _ = u.shape
    uf = u.astype(jnp.float32)
    c = jnp.pad(jnp.cumsum(uf, axis=1), ((0, 0), (1, 0), (0, 0)))
    t = jnp.arange(S)
    groups = []
    for gi, w in enumerate(POOL_WINDOWS):
        sl = slice(gi * POOL_GROUP, (gi + 1) * POOL_GROUP)
        lo = jnp.maximum(t + 1 - w, 0)
        cg = c[..., sl]
        cnt = (t + 1 - lo).astype(jnp.float32)
        groups.append((cg[:, t + 1] - cg[:, lo]) / cnt[None, :, None] - uf[..., sl])
    z = jnp.stack(groups, axis=2)
    z = jnp.einsum('bsgc,gce->bsge', z, w_pool.astype(jnp.float32)).reshape(B, S, POOL_WIDTH)
    return (z * pool_scale.astype(jnp.float32)).astype(u.dtype)

def memory_xattn(q, mem_n, w_mem_kv):
    B, S, _ = q.shape
    M = mem_n.shape[1]
    kv = (mem_n @ w_mem_kv).reshape(B, M, 2, MEM_HEADS, HEAD_DIM)
    qh = q.reshape(B, S, MEM_HEADS, HEAD_DIM)
    s = jnp.einsum('bshd,bmhd->bhsm', qh, kv[:, :, 0]) * (HEAD_DIM ** -0.5)
    p = jax.nn.softmax(s.astype(jnp.float32), axis=-1)
    o = jnp.einsum('bhsm,bmhd->bshd', p.astype(kv.dtype), kv[:, :, 1])
    return o.reshape(B, S, MEM_WIDTH)

def clamped_swiglu(gu):
    gate, up = gu[..., :D_FF], gu[..., D_FF:]
    gate = jnp.minimum(gate, SWIGLU_LIMIT)
    up = jnp.clip(up, -SWIGLU_LIMIT, SWIGLU_LIMIT)
    return (up + 1.0) * (gate * jax.nn.sigmoid(SWIGLU_ALPHA * gate))

def moe_ffn(h, w_router, b_router, w_gate_up, b_gate_up, w_down, b_down):
    B, S, D = h.shape
    hf = h.reshape(B * S, D)
    logits = (hf @ w_router + b_router).astype(jnp.float32)
    top_val, top_idx = lax.top_k(logits, TOP_K)
    weights = jax.nn.softmax(top_val, axis=-1)
    combine = jnp.sum(jax.nn.one_hot(top_idx, N_EXPERTS, dtype=jnp.float32) * weights[..., None], axis=1)
    out = jnp.zeros_like(hf)
    for e in range(N_EXPERTS):
        y = clamped_swiglu(hf @ w_gate_up[e] + b_gate_up[e]) @ w_down[e] + b_down[e]
        out = out + combine[:, e:e + 1].astype(hf.dtype) * y
    return out.reshape(B, S, D)

def setup_inputs(seed: int = 0) -> dict:
    key = jax.random.key(seed)
    ks = jax.random.split(key, 24)
    f32 = jnp.float32

    def nrm(k, shape, scale):
        return jax.random.normal(k, shape, f32) * scale

    L = DEPTH
    return {
        "x": nrm(ks[0], (BATCH, SEQ, D_MODEL), 1.0),
        "mem": nrm(ks[1], (BATCH, 256, D_MODEL), 1.0),
        "norm_mix": 1.0 + nrm(ks[2], (L, D_MODEL), 0.02),
        "norm_mem": 1.0 + nrm(ks[3], (L, D_MODEL), 0.02),
        "w_in": nrm(ks[4], (L, D_MODEL, IN_WIDTH), D_MODEL ** -0.5),
        "cmp_pos": nrm(ks[5], (L, 2, CMP_BLOCK, HEAD_DIM), 0.1),
        "cmp_w1": nrm(ks[6], (L, 2, CMP_BLOCK, HEAD_DIM, HEAD_DIM), (CMP_BLOCK * HEAD_DIM) ** -0.5),
        "cmp_w2": nrm(ks[7], (L, 2, HEAD_DIM, HEAD_DIM), HEAD_DIM ** -0.5),
        "w_pool": nrm(ks[8], (L, len(POOL_WINDOWS), POOL_GROUP, POOL_GROUP), POOL_GROUP ** -0.5),
        "pool_scale": 1.0 + nrm(ks[9], (L, POOL_WIDTH), 0.02),
        "w_mem_kv": nrm(ks[10], (L, D_MODEL, 2 * MEM_WIDTH), D_MODEL ** -0.5),
        "w_up_nsa": nrm(ks[11], (L, NSA_WIDTH, D_MODEL), NSA_WIDTH ** -0.5),
        "w_up_pool": nrm(ks[12], (L, POOL_WIDTH, D_MODEL), POOL_WIDTH ** -0.5),
        "w_up_mem": nrm(ks[13], (L, MEM_WIDTH, D_MODEL), MEM_WIDTH ** -0.5),
        "w_out": nrm(ks[14], (L, D_MODEL, D_MODEL), D_MODEL ** -0.5),
        "norm_ffn": 1.0 + nrm(ks[15], (L, D_MODEL), 0.02),
        "w_router": nrm(ks[16], (L, D_MODEL, N_EXPERTS), D_MODEL ** -0.5),
        "b_router": nrm(ks[17], (L, N_EXPERTS), 0.01),
        "w_gate_up": nrm(ks[18], (L, N_EXPERTS, D_MODEL, 2 * D_FF), D_MODEL ** -0.5),
        "b_gate_up": nrm(ks[19], (L, N_EXPERTS, 2 * D_FF), 0.01),
        "w_down": nrm(ks[20], (L, N_EXPERTS, D_FF, D_MODEL), D_FF ** -0.5),
        "b_down": nrm(ks[21], (L, N_EXPERTS, D_MODEL), 0.01),
        "norm_final": 1.0 + nrm(ks[22], (D_MODEL,), 0.02),
    }

def reference(x, mem, norm_mix, norm_mem, w_in, cmp_pos, cmp_w1, cmp_w2, w_pool, pool_scale,
              w_mem_kv, w_up_nsa, w_up_pool, w_up_mem, w_out, norm_ffn, w_router, b_router,
              w_gate_up, b_gate_up, w_down, b_down, norm_final):
    B, S, D = x.shape
    pos = jnp.arange(S)
    split_points = []
    acc = 0
    for w in IN_WIDTHS[:-1]:
        acc += w
        split_points.append(acc)

    for l in range(DEPTH):
        h = rms_norm(x, norm_mix[l])
        proj = h @ w_in[l]
        q, kv, nsa_gate, pool_in, q_mem, merge_gate = jnp.split(proj, split_points, axis=-1)
        q = q.reshape(B, S, NSA_HEADS, HEAD_DIM)
        kv = kv.reshape(B, S, 6, NSA_KV_GROUPS, HEAD_DIM)
        k_cmp, v_cmp = kv[:, :, 0], kv[:, :, 1]
        k_sel, v_sel = rope(kv[:, :, 2], pos), kv[:, :, 3]
        k_win, v_win = rope(kv[:, :, 4], pos), kv[:, :, 5]
        q_rot = rope(q, pos)

        o_cmp, p_grp = nsa_compressed(q, k_cmp, v_cmp, cmp_pos[l], cmp_w1[l], cmp_w2[l])
        sel_idx = nsa_select_indices(p_grp, S)
        o_sel = nsa_selected(q_rot, k_sel, v_sel, sel_idx)
        o_win = nsa_window(q_rot, k_win, v_win)
        g = jax.nn.sigmoid(nsa_gate.astype(jnp.float32)).astype(x.dtype).reshape(
            B, S, NSA_KV_GROUPS, NSA_Q_PER_GROUP, 3)
        o_nsa = (g[..., 0:1] * o_cmp + g[..., 1:2] * o_sel + g[..., 2:3] * o_win).reshape(B, S, NSA_WIDTH)

        o_pool = pool_mixer(pool_in, w_pool[l], pool_scale[l])

        o_mem = memory_xattn(q_mem, rms_norm(mem, norm_mem[l]), w_mem_kv[l])

        mg = jax.nn.sigmoid(merge_gate.astype(jnp.float32)).astype(x.dtype).reshape(B, S, N_BRANCH, D)
        merged = (mg[:, :, 0] * (o_nsa @ w_up_nsa[l])
                  + mg[:, :, 1] * (o_pool @ w_up_pool[l])
                  + mg[:, :, 2] * (o_mem @ w_up_mem[l]))
        x = x + merged @ w_out[l]

        x = x + moe_ffn(rms_norm(x, norm_ffn[l]), w_router[l], b_router[l],
                        w_gate_up[l], b_gate_up[l], w_down[l], b_down[l])

    return rms_norm(x, norm_final)


_drawn_inputs = setup_inputs


def setup_inputs(seed=0):
    import zlib

    import numpy as np

    out = dict(_drawn_inputs(seed))
    spreads = {}
    factors = {'norm_mem': 6.997,
     'b_gate_up': 28.413,
     'b_down': 32.602,
     'norm_final': 7.99,
     'cmp_pos': 8.0,
     'pool_scale': 8.0,
     'norm_ffn': 3.609,
     'b_router': 7.311}
    for name, (base, spread) in spreads.items():
        noise = np.random.default_rng([zlib.crc32(name.encode()), seed]).standard_normal(out[name].shape)
        drawn = base * np.exp(spread * noise) if base else spread * noise
        out[name] = __import__('jax').numpy.asarray(drawn.astype(out[name].dtype))
    for name, factor in factors.items():
        out[name] = (out[name] * factor).astype(out[name].dtype)
    return out
```

```python
from contextlib import ExitStack

import numpy as np

import concourse.bass as bass
from concourse import mybir

F32 = mybir.dt.float32
F32R = mybir.dt.float32r
BF16 = mybir.dt.bfloat16
I32 = mybir.dt.int32
U32 = mybir.dt.uint32
ALU = mybir.AluOpType
ACT = mybir.ActivationFunctionType
AX = mybir.AxisListType.X

P = 128
D = 1024
T = 256
KD = D // P
NT = T // P
HD = 64
HEADS = 8
GROUPS = 2
MEM_HEADS = 4
SCALE = HD ** -0.5
CMP_BLOCK, CMP_STRIDE = 32, 16
NC = (T - CMP_BLOCK) // CMP_STRIDE + 1
CP = 32
POOL_WINDOWS = (2, 4, 8, 16)
PAD = 16
EPS = 1e-5
NEG = -1e30
TINY = 1e-30
LIMIT, ALPHA = 7.0, 1.702
NE = 32
FF = 1024
TOPK = 4
SLOTS = 64
ROUNDS = T // SLOTS
NCOL = ROUNDS * NE

Q0, KV0, NG0, PO0, QM0, MG0 = 0, 512, 1280, 1304, 1560, 1816
NGATE = 3 * HEADS

CONSTS = {}


def _lay_out():
    at = 0
    for name, n in (("ident", P), ("cos", T), ("sin", T), ("swap", P), ("pinv", 2 * T), ("slot", P),
                    ("iota", NE), ("seen", NT * NC), ("b_ident", P), ("b_causal", P), ("b_before", P),
                    ("b_ones", P), ("b_cmp", NT * NC), ("b_expert", NE)):
        CONSTS[name] = (at, at + n)
        at += n
    return at


NCONST = _lay_out()
NF = CONSTS["b_ident"][0]


def constants():
    c = np.zeros((P, NCONST), np.float32)

    def put(name, a):
        lo, hi = CONSTS[name]
        c[:, lo:hi] = np.asarray(a, np.float32).reshape(P, hi - lo)

    p = np.arange(P)
    half = HD // 2
    inv = np.float32(10000.0) ** (-np.arange(half, dtype=np.float32) / np.float32(half))
    ang = (np.arange(T, dtype=np.float32)[None, :] * inv.astype(np.float32)[p % half][:, None]).astype(np.float32)
    put("ident", np.eye(P))
    put("b_ident", np.eye(P))
    put("cos", np.cos(ang.astype(np.float64)))
    put("sin", np.sin(ang.astype(np.float64)))
    swap = np.zeros((P, P))
    for m in range(P):
        first = m % HD < half
        swap[m + half if first else m - half, m] = -1.0 if first else 1.0
    put("swap", swap)
    pinv = np.zeros((P, 2, T))
    for j in range(2):
        for g in range(2):
            pinv[64 * g:64 * g + 64, j] = 1.0 / np.minimum(np.arange(T) + 1, POOL_WINDOWS[2 * j + g])
    put("pinv", pinv)
    put("slot", np.tile(np.arange(P) % SLOTS, (P, 1)))
    put("iota", np.tile(np.arange(NE), (P, 1)))
    tok = np.arange(NT)[None, :, None] * P + p[:, None, None]
    seen = (np.arange(NC) * CMP_STRIDE + CMP_BLOCK - 1)[None, None, :] <= tok
    put("seen", seen)
    put("b_cmp", np.where(seen, 0.0, NEG))
    put("b_causal", np.where(p[None, :] <= p[:, None], 0.0, NEG))
    put("b_before", p[:, None] < p[None, :])
    put("b_ones", np.ones((P, P)))
    put("b_expert", (p[:, None] % NE == np.arange(NE)[None, :]) & (p[:, None] < 3 * NE))
    return c


UNITS = [("nsa", h, v) for h in range(HEADS) for v in range(2)] + [("mem", h, 0) for h in range(MEM_HEADS)]
NU = len(UNITS)
NMG = 12


def fillers(u):
    return range(NMG * u // NU, NMG * (u + 1) // NU)


CHUNKS = [(w, kh) for w in ("q", "kv1", "kv2", "pq", "memkv") for kh in range(2)]
CHUNKS += [(f"mg{j}", kh) for j in range(6) for kh in range(2)]
CHUNKS += [("upn", 0), ("uppm", 0), ("upn", 1), ("uppm", 1)]
CHUNKS += [("out", i) for i in range(4)]
RAW = 6
EXPERT_CHUNKS = 12
SPLIT = 3
assert len(CHUNKS) % RAW == 0 and EXPERT_CHUNKS % RAW == 0 and EXPERT_CHUNKS % SPLIT == 0


def job_order():
    jobs, turn = [], [0]

    def work(*names):
        for n in names:
            jobs.append((n, 2 + turn[0] % 6))
            turn[0] += 1

    work("vec", "xT0", "xT1", "xT2", "xT3", "qA", "qB", "kcv", "ksw", "vsw", "ng", "pool", "qm",
         "swA", "swB", "swk", "mT0", "mT1", "mT2", "mT3", "km", "vm", "hid", "kcvc", "zp",
         "cs00", "cs01", "cs10", "cs11", "S0", "S1", "ct")
    for u in range(NU):
        if u + 2 < NU:
            work(f"S{u + 2}")
        work(f"T{u}")
        work(*[f"mg{j}" for j in fillers(u)])
        if u >= 1 and first_of_pair(u - 1):
            pair = pair_of(u - 1)
            jobs.append((f"o{pair}", pair % 2))
    work(*[f"up{b}{q}" for q in range(4) for b in range(3)])
    jobs.extend((f"acc{b}", b) for b in range(4))
    turn[0] = 0
    for n in ("hT0", "hT1", "hT2", "hT3", "lg", "cs", "cnt", "cbT"):
        jobs.append((n, 4 + turn[0] % 4))
        turn[0] += 1
    return jobs


def pair_of(u):
    kind, h, _ = UNITS[u]
    return h // 2 + (4 if kind == "mem" else 0)


def first_of_pair(u):
    return UNITS[u][1] % 2 == 0 and UNITS[u][2] == 0


def last_of_pair(u):
    return UNITS[u][1] % 2 == 1 and UNITS[u][2] == (UNITS[u][0] == "nsa")


def spans(kind):
    return [(0, T), (T, 2 * T)] if kind == "mem" else [(0, P), (P, P + T)]


def transposed(kind):
    if kind == "mem":
        return [(t * T + k * P, k * T + t * P) for k in range(2) for t in range(NT)]
    return [(0, 0), (P, P), (2 * P, 2 * P)]


LAST_USE = {"q": "qB", "kv1": "vsw", "kv2": "ng", "pq": "qm", "memkv": "vm"}


def last_use(w, i):
    if w.startswith("mg"):
        return f"mg{2 * int(w[2:]) + 1}"
    if w in ("upn", "uppm"):
        return f"up{0 if w == 'upn' else 2}{2 * i + 1}"
    if w == "out":
        return f"acc{2 + i // 2}"
    return LAST_USE[w]


def job_table():
    used, table = [0] * 8, {}
    for name, bank in job_order():
        assert name not in table
        table[name] = (bank, used[bank])
        used[bank] += 1
    return table, used


JOBS, BANK_USES = job_table()


def build(nc, ins, out):
    with ExitStack() as ctx:
        sb = lambda name, shape, dt=F32: ctx.enter_context(nc.sbuf_tensor(name, shape, dt))
        sem = lambda name: ctx.enter_context(nc.semaphore(name))

        raw = sb("raw", [P, RAW, 4, 512])
        cst = sb("cst", [P, NF])
        cb = sb("cb", [P, NCONST - NF], BF16)
        hpart = sb("hpart", [P, 3, NT, D], BF16)
        bparts = sb("bparts", [96, 2 * FF], BF16)
        pos = sb("pos", [P, NT, NCOL])
        wgt = sb("wgt", [P, NT, NCOL])
        rounds = sb("rounds", [1, 1], I32)
        stat = sb("stat", [P, 16])

        def const(name):
            lo, hi = CONSTS[name]
            return cb[:, lo - NF:hi - NF] if lo >= NF else cst[:, lo:hi]

        with ExitStack() as early:
            se = lambda name, shape, dt=F32: early.enter_context(nc.sbuf_tensor(name, shape, dt))
            x_sb = se("x_sb", [P, NT, D])
            bufA = se("bufA", [P, 2 * D])
            bufB = se("bufB", [P, 2 * D])
            w1bd = se("w1bd", [P, 2, CMP_BLOCK, P])
            mem_sb = se("mem_sb", [P, NT, D])
            bufM = se("bufM", [P, 2 * D])
            cstage = se("cstage", [P, NCONST - NF])
            vrow = se("vrow", [18, P])
            prow = se("prow", [CMP_BLOCK, 2, 2, HD])
            vcol = se("vcol", [P, 96])
            w2bd = se("w2bd", [P, 2, P])
            wpbd = se("wpbd", [P, 2, P])
            wrt = se("wrt", [P, KD, NE])
            brt = se("brt", [1, NE])
            qraw = se("qraw", [P, 4, T])
            qrot = se("qrot", [P, 4, T])
            kcv = se("kcv", [P, 2, T])
            kraw = se("kraw", [P, 2, T])
            krot = se("krot", [P, 2, T])
            vnat = se("vnat", [P, NT, 2, P])
            gates = se("gates", [P, NT, NGATE])
            qm = se("qm", [P, 2, T])
            km = se("km", [P, 2, T])
            vm = se("vm", [P, NT, T])
            pb = [se(f"pb{i}", [P, 2, PAD + T]) for i in range(3)]
            zt = se("zt", [P, 2, T])
            hide = se("hide", [P, 2, 16])
            hid = se("hid", [P, 2, 16])
            hrep = se("hrep", [P, 4, CP])
            kc = se("kc", [P, 16])
            vc = se("vc", [P, P])
            pc = se("pc", [P, NT, HEADS, CP])
            pcT = se("pcT", [P, GROUPS, T])
            sm = se("sm", [P, 4, 16])
            pbuf = se("pbuf", [P, 3, 512])
            ptb = se("ptb", [P, 2, 512])
            us = se("us", [P, 3, 8])
            onsa = se("onsa", [P, 4, T])
            opool = se("opool", [P, 2, T])
            omem = kcv
            lgt = se("lgt", [P, NT, NE])
            top = se("top", [P, NT, 8])
            topi = se("topi", [P, NT, 8], U32)
            topf = se("topf", [P, NT, 8])
            ex4 = se("ex4", [P, NT, 8])
            comb = se("comb", [P, NT, NE])
            rtm = se("rtm", [P, NT, NE])
            selb = se("selb", [P, NT, NE], BF16)
            cbT = se("cbT", [NE, T])
            cntb = se("cntb", [1, 8])
            ones1 = se("ones1", [1, P])
        xn = bufA[:, :].rearrange("p (t d) -> p t d", t=NT)
        merged = bufA[:, :].rearrange("p (k t) -> p k t", k=KD)
        h2T = merged
        xT = bufB[:, :].rearrange("p (k t) -> p k t", k=KD)
        h2 = bufB[:, :].rearrange("p (t d) -> p t d", t=NT)
        memT = bufM[:, :].rearrange("p (k t) -> p k t", k=KD)
        sig = w1bd[:, :, :, :].rearrange("p a b c -> p (a b c)")[:, 0:24 * T].rearrange("p (k t) -> p k t", t=T)
        blk = ptb[:, :, 0:CMP_BLOCK * NC]
        rtmp = pbuf
        bsrc = bufM[0:96, :]
        gffn = mem_sb[:, 0, :]
        bdn = mem_sb[0:NE, 1, :]
        
        whi = sb("whi", [P, SPLIT, 4, 512], F32R)
        wlo = sb("wlo", [P, SPLIT, 4, 512], F32R)
        xe = sb("xe", [P, 2, KD, P], F32R)
        aT = sb("aT", [P, KD, P], F32R)
        a_sb = sb("a_sb", [SLOTS, 2, 512])
        glow = sb("glow", [SLOTS, 512])
        ulow = sb("ulow", [SLOTS, 512])
        g_sb = sb("g_sb", [SLOTS, 512])
        u_sb = sb("u_sb", [SLOTS, 512])
        s_sb = sb("s_sb", [SLOTS, 512])
        y_sb = sb("y_sb", [P, D])
        scat = sb("scat", [P, 2, T])
        gw = sb("gw", [P, NT, P])
        onehot = sb("onehot", [P, NT, SLOTS], BF16)
        bsel = sb("bsel", [96, 2, P], BF16)
        gfin = sb("gfin", [P, D])

        ps = ctx.enter_context(nc.psum_tensor("ps", [P, 8, 512], F32))

        full = [sem(f"bank_full{b}") for b in range(8)]
        free = [sem(f"bank_free{b}") for b in range(8)]
        landed = [sem(f"raw_landed{i}") for i in range(RAW)]
        s_const, s_cst2, s_x, s_mem, s_vec = (sem(n) for n in ("in_const", "in_const_bf16", "in_x", "in_mem", "in_vec"))
        s_cmp, s_pw, s_rt, s_gf = (sem(n) for n in ("in_cmp", "in_pool_w", "in_router", "in_norm_final"))
        s_bias, s_bdn, s_gffn = (sem(n) for n in ("in_bias", "in_b_down", "in_norm_ffn"))
        s_zero, s_zeros, s_cb = sem("dve_zeroed"), sem("pool_zeroed"), sem("consts_cast")
        s_dve, s_pool = sem("dve_chain"), sem("pool_chain")
        s_ss, s_var, s_sd, s_xn = sem("sumsq"), sem("variance"), sem("deviation"), sem("normed")
        s_rot, s_blk, s_hexp, s_hid, s_z = (sem(n) for n in ("rotated", "blocks", "hid_exp", "hid_ready", "pooled"))
        s_cd, s_ce, s_cp = sem("cmp_diff"), sem("cmp_exp"), sem("cmp_probs")
        s_nm, s_pr = sem("unit_negmax"), sem("unit_probs")
        s_mrg, s_h2 = sem("merged_ready"), sem("h2_ready")
        s_part, s_rest = sem("part_cast"), sem("part_rest")
        s_rv, s_re, s_sel, s_rounds = sem("router_top"), sem("router_exp"), sem("selected"), sem("rounds_ready")
        s_over, s_init = sem("phase1_over"), sem("expert_memory_zeroed")
        s_fin, s_out = sem("final_rows"), sem("out_stored")
        e_hi, e_lo, e_mul = sem("chunk_hi"), sem("chunk_lo"), sem("chunk_multiplied")
        e_low, e_gur, e_gm, e_sg, e_dv = (sem(n) for n in ("low_rows_copied", "product_read", "gate_clamped", "sigmoid_done", "dve_step"))
        e_act, e_oh, e_gw, e_bs = sem("activation_ready"), sem("onehot_ready"), sem("weights_ready"), sem("bias_row_ready")
        e_ga, e_gah, e_gal = sem("gathered"), sem("tokens_hi"), sem("tokens_lo")
        e_tr, e_trh, e_trl, e_st = sem("transposed"), sem("act_hi"), sem("act_lo"), sem("scatter_weights")
        e_yc, e_sc, e_turn = sem("y_copied"), sem("scattered"), sem("turn_begun")

        def start(eng, name):
            bank, use = JOBS[name]
            if use:
                eng.wait_ge(free[bank], use)
            return ps[:, bank, :]

        def computed(eng, name):
            bank, use = JOBS[name]
            eng.wait_ge(full[bank], use + 1)
            return ps[:, bank, :]

        def taken(eng, name):
            bank, use = JOBS[name]
            eng.wait_ge(free[bank], use + 1)

        def full_of(name):
            return full[JOBS[name][0]]

        def free_of(name):
            return free[JOBS[name][0]]

        counts, chunk_at, arrived_at = [0] * RAW, {}, {}
        for c, (w, i) in enumerate(CHUNKS):
            counts[c % RAW] += 16 * {"q": 4 * GROUPS, "uppm": 2}.get(w, 1)
            chunk_at[(w, i)] = c
            arrived_at[(w, i)] = counts[c % RAW]
        LANDED0 = counts

        def arrived(eng, w, i):
            c = chunk_at[(w, i)]
            eng.wait_ge(landed[c % RAW], arrived_at[(w, i)])
            return raw[:, c % RAW]

        w_in = ins["w_in"][0].rearrange("(k p) n -> p k n", p=P)
        w_memkv = ins["w_mem_kv"][0].rearrange("(k p) n -> p k n", p=P)
        w_upn = ins["w_up_nsa"][0].rearrange("(k p) n -> p k n", p=P)
        w_upp = ins["w_up_pool"][0].rearrange("(k p) n -> p k n", p=P)
        w_upm = ins["w_up_mem"][0].rearrange("(k p) n -> p k n", p=P)
        w_o = ins["w_out"][0].rearrange("(k p) n -> p k n", p=P)
        w_gu = ins["w_gate_up"][0].rearrange("e (k p) n -> e p k n", p=P)
        w_dn = ins["w_down"][0].rearrange("e (k p) n -> e p k n", p=P)
        x_d = ins["x"][0].rearrange("(t p) d -> p t d", p=P)
        mem_d = ins["mem"][0].rearrange("(t p) d -> p t d", p=P)
        out_d = out[0].rearrange("(t p) d -> p t d", p=P)

        def expert_chunk(e, i):
            if i < 8:
                col = (0, FF, 512, FF + 512)[i // 2]
                src, k = w_gu, 4 * (i % 2)
            else:
                col = 512 * (i % 2)
                src, k = w_dn, 4 * ((i - 8) // 2)
            src = src[e] if isinstance(e, int) else src[bass.ds(e, 1)].rearrange("a p k n -> (a p) k n")
            return src[:, k:k + 4, col:col + 512]

        def y_out(t):
            return raw[:, t, 0:2, :].rearrange("p a b -> p (a b)")

        block = ctx.enter_context(nc.Block())

        @block.sync
        def _(sp):
            sources = {"kv1": (KV0, 512), "kv2": (KV0 + 512, NG0 + NGATE - KV0 - 512), "pq": (PO0, 512)}
            sources.update({f"mg{j}": (MG0 + 512 * j, 512) for j in range(6)})
            for c, (w, i) in enumerate(CHUNKS):
                s = c % RAW
                if c >= RAW:
                    computed(sp, last_use(*CHUNKS[c - RAW]))
                if w in sources:
                    c0, n = sources[w]
                    sp.dma_start(raw[:, s, :, 0:n], w_in[:, 4 * i:4 * i + 4, c0:c0 + n]).then_inc(landed[s], 16)
                elif w == "q":
                    for k in range(4):
                        for g in range(GROUPS):
                            dst = raw[:, s, k].rearrange("p (h g d) -> p h g d", h=4, g=GROUPS)[:, :, g]
                            c0 = Q0 + 4 * HD * g
                            src = w_in[:, 4 * i + k, c0:c0 + 4 * HD].rearrange("p (h d) -> p h d", h=4)
                            sp.dma_start(dst, src).then_inc(landed[s], 16)
                elif w == "memkv":
                    sp.dma_start(raw[:, s], w_memkv[:, 4 * i:4 * i + 4, :]).then_inc(landed[s], 16)
                elif w == "upn":
                    sp.dma_start(raw[:, s], w_upn[:, :, 512 * i:512 * i + 512]).then_inc(landed[s], 16)
                elif w == "uppm":
                    sp.dma_start(raw[:, s, 0:2], w_upp[:, :, 512 * i:512 * i + 512]).then_inc(landed[s], 16)
                    sp.dma_start(raw[:, s, 2:4], w_upm[:, :, 512 * i:512 * i + 512]).then_inc(landed[s], 16)
                else:
                    k, col = 4 * (i % 2), 512 * (i // 2)
                    sp.dma_start(raw[:, s], w_o[:, k:k + 4, col:col + 512]).then_inc(landed[s], 16)
            for i in range(EXPERT_CHUNKS):
                if i < RAW:
                    computed(sp, last_use(*CHUNKS[len(CHUNKS) - RAW + i]))
                else:
                    sp.wait_ge(e_lo, i - RAW + 1)
                sp.dma_start(raw[:, i % RAW], expert_chunk(0, i)).then_inc(landed[i % RAW], 16)
            sp.wait_ge(s_rounds, 1)
            more_rounds = sp.value_load(rounds[0:1, 0:1], min_val=0, max_val=ROUNDS - 1)
            with sp.Fori(1, more_rounds * NE + NE) as n:
                for i in range(EXPERT_CHUNKS):
                    sp.wait_ge(e_lo, n * EXPERT_CHUNKS + (i - RAW + 1))
                    sp.dma_start(raw[:, i % RAW], expert_chunk(n % NE, i)).then_inc(landed[i % RAW], 16)
            for t in range(NT):
                sp.wait_ge(s_fin, t + 1)
                sp.dma_start(out_d[:, t, :], y_out(t)).then_inc(s_out, 16)
            sp.wait_ge(s_out, 16 * NT)

        @block.tensor
        def _(pe):
            ident = const("ident")
            b_ident = const("b_ident")
            def project(name, parts):
                o = start(pe, name)
                for j, (w, lhs) in enumerate(parts):
                    for k in range(KD):
                        m = pe.matmul(o[:, j * T:(j + 1) * T], lhs(arrived(pe, w, k // 4), k % 4), xT[:, k, :],
                                      start=(k == 0), stop=(k == KD - 1), skip_group_check=True)
                m.then_inc(full_of(name), 1)

            pe.wait_ge(s_const, 16)
            pe.wait_ge(s_vec, 16 * 7)
            o = start(pe, "vec")
            pe.transpose(o[:, 0:18], vrow[:, :], ident[0:18, 0:18])
            for i in range(2):
                m = pe.transpose(o[:, 32 + 32 * i:64 + 32 * i], prow[:, i].rearrange("l a d -> l (a d)"),
                                 ident[0:CMP_BLOCK, 0:CMP_BLOCK])
            m.then_inc(full_of("vec"), 1)

            def transposes(prefix, src, ready, count):
                pe.wait_ge(ready, count)
                for j in range(4):
                    o = start(pe, f"{prefix}{j}")
                    for kk in range(2):
                        for t in range(NT):
                            k = 2 * j + kk
                            m = pe.transpose(o[:, kk * T + t * P:kk * T + t * P + P], src[:, t, k * P:(k + 1) * P], ident)
                    m.then_inc(full_of(f"{prefix}{j}"), 1)

            transposes("xT", xn, s_xn, 2)
            for j in range(4):
                taken(pe, f"xT{j}")
            cols = lambda c: (lambda w, k: w[:, k, c:c + P])
            project("qA", [("q", cols(0)), ("q", cols(P))])
            project("qB", [("q", cols(2 * P)), ("q", cols(3 * P))])
            project("kcv", [("kv1", cols(0)), ("kv1", cols(P))])
            project("ksw", [("kv1", cols(2 * P)), ("kv2", cols(0))])
            o = start(pe, "vsw")
            for t in range(NT):
                for v, (w, c) in enumerate((("kv1", 3 * P), ("kv2", P))):
                    for k in range(KD):
                        m = pe.matmul(o[:, (2 * t + v) * P:(2 * t + v + 1) * P], xT[:, k, t * P:(t + 1) * P],
                                      arrived(pe, w, k // 4)[:, k % 4, c:c + P],
                                      start=(k == 0), stop=(k == KD - 1), skip_group_check=True)
            m.then_inc(full_of("vsw"), 1)
            o = start(pe, "ng")
            for t in range(NT):
                for k in range(KD):
                    m = pe.matmul(o[:, t * NGATE:(t + 1) * NGATE], xT[:, k, t * P:(t + 1) * P],
                                  arrived(pe, "kv2", k // 4)[:, k % 4, 2 * P:2 * P + NGATE],
                                  start=(k == 0), stop=(k == KD - 1), skip_group_check=True)
            m.then_inc(full_of("ng"), 1)
            project("pool", [("pq", cols(0)), ("pq", cols(P))])
            project("qm", [("pq", cols(2 * P)), ("pq", cols(3 * P))])
            for name, src, job in (("swA", qraw[:, 0:2], "qA"), ("swB", qraw[:, 2:4], "qB"), ("swk", kraw[:, :], "ksw")):
                taken(pe, job)
                o = start(pe, name)
                m = pe.matmul(o[:, :], const("swap"), src.rearrange("p a t -> p (a t)"), start=True, stop=True)
                m.then_inc(full_of(name), 1)
            transposes("mT", mem_sb, s_xn, 4)
            for j in range(4):
                taken(pe, f"mT{j}")
            o = start(pe, "km")
            for j in range(2):
                for k in range(KD):
                    m = pe.matmul(o[:, j * T:(j + 1) * T], arrived(pe, "memkv", k // 4)[:, k % 4, j * P:(j + 1) * P],
                                  memT[:, k, :], start=(k == 0), stop=(k == KD - 1), skip_group_check=True)
            m.then_inc(full_of("km"), 1)
            o = start(pe, "vm")
            for t in range(NT):
                for k in range(KD):
                    m = pe.matmul(o[:, t * T:(t + 1) * T], memT[:, k, t * P:(t + 1) * P],
                                  arrived(pe, "memkv", k // 4)[:, k % 4, T:2 * T],
                                  start=(k == 0), stop=(k == KD - 1), skip_group_check=True)
            m.then_inc(full_of("vm"), 1)

            o = start(pe, "hid")
            pe.wait_ge(s_cmp, 16 * 8)
            pe.wait_ge(s_zeros, 1)
            for i in range(2):
                pe.wait_ge(s_blk, i + 1)
                for l in range(CMP_BLOCK):
                    m = pe.matmul(o[:, 16 * i:16 * i + NC], w1bd[:, i, l, :], blk[:, i, l * NC:(l + 1) * NC],
                                  start=(l == 0), stop=(l == CMP_BLOCK - 1), skip_group_check=True)
            m.then_inc(full_of("hid"), 1)
            pe.wait_ge(s_hid, 1)
            o = start(pe, "kcvc")
            pe.matmul(o[:, 0:NC], w2bd[:, 0, :], hid[:, 0, 0:NC], start=True, stop=True, skip_group_check=True)
            m = pe.matmul(o[:, P:2 * P], hrep[:, :, :].rearrange("p a n -> p (a n)"), w2bd[:, 1, :],
                          start=True, stop=True, skip_group_check=True)
            m.then_inc(full_of("kcvc"), 1)
            pe.wait_ge(s_z, 1)
            pe.wait_ge(s_pw, 16 * 4)
            o = start(pe, "zp")
            for j in range(2):
                m = pe.matmul(o[:, j * T:(j + 1) * T], wpbd[:, j, :], zt[:, j, :], start=True, stop=True,
                              skip_group_check=True)
            m.then_inc(full_of("zp"), 1)

            taken(pe, "kcvc")
            pe.wait_ge(s_cb, 1)
            for t in range(NT):
                for g in range(GROUPS):
                    name = f"cs{t}{g}"
                    o = start(pe, name)
                    rows = slice(64 * g, 64 * g + 64)
                    for h in range(4):
                        pe.matmul(o[:, 16 * h:16 * h + NC], qraw[rows, h, t * P:(t + 1) * P], kc[rows, 0:NC],
                                  start=True, stop=False, skip_group_check=True)
                        m = pe.matmul(o[:, 16 * h:16 * h + NC], b_ident, const("b_cmp")[:, t * NC:(t + 1) * NC],
                                      start=False, stop=True, skip_group_check=True)
                    m.then_inc(full_of(name), 1)

            def scores(u):
                kind, h, v = UNITS[u]
                o = start(pe, f"S{u}")
                if kind == "mem":
                    if h == 0:
                        taken(pe, "km")
                        taken(pe, "qm")
                    rows = slice(64 * (h % 2), 64 * (h % 2) + 64)
                    for t in range(NT):
                        m = pe.matmul(o[:, t * T:(t + 1) * T], qm[rows, h // 2, t * P:(t + 1) * P], km[rows, h // 2, :],
                                      start=True, stop=True, skip_group_check=True)
                else:
                    if u == 0:
                        pe.wait_ge(s_rot, 3)
                    g = h // 4
                    rows = slice(64 * g, 64 * g + 64)
                    for t in range(NT):
                        at, n = t * P, (t + 1) * P
                        pe.matmul(o[:, at:at + n], qrot[rows, h % 4, t * P:(t + 1) * P], krot[rows, v, 0:n],
                                  start=True, stop=False, skip_group_check=True)
                        m = pe.matmul(o[:, at + t * P:at + n], b_ident, const("b_causal"),
                                      start=False, stop=True, skip_group_check=True)
                m.then_inc(full_of(f"S{u}"), 1)

            def turn(u):
                pe.wait_ge(s_pr, u + 1)
                kind = UNITS[u][0]
                o = start(pe, f"T{u}")
                for src, dst in transposed(kind):
                    m = pe.transpose(o[:, dst:dst + P], pbuf[:, u % 3, src:src + P], ident)
                m.then_inc(full_of(f"T{u}"), 1)

            def values(u):
                kind, h, v = UNITS[u]
                name = f"o{pair_of(u)}"
                rows = slice(64 * (h % 2), 64 * (h % 2) + 64)
                if h % 2 == 0 and v == 0:
                    start(pe, name)
                o = ps[:, JOBS[name][0], :]
                if kind == "nsa" and v == 0:
                    if u == 0:
                        taken(pe, "ct")
                    q = slice(CP * (h % 4), CP * (h % 4) + CP)
                    pe.matmul(o[rows, 0:T], vc[q, 64 * (h // 4):64 * (h // 4) + 64], pcT[q, h // 4, :],
                              start=True, stop=False, skip_group_check=True)
                taken(pe, f"T{u}")
                pt = ptb[:, u % 2, :]
                if kind == "nsa":
                    if u == 0:
                        taken(pe, "vsw")
                    g = h // 4
                    pe.matmul(o[rows, 0:T], vnat[:, 0, v, 64 * g:64 * g + 64], pt[:, 0:T],
                              start=False, stop=False, skip_group_check=True)
                    m = pe.matmul(o[rows, P:T], vnat[:, 1, v, 64 * g:64 * g + 64], pt[:, T:T + P],
                                  start=False, stop=(v == 1), skip_group_check=True)
                    last = h % 2 == 1 and v == 1
                else:
                    if h == 0:
                        taken(pe, "vm")
                    for k in range(2):
                        m = pe.matmul(o[rows, 0:T], vm[:, k, 64 * h:64 * h + 64], pt[:, k * T:(k + 1) * T],
                                      start=(k == 0), stop=(k == 1), skip_group_check=True)
                    last = h % 2 == 1
                if last:
                    m.then_inc(full_of(name), 1)

            scores(0)
            scores(1)
            pe.wait_ge(s_cp, 1)
            o = start(pe, "ct")
            for g in range(GROUPS):
                for t in range(NT):
                    m = pe.transpose(o[:, (2 * g + t) * P:(2 * g + t + 1) * P],
                                     pc[:, t, 4 * g:4 * g + 4, :].rearrange("p h n -> p (h n)"), ident)
            m.then_inc(full_of("ct"), 1)
            for u in range(NU):
                if u + 2 < NU:
                    scores(u + 2)
                turn(u)
                for j in fillers(u):
                    w = f"mg{j // 2}"
                    project(f"mg{j}", [(w, cols((2 * (j % 2) + i) * P)) for i in range(2)])
                if u:
                    values(u - 1)
            values(NU - 1)

            for q in range(4):
                for b, (w, k0, nk, src) in enumerate((("upn", 0, 4, onsa), ("uppm", 0, 2, opool), ("uppm", 2, 2, omem))):
                    if q == 0:
                        for job in (("o0", "o1", "o2", "o3"), ("zp",), ("o4", "o5"))[b]:
                            taken(pe, job)
                    name = f"up{b}{q}"
                    o = start(pe, name)
                    wt = arrived(pe, w, q // 2)
                    for j in range(2):
                        c = (2 * (q % 2) + j) * P
                        for k in range(nk):
                            m = pe.matmul(o[:, j * T:(j + 1) * T], wt[:, k0 + k, c:c + P], src[:, k, :],
                                          start=(k == 0), stop=(k == nk - 1), skip_group_check=True)
                    m.then_inc(full_of(name), 1)

            pe.wait_ge(s_mrg, 4)
            for half in range(2):
                for t in range(NT):
                    name = f"acc{2 * t + half}"
                    o = start(pe, name)
                    pe.matmul(o[:, :], ident, x_sb[:, t, 512 * half:512 * half + 512], start=True, stop=False,
                              skip_group_check=True)
                    for k in range(KD):
                        m = pe.matmul(o[:, :], merged[:, k, t * P:(t + 1) * P], arrived(pe, "out", 2 * half + k // 4)[:, k % 4, :],
                                      start=False, stop=(k == KD - 1), skip_group_check=True)
                    m.then_inc(full_of(name), 1)

            transposes("hT", h2, s_h2, 2)
            for j in range(4):
                taken(pe, f"hT{j}")
            pe.wait_ge(s_rt, 32)
            o = start(pe, "lg")
            for t in range(NT):
                for k in range(KD):
                    pe.matmul(o[:, NE * t:NE * t + NE], h2T[:, k, t * P:(t + 1) * P], wrt[:, k, :],
                              start=(k == 0), stop=False, skip_group_check=True)
                m = pe.matmul(o[:, NE * t:NE * t + NE], ones1[0:1, :], brt[0:1, :], start=False, stop=True,
                              skip_group_check=True)
            m.then_inc(full_of("lg"), 1)
            pe.wait_ge(s_sel, 1)
            o = start(pe, "cs")
            pe.matmul(o[:, 0:NE], const("b_before"), selb[:, 0, :], start=True, stop=True, skip_group_check=True)
            pe.matmul(o[:, NE:2 * NE], const("b_ones"), selb[:, 0, :], start=True, stop=False, skip_group_check=True)
            m = pe.matmul(o[:, NE:2 * NE], const("b_before"), selb[:, 1, :], start=False, stop=True, skip_group_check=True)
            m.then_inc(full_of("cs"), 1)
            o = start(pe, "cnt")
            for t in range(NT):
                m = pe.matmul(o[:, 0:NE], const("b_ones"), selb[:, t, :], start=(t == 0), stop=(t == 1),
                              skip_group_check=True)
            m.then_inc(full_of("cnt"), 1)
            o = start(pe, "cbT")
            for t in range(NT):
                m = pe.matmul(o[0:NE, t * P:(t + 1) * P], comb[:, t, :], ident, start=True, stop=True,
                              skip_group_check=True)
            m.then_inc(full_of("cbT"), 1)
            taken(pe, "cbT")
            pe.wait_ge(s_bdn, 16)
            for b in range(4):
                m = pe.matmul(ps[:, b, :], cbT[:, (b // 2) * P:(b // 2 + 1) * P], bdn[:, 512 * (b % 2):512 * (b % 2) + 512],
                              start=False, stop=True, skip_group_check=True)
            m.then_inc(s_over, 1)

            def gather(n, xbank):
                pe.wait_ge(e_oh, n + 1)
                o = ps[:, xbank, :]
                for k in range(KD):
                    for part in range(3):
                        for t in range(NT):
                            m = pe.matmul(o[:, SLOTS * k:SLOTS * (k + 1)], hpart[:, part, t, k * P:(k + 1) * P],
                                          onehot[:, t, :], start=(part == 0 and t == 0), stop=(part == 2 and t == 1),
                                          skip_group_check=True)
                m.then_inc(e_ga, 1)

            def turn_act(n, b, bank, weights):
                pe.wait_ge(e_act, 2 * n + (b + 1))
                pe.wait_ge(e_gur, 4 * n + (2 if b == 0 else 4))
                pe.sem_inc(e_turn, 1)
                for j in range(4):
                    m = pe.transpose(ps[:, bank, SLOTS * j:SLOTS * (j + 1)], a_sb[:, b, j * P:(j + 1) * P],
                                     ident[0:SLOTS, 0:SLOTS])
                if weights:
                    pe.wait_ge(e_gw, n + 1)
                    for t in range(NT):
                        m = pe.transpose(ps[:, bank, T + t * P:T + (t + 1) * P], gw[:, t, :], ident)
                m.then_inc(e_tr, 1)

            def scatter(n, parity):
                pe.wait_ge(e_yc, n + 1)
                for b in range(4):
                    m = pe.matmul(ps[:, b, :], scat[:, parity, (b // 2) * P:(b // 2 + 1) * P],
                                  y_sb[:, 512 * (b % 2):512 * (b % 2) + 512], start=False, stop=True, skip_group_check=True)
                m.then_inc(e_sc, 1)

            def expert(n, par, last):
                X, Y = ((4, 5), (6, 7)) if par == 0 else ((6, 7), (4, 5))
                banks = (X[0], X[1], Y[0], Y[1])

                def passes(i, stationary, bank, first):
                    k0 = 4 * (i % 2) if i < 8 else 4 * ((i - 8) // 2)
                    pe.wait_ge(e_lo, n * EXPERT_CHUNKS + (i + 1))
                    for w in (whi, wlo):
                        for k in range(4):
                            m = pe.matmul(ps[:, bank, :], stationary[:, k0 + k, :], w[:, i % SPLIT, k, :],
                                          start=(first and w is whi and k == 0), stop=True, skip_group_check=True)
                    m.then_inc(e_mul, 1)

                for q in range(4):
                    if q == 0:
                        pe.wait_ge(e_trl, 2 * n + 1)
                        pe.wait_ge(e_bs, n + 1)
                        pe.wait_ge(e_gah, n + 1)
                        pe.wait_ge(e_gal, n + 1)
                    if q == 1:
                        pe.wait_ge(e_gur, 4 * n + 1)
                    if q == 2:
                        pe.wait_ge(e_yc, n + 1)
                    col = (0, FF, 512, FF + 512)[q]
                    pe.matmul(ps[:, banks[q], :], bsel[:, par, :], bparts[:, col:col + 512], start=True, stop=False,
                              skip_group_check=True)
                    for i in (2 * q, 2 * q + 1):
                        passes(i, xe[:, par], banks[q], False)
                    if q == 2:
                        turn_act(n, 0, X[0], True)
                        if not last:
                            pe.wait_ge(e_gur, 4 * n + 3)
                            gather(n + 1, X[1])
                pe.wait_ge(e_trl, 2 * n + 2)
                pe.wait_ge(e_st, n + 2)
                passes(8, aT, X[0], True)
                if last:
                    pe.wait_ge(e_gur, 4 * n + 3)
                else:
                    pe.wait_ge(e_gah, n + 2)
                    pe.wait_ge(e_gal, n + 2)
                passes(9, aT, X[1], True)
                turn_act(n, 1, Y[0], False)
                scatter(n, 1 - par)
                pe.wait_ge(e_trl, 2 * n + 3)
                passes(10, aT, X[0], False)
                passes(11, aT, X[1], False)

            pe.wait_ge(s_over, 4)
            pe.wait_ge(s_init, 3)
            gather(0, 5)
            more_rounds = pe.value_load(rounds[0:1, 0:1], min_val=0, max_val=ROUNDS - 1)
            with pe.Fori(0, more_rounds * (NE // 2) + (NE // 2 - 1)) as i:
                expert(i * 2, 0, False)
                expert(i * 2 + 1, 1, False)
            expert(more_rounds * NE + (NE - 2), 0, False)
            expert(more_rounds * NE + (NE - 1), 1, True)
            scatter(more_rounds * NE + NE, 1)

        @block.scalar
        def _(act):
            act.dma_start(x_sb[:, :, :], x_d).then_inc(s_x, 16)
            act.dma_start(cst[:, :], ins["consts"][:, 0:NF]).then_inc(s_const, 16)
            act.dma_start(vrow[0:8, :], ins["norm_mix"][0].rearrange("(k p) -> k p", p=P)).then_inc(s_vec, 16)
            act.dma_start(vrow[8:16, :], ins["norm_mem"][0].rearrange("(k p) -> k p", p=P)).then_inc(s_vec, 16)
            act.dma_start(vrow[16:18, :], ins["pool_scale"][0].rearrange("(k p) -> k p", p=P)).then_inc(s_vec, 16)
            for i in range(2):
                for g in range(GROUPS):
                    act.dma_start(prow[:, i, g, :], ins["cmp_pos"][0, i]).then_inc(s_vec, 16)
            act.dma_start(mem_sb[:, :, :], mem_d).then_inc(s_mem, 16)

            def sumsq(src, junk, t, count):
                act.activation(junk, src, ACT.Square, accum_out=stat[:, t:t + 1]).then_inc(s_ss, 1)
                act.wait_ge(s_ss, count)

            def deviation(count, lo):
                act.wait_ge(s_var, count)
                act.activation(stat[:, lo + 2:lo + 4], stat[:, lo + 2:lo + 4], ACT.Sqrt).then_inc(s_sd, 1)

            def take(name, dst, o=None, **kw):
                o = computed(act, name) if o is None else o
                act.activation(dst, o, kw.pop("func", ACT.Copy), **kw).then_inc(free_of(name), 1)

            act.wait_ge(s_x, 16)
            for t in range(NT):
                sumsq(x_sb[:, t, :], xn[:, t, :], t, t + 1)
            deviation(1, 0)
            act.wait_ge(s_mem, 16)
            for t in range(NT):
                sumsq(mem_sb[:, t, :], bufM[:, t * D:(t + 1) * D], 4 + t, t + 3)
            deviation(2, 4)
            o = computed(act, "vec")
            act.activation(vcol[:, 0:18], o[:, 0:18], ACT.Copy)
            take("vec", vcol[:, 32:96], o[:, 32:96])
            take("qA", qraw[:, 0:2].rearrange("p a t -> p (a t)"))
            take("qB", qraw[:, 2:4].rearrange("p a t -> p (a t)"))
            take("kcv", kcv[:, :].rearrange("p a t -> p (a t)"))
            take("ksw", kraw[:, :].rearrange("p a t -> p (a t)"))
            take("vsw", vnat[:, :].rearrange("p t v d -> p (t v d)"))
            o = computed(act, "ng")
            take("ng", gates[:, :].rearrange("p t n -> p (t n)"), o[:, 0:NT * NGATE], func=ACT.Exp, scale=-1.0)
            o = computed(act, "pool")
            take("pool", pb[0][:, :, PAD:], o[:, :].rearrange("p (a t) -> p a t", a=2))
            take("qm", qm[:, :].rearrange("p a t -> p (a t)"))
            take("km", km[:, :].rearrange("p a t -> p (a t)"))
            take("vm", vm[:, :].rearrange("p a t -> p (a t)"))
            o = computed(act, "hid")
            act.activation(hide[:, :, 0:NC], o[:, 0:32].rearrange("p (i n) -> p i n", i=2)[:, :, 0:NC], ACT.Exp,
                           scale=-1.0).then_inc(s_hexp, 1)
            o = computed(act, "zp")
            act.activation(opool[:, 0, :], o[:, 0:T], ACT.Copy, scale=vcol[:, 16:17])
            take("zp", opool[:, 1, :], o[:, T:2 * T], scale=vcol[:, 17:18])
            act.wait_ge(s_cd, 4)
            pcv = pc[:, :, :, :].rearrange("p t h n -> p (t h) n")[:, :, 0:NC]
            act.activation(pcv, pcv, ACT.Exp, scale=SCALE).then_inc(s_ce, 1)

            def unit_exp(u):
                act.wait_ge(s_nm, u + 1)
                o = ps[:, JOBS[f"S{u}"][0], :]
                for t, (a, b) in enumerate(spans(UNITS[u][0])):
                    m = act.activation(pbuf[:, u % 3, a:b], o[:, a:b], ACT.Exp, bias=us[:, u % 3, 2 + t:3 + t],
                                       scale=SCALE, accum_out=us[:, u % 3, 4 + t:5 + t])
                m.then_inc(free_of(f"S{u}"), 1)

            def take_pair(u):
                pair = pair_of(u)
                o = computed(act, f"o{pair}")
                dst = onsa[:, pair, :] if pair < 4 else omem[:, pair - 4, :]
                take(f"o{pair}", dst, o[:, 0:T])

            unit_exp(0)
            unit_exp(1)
            take("ct", pcT[:, :].rearrange("p g t -> p (g t)"))
            for u in range(NU):
                if u + 2 < NU:
                    unit_exp(u + 2)
                n = 512 if UNITS[u][0] == "mem" else 3 * P
                o = computed(act, f"T{u}")
                take(f"T{u}", ptb[:, u % 2, 0:n], o[:, 0:n])
                for j in fillers(u):
                    take(f"mg{j}", sig[:, 2 * j:2 * j + 2, :].rearrange("p a t -> p (a t)"), func=ACT.Exp, scale=-1.0)
                if u and last_of_pair(u - 1):
                    take_pair(u - 1)
            take_pair(NU - 1)

            for t in range(NT):
                computed(act, f"acc{2 * t}")
                computed(act, f"acc{2 * t + 1}")
                sumsq(ps[:, 2 * t:2 * t + 2, :].rearrange("p b n -> p (b n)"), h2[:, t, :], 8 + t, t + 5)
            deviation(3, 8)
            act.wait_ge(s_h2, 2)
            flat = lambda part: hpart[:, part].rearrange("p t d -> p (t d)")
            act.activation(flat(0), bufB[:, :], ACT.Copy).then_inc(s_part, 1)
            act.wait_ge(s_rv, 2)
            for t in range(NT):
                act.activation(ex4[:, t, 0:TOPK], top[:, t, 0:TOPK], ACT.Exp, bias=ex4[:, t, 5:6],
                               accum_out=ex4[:, t, 4:5]).then_inc(s_re, 1)
            for part in (1, 2):
                act.wait_ge(s_rest, part)
                act.activation(flat(part), bufM[:, :], ACT.Copy).then_inc(s_part, 1)
            act.wait_ge(s_part, 3)
            act.sem_inc(s_over, 1)

            act.wait_ge(s_over, 4)
            for signal in (e_yc, e_st):
                act.sem_inc(signal, 1)
            act.dma_start(gfin[:, :], ins["norm_final"].partition_broadcast(P)).then_inc(s_gf, 16)

            def tokens_hi(n, par, bank):
                act.wait_ge(e_ga, n + 1)
                act.activation(xe[:, par, :, 0:SLOTS], ps[:, bank, :].rearrange("p (k s) -> p k s", s=SLOTS),
                               ACT.Copy).then_inc(e_gah, 1)

            def expert(n, par, last):
                X, Y = ((4, 5), (6, 7)) if par == 0 else ((6, 7), (4, 5))
                banks = (X[0], X[1], Y[0], Y[1])
                more = lambda i: i + SPLIT < EXPERT_CHUNKS or not last

                def ahead(i):
                    if more(i):
                        act.wait_ge(e_mul, n * EXPERT_CHUNKS + (i + 1))
                        c = i + SPLIT
                        act.wait_ge(landed[c % RAW], n * 32 + (LANDED0[c % RAW] + 16 * (c // RAW + 1)))
                        act.activation(whi[:, c % SPLIT], raw[:, c % RAW], ACT.Copy).then_inc(e_hi, 1)

                def low_rows(q):
                    act.wait_ge(e_mul, n * EXPERT_CHUNKS + (2 * q + 2))
                    act.activation((glow, ulow)[q % 2][:, :], ps[SLOTS:P, banks[q], :], ACT.Copy).then_inc(e_low, 1)

                def sigmoid(b):
                    act.wait_ge(e_gm, n * 2 + (b + 1))
                    act.activation(s_sb[:, :], g_sb[:, :], ACT.Sigmoid, scale=ALPHA).then_inc(e_sg, 1)

                def act_hi(b, bank):
                    act.wait_ge(e_tr, n * 2 + (b + 1))
                    act.activation(aT[:, 4 * b:4 * b + 4, 0:SLOTS],
                                   ps[:, bank, 0:4 * SLOTS].rearrange("p (k s) -> p k s", s=SLOTS),
                                   ACT.Copy).then_inc(e_trh, 1)

                ahead(0)
                ahead(1)
                low_rows(0)
                ahead(2)
                sigmoid(0)
                ahead(3)
                low_rows(1)
                ahead(4)
                ahead(5)
                low_rows(2)
                act.wait_ge(e_tr, n * 2 + 1)
                act.activation(scat[:, par, :], ps[:, X[0], T:2 * T], ACT.Copy).then_inc(e_st, 1)
                act_hi(0, X[0])
                if not last:
                    tokens_hi(n + 1, 1 - par, X[1])
                ahead(6)
                sigmoid(1)
                ahead(7)
                low_rows(3)
                ahead(8)
                act_hi(1, Y[0])
                ahead(9)
                ahead(10)
                act.wait_ge(e_mul, n * EXPERT_CHUNKS + EXPERT_CHUNKS)
                act.activation(y_sb[:, :], ps[:, X[0]:X[0] + 2, :].rearrange("p b n -> p (b n)"), ACT.Copy).then_inc(e_yc, 1)
                ahead(11)

            for i in range(SPLIT):
                act.wait_ge(landed[i % RAW], LANDED0[i % RAW] + 16)
                act.activation(whi[:, i], raw[:, i], ACT.Copy).then_inc(e_hi, 1)
            tokens_hi(0, 0, 5)
            more_rounds = act.value_load(rounds[0:1, 0:1], min_val=0, max_val=ROUNDS - 1)
            with act.Fori(0, more_rounds * (NE // 2) + (NE // 2 - 1)) as i:
                expert(i * 2, 0, False)
                expert(i * 2 + 1, 1, False)
            expert(more_rounds * NE + (NE - 2), 0, False)
            expert(more_rounds * NE + (NE - 1), 1, True)

            act.wait_ge(e_sc, more_rounds * NE + (NE + 1))
            for t in range(NT):
                sumsq(ps[:, 2 * t:2 * t + 2, :].rearrange("p b n -> p (b n)"), y_sb[:, :], 12 + t, t + 7)
            deviation(4, 12)

        @block.vector
        def _(dve):
            n_link = [0]

            def link(m):
                n_link[0] += 1
                m.then_inc(s_dve, 1)
                dve.wait_ge(s_dve, n_link[0])

            def variance(lo, squares, count):
                dve.wait_ge(s_ss, squares)
                dve.tensor_scalar(stat[:, lo + 2:lo + 4], stat[:, lo:lo + 2], 1.0 / D, EPS, ALU.mult, ALU.add).then_inc(s_var, 1)
                dve.wait_ge(s_sd, count)
                link(dve.reciprocal(stat[:, lo:lo + 2], stat[:, lo + 2:lo + 4]))

            def sigmoid_of_exp(a):
                link(dve.tensor_scalar(a, a, 1.0, None, ALU.add))
                link(dve.reciprocal(a, a))

            dve.memset(ones1[:, :], 1.0).then_inc(s_zero, 1)
            dve.memset(pc[:, :, :, :], 0.0).then_inc(s_zero, 1)
            link(dve.memset(hrep[:, :, :], 0.0))
            variance(0, 2, 1)
            for t in range(NT):
                dve.tensor_scalar(xn[:, t, :], x_sb[:, t, :], stat[:, t:t + 1], None, ALU.mult).then_inc(s_xn, 1)
            variance(4, 4, 2)
            for t in range(NT):
                dve.tensor_scalar(mem_sb[:, t, :], mem_sb[:, t, :], stat[:, 4 + t:5 + t], None, ALU.mult).then_inc(s_xn, 1)
            taken(dve, "vec")

            def scaled(name, dst, col):
                o = computed(dve, name)
                dve.tensor_tensor(dst, o[:, :].rearrange("p (k t) -> p k t", t=T),
                                  vcol[:, col:col + 2].unsqueeze(2).to_broadcast([P, 2, T]), ALU.mult).then_inc(free_of(name), 1)

            for j in range(4):
                scaled(f"xT{j}", xT[:, 2 * j:2 * j + 2, :], 2 * j)
            dve.wait_ge(s_cst2, 16)
            dve.tensor_copy(cb[:, :], cstage[:, :]).then_inc(s_cb, 1)
            taken(dve, "ng")
            sigmoid_of_exp(gates[:, :, :].rearrange("p t n -> p (t n)"))
            dve.wait_ge(s_const, 16)
            for name, job, src, dst in (("swA", "qA", qraw[:, 0:2], qrot[:, 0:2]), ("swB", "qB", qraw[:, 2:4], qrot[:, 2:4]),
                                        ("swk", "ksw", kraw[:, :], krot[:, :])):
                o = computed(dve, name)
                taken(dve, job)
                wide = lambda c: const(c).unsqueeze(1).to_broadcast([P, 2, T])
                own = rtmp[:, 0, :].rearrange("p (a t) -> p a t", a=2)
                other = rtmp[:, 1, :].rearrange("p (a t) -> p a t", a=2)
                dve.tensor_tensor(other, o[:, :].rearrange("p (a t) -> p a t", a=2), wide("sin"), ALU.mult).then_inc(free_of(name), 1)
                taken(dve, name)
                link(dve.tensor_tensor(own, src, wide("cos"), ALU.mult))
                dve.tensor_tensor(dst, own, other, ALU.add).then_inc(s_rot, 1)
                dve.wait_ge(s_rot, {"swA": 1, "swB": 2, "swk": 3}[name])
            for j in range(4):
                scaled(f"mT{j}", memT[:, 2 * j:2 * j + 2, :], 8 + 2 * j)
            o = computed(dve, "hid")
            dve.wait_ge(s_hexp, 1)
            sigmoid_of_exp(hide[:, :, 0:NC])
            dve.tensor_tensor(hid[:, :, 0:NC], o[:, 0:32].rearrange("p (i n) -> p i n", i=2)[:, :, 0:NC],
                              hide[:, :, 0:NC], ALU.mult).then_inc(free_of("hid"), 1)
            taken(dve, "hid")
            dve.tensor_copy(hrep[:, :, 0:NC], hid[:, 1:2, 0:NC].to_broadcast([P, 4, NC])).then_inc(s_hid, 1)
            o = computed(dve, "kcvc")
            dve.tensor_copy(kc[:, 0:NC], o[:, 0:NC])
            dve.tensor_copy(vc[:, :], o[:, P:2 * P]).then_inc(free_of("kcvc"), 1)

            for t in range(NT):
                for g in range(GROUPS):
                    name = f"cs{t}{g}"
                    o = computed(dve, name)[:, 0:64].rearrange("p (h n) -> p h n", h=4)[:, :, 0:NC]
                    mx = sm[:, 0, 8 * t + 4 * g:8 * t + 4 * g + 4]
                    link(dve.tensor_reduce(mx, o, AX, ALU.max))
                    dve.tensor_tensor(pc[:, t, 4 * g:4 * g + 4, 0:NC], o, mx.unsqueeze(2).to_broadcast([P, 4, NC]),
                                      ALU.subtract).then_inc(s_cd, 1)
                    dve.wait_ge(s_cd, 2 * t + g + 1)
                    dve.sem_inc(free_of(name), 1)
            pcv = pc[:, :, :, :].rearrange("p t h n -> p (t h) n")[:, :, 0:NC]
            dve.wait_ge(s_ce, 1)
            for t in range(NT):
                seen = const("seen")[:, t * NC:(t + 1) * NC].unsqueeze(1).to_broadcast([P, HEADS, NC])
                link(dve.tensor_tensor(pc[:, t, :, 0:NC], pc[:, t, :, 0:NC], seen, ALU.mult))
            link(dve.tensor_reduce(sm[:, 1, :], pcv, AX, ALU.add))
            link(dve.tensor_scalar(sm[:, 1, :], sm[:, 1, :], TINY, None, ALU.max))
            link(dve.reciprocal(sm[:, 2, :], sm[:, 1, :]))
            link(dve.tensor_tensor(sm[:, 3, :].rearrange("p (t h) -> p t h", t=NT), sm[:, 2, :].rearrange("p (t h) -> p t h", t=NT),
                                   gates[:, :, :].rearrange("p t (h b) -> p t h b", b=3)[:, :, :, 0], ALU.mult))
            dve.tensor_tensor(pcv, pcv, sm[:, 3, :].unsqueeze(2).to_broadcast([P, 16, NC]), ALU.mult).then_inc(s_cp, 1)

            def unit_max(u):
                o = computed(dve, f"S{u}")
                for t, (a, b) in enumerate(spans(UNITS[u][0])):
                    link(dve.tensor_reduce(us[:, u % 3, t:t + 1], o[:, a:b], AX, ALU.max))
                dve.tensor_scalar(us[:, u % 3, 2:4], us[:, u % 3, 0:2], -SCALE, None, ALU.mult).then_inc(s_nm, 1)

            def unit_norm(u):
                kind, h, v = UNITS[u]
                taken(dve, f"S{u}")
                link(dve.reciprocal(us[:, u % 3, 6:8], us[:, u % 3, 4:6]))
                if kind == "nsa":
                    link(dve.tensor_tensor(us[:, u % 3, 6:8], us[:, u % 3, 6:8], gates[:, :, 3 * h + 1 + v], ALU.mult))
                for t, (a, b) in enumerate(spans(kind)):
                    m = dve.tensor_scalar(pbuf[:, u % 3, a:b], pbuf[:, u % 3, a:b], us[:, u % 3, 6 + t:7 + t], None, ALU.mult)
                m.then_inc(s_pr, 1)

            unit_max(0)
            unit_max(1)
            unit_norm(0)
            for u in range(NU):
                if u + 2 < NU:
                    unit_max(u + 2)
                if u + 1 < NU:
                    unit_norm(u + 1)
                for j in fillers(u):
                    taken(dve, f"mg{j}")
                    sigmoid_of_exp(sig[:, 2 * j:2 * j + 2, :].rearrange("p a t -> p (a t)"))

            for q in range(4):
                for b in range(3):
                    name = f"up{b}{q}"
                    o = computed(dve, name)[:, :].rearrange("p (a t) -> p a t", a=2)
                    gate = sig[:, 8 * b + 2 * q:8 * b + 2 * q + 2, :]
                    part = merged[:, 2 * q:2 * q + 2, :]
                    dst = part if b == 0 else pbuf[:, b, :].rearrange("p (a t) -> p a t", a=2)
                    dve.tensor_tensor(dst, o, gate, ALU.mult).then_inc(free_of(name), 1)
                    taken(dve, name)
                    if b == 1:
                        link(dve.tensor_tensor(part, part, dst, ALU.add))
                    if b == 2:
                        dve.tensor_tensor(part, part, dst, ALU.add).then_inc(s_mrg, 1)

            variance(8, 6, 3)
            dve.wait_ge(s_gffn, 16)
            for t in range(NT):
                dve.scalar_tensor_tensor(h2[:, t, :], ps[:, 2 * t:2 * t + 2, :].rearrange("p b n -> p (b n)"), stat[:, 8 + t:9 + t],
                                         gffn, ALU.mult, ALU.mult).then_inc(s_h2, 1)
            for j in range(4):
                o = computed(dve, f"hT{j}")
                dve.tensor_copy(h2T[:, 2 * j:2 * j + 2, :].rearrange("p a t -> p (a t)"), o).then_inc(free_of(f"hT{j}"), 1)
            o = computed(dve, "lg")
            dve.tensor_copy(lgt[:, :, :].rearrange("p t e -> p (t e)"), o[:, 0:NT * NE]).then_inc(free_of("lg"), 1)
            taken(dve, "lg")
            for t in range(NT):
                link(dve.max(top[:, t, :], lgt[:, t, :]))
                link(dve.max_index(topi[:, t, :], top[:, t, :], lgt[:, t, :]))
                dve.tensor_scalar(ex4[:, t, 5:6], top[:, t, 0:1], -1.0, None, ALU.mult).then_inc(s_rv, 1)
            link(dve.tensor_copy(topf[:, :, :], topi[:, :, :]))
            dve.wait_ge(s_re, 2)
            for t in range(NT):
                link(dve.reciprocal(ex4[:, t, 6:7], ex4[:, t, 4:5]))
                link(dve.tensor_scalar(ex4[:, t, 0:4], ex4[:, t, 0:4], ex4[:, t, 6:7], None, ALU.mult))
                for j in range(TOPK):
                    dst = comb if j == 0 else rtm
                    link(dve.tensor_scalar(dst[:, t, :], const("iota"), topf[:, t, j:j + 1], ex4[:, t, j:j + 1],
                                           ALU.is_equal, ALU.mult))
                    if j:
                        link(dve.tensor_tensor(comb[:, t, :], comb[:, t, :], rtm[:, t, :], ALU.add))
            dve.tensor_scalar(selb[:, :, :], comb[:, :, :], 0.0, None, ALU.is_gt).then_inc(s_sel, 1)
            dve.wait_ge(s_sel, 1)
            o = computed(dve, "cs")
            dve.scalar_tensor_tensor(rtm[:, :, :].rearrange("p t e -> p (t e)"), o[:, 0:NT * NE], 1.0,
                                     selb[:, :, :].rearrange("p t e -> p (t e)"), ALU.add, ALU.mult).then_inc(free_of("cs"), 1)
            taken(dve, "cs")
            for i in range(ROUNDS):
                dve.tensor_scalar(pos[:, :, NE * i:NE * (i + 1)], rtm[:, :, :], -1.0 - SLOTS * i, None, ALU.add)
                link(dve.tensor_copy(wgt[:, :, NE * i:NE * (i + 1)], comb[:, :, :]))
            o = computed(dve, "cnt")
            dve.tensor_reduce(cntb[:, 0:1], o[0:1, 0:NE], AX, ALU.max).then_inc(free_of("cnt"), 1)
            taken(dve, "cnt")
            link(dve.tensor_scalar(cntb[:, 1:2], cntb[:, 0:1], float(SLOTS), None, ALU.is_gt))
            for i in range(2, ROUNDS):
                link(dve.tensor_scalar(cntb[:, 2:3], cntb[:, 0:1], float(SLOTS * i), None, ALU.is_gt))
                link(dve.tensor_tensor(cntb[:, 1:2], cntb[:, 1:2], cntb[:, 2:3], ALU.add))
            dve.tensor_copy(rounds[:, :], cntb[:, 1:2]).then_inc(s_rounds, 1)
            o = computed(dve, "cbT")
            dve.tensor_copy(cbT[:, :], o[0:NE, 0:T]).then_inc(free_of("cbT"), 1)
            taken(dve, "cbT")
            dve.wait_ge(s_rounds, 1)
            dve.sem_inc(s_over, 1)

            dve.wait_ge(s_over, 4)
            for signal in (e_trl, e_gur):
                dve.sem_inc(signal, 1)
            dve.memset(y_sb[:, :], 0.0).then_inc(s_init, 1)
            dve.memset(scat[:, 1, :], 0.0).then_inc(s_init, 1)

            def make_onehot(n):
                for t in range(NT):
                    m = dve.tensor_scalar(onehot[:, t, :], const("slot")[:, 0:SLOTS], col(pos, t, n), None, ALU.is_equal)
                m.then_inc(e_oh, 1)

            def col(table, t, n):
                return table[:, t, n:n + 1] if isinstance(n, int) else table[:, t, bass.ds(n, 1)]

            def tokens_lo(n, par, bank):
                dve.wait_ge(e_gah, n + 1)
                dve.tensor_tensor(xe[:, par, :, SLOTS:P], ps[:, bank, :].rearrange("p (k s) -> p k s", s=SLOTS),
                                  xe[:, par, :, 0:SLOTS].bitcast(F32), ALU.subtract).then_inc(e_gal, 1)

            def split_lo(c, i):
                dve.wait_ge(e_hi, c)
                dve.tensor_tensor(wlo[:, i % SPLIT], raw[:, i % RAW], whi[:, i % SPLIT].bitcast(F32), ALU.subtract).then_inc(e_lo, 1)

            def expert(n, par, last):
                X, Y = ((4, 5), (6, 7)) if par == 0 else ((6, 7), (4, 5))
                banks = (X[0], X[1], Y[0], Y[1])

                def ahead(i):
                    if i + SPLIT < EXPERT_CHUNKS or not last:
                        split_lo(n * EXPERT_CHUNKS + (i + SPLIT + 1), i + SPLIT)

                def both_rows(q):
                    dve.wait_ge(e_low, n * 4 + (q + 1))
                    dve.tensor_tensor((g_sb, u_sb)[q % 2][:, :], ps[0:SLOTS, banks[q], :], (glow, ulow)[q % 2][:, :],
                                      ALU.add).then_inc(e_gur, 1)
                    dve.wait_ge(e_gur, n * 4 + (q + 2))

                def gate(b):
                    both_rows(2 * b)
                    dve.tensor_scalar(g_sb[:, :], g_sb[:, :], LIMIT, None, ALU.min).then_inc(e_gm, 1)

                def up(b):
                    both_rows(2 * b + 1)
                    dve.tensor_scalar(u_sb[:, :], u_sb[:, :], LIMIT, -LIMIT, ALU.min, ALU.max).then_inc(e_dv, 1)
                    dve.wait_ge(e_gm, n * 2 + (b + 1))
                    dve.wait_ge(e_dv, n * 4 + (2 * b + 1))
                    dve.scalar_tensor_tensor(u_sb[:, :], u_sb[:, :], 1.0, g_sb[:, :], ALU.add, ALU.mult).then_inc(e_dv, 1)
                    dve.wait_ge(e_dv, n * 4 + (2 * b + 2))
                    dve.wait_ge(e_sg, n * 2 + (b + 1))
                    dve.tensor_tensor(a_sb[:, b, :], u_sb[:, :], s_sb[:, :], ALU.mult).then_inc(e_act, 1)

                def act_lo(b, bank):
                    dve.wait_ge(e_trh, n * 2 + (b + 1))
                    dve.tensor_tensor(aT[:, 4 * b:4 * b + 4, SLOTS:P], ps[:, bank, 0:4 * SLOTS].rearrange("p (k s) -> p k s", s=SLOTS),
                                      aT[:, 4 * b:4 * b + 4, 0:SLOTS].bitcast(F32), ALU.subtract).then_inc(e_trl, 1)

                dve.wait_ge(e_st, n + 1)
                for t in range(NT):
                    m = dve.tensor_scalar(gw[:, t, :], const("slot"), col(pos, t, n), col(wgt, t, n), ALU.is_equal, ALU.mult)
                m.then_inc(e_gw, 1)
                if not last:
                    dve.wait_ge(e_ga, n + 1)
                    make_onehot(n + 1)
                ahead(0)
                ahead(1)
                gate(0)
                ahead(2)
                ahead(3)
                up(0)
                ahead(4)
                ahead(5)
                gate(1)
                dve.wait_ge(e_st, n + 2)
                act_lo(0, X[0])
                if not last:
                    tokens_lo(n + 1, 1 - par, X[1])
                ahead(6)
                ahead(7)
                up(1)
                ahead(8)
                act_lo(1, Y[0])
                ahead(9)
                ahead(10)
                ahead(11)

            make_onehot(0)
            for i in range(SPLIT):
                split_lo(i + 1, i)
            tokens_lo(0, 0, 5)
            more_rounds = dve.value_load(rounds[0:1, 0:1], min_val=0, max_val=ROUNDS - 1)
            with dve.Fori(0, more_rounds * (NE // 2) + (NE // 2 - 1)) as i:
                expert(i * 2, 0, False)
                expert(i * 2 + 1, 1, False)
            expert(more_rounds * NE + (NE - 2), 0, False)
            expert(more_rounds * NE + (NE - 1), 1, True)

            variance(12, 8, 4)
            dve.wait_ge(s_gf, 16)
            for t in range(NT):
                dve.scalar_tensor_tensor(y_out(t), ps[:, 2 * t:2 * t + 2, :].rearrange("p b n -> p (b n)"), stat[:, 12 + t:13 + t],
                                         gfin[:, :], ALU.mult, ALU.mult).then_inc(s_fin, 1)

        @block.gpsimd
        def _(pool):
            n_link = [0]

            def link(m):
                n_link[0] += 1
                m.then_inc(s_pool, 1)
                pool.wait_ge(s_pool, n_link[0])

            pool.dma_start(cstage[:, :], ins["consts"][:, NF:NCONST]).then_inc(s_cst2, 16)
            for w in (w1bd[:, :, :, :].rearrange("p a l e -> p (a l) e"), w2bd[:, :, :], wpbd[:, :, :]):
                link(pool.memset(w[0:HD, :, HD:P], 0.0))
                link(pool.memset(w[HD:P, :, 0:HD], 0.0))
            for b in pb:
                link(pool.memset(b[:, :, 0:PAD], 0.0))
            pool.sem_inc(s_zeros, 1)
            for g in range(GROUPS):
                rows = slice(HD * g, HD * g + HD)
                for i in range(2):
                    pool.dma_start(w1bd[rows, i, :, rows], ins["cmp_w1"][0, i].rearrange("l d e -> d l e")).then_inc(s_cmp, 16)
                    pool.dma_start(w2bd[rows, i, rows], ins["cmp_w2"][0, i]).then_inc(s_cmp, 16)
                for j in range(2):
                    pool.dma_start(wpbd[rows, j, rows], ins["w_pool"][0, 2 * j + g]).then_inc(s_pw, 16)
            pool.dma_start(wrt[:, :, :], ins["w_router"][0].rearrange("(k p) e -> p k e", p=P)).then_inc(s_rt, 16)
            pool.dma_start(brt[:, :], ins["b_router"]).then_inc(s_rt, 16)

            taken(pool, "vec")
            taken(pool, "kcv")
            for i in range(2):
                tok = kcv[:, i, :].rearrange("p (n l) -> p l n", l=CMP_STRIDE)
                for half in range(2):
                    posn = vcol[:, 32 + 32 * i + 16 * half:48 + 32 * i + 16 * half].unsqueeze(2).to_broadcast([P, CMP_STRIDE, NC])
                    dst = blk[:, i, half * CMP_STRIDE * NC:(half + 1) * CMP_STRIDE * NC].rearrange("p (l n) -> p l n", n=NC)
                    m = pool.tensor_tensor(dst, tok[:, :, half:half + NC], posn, ALU.add)
                m.then_inc(s_blk, 1)

            taken(pool, "pool")
            a, b, c = pb
            lo, hi = slice(0, HD), slice(HD, P)

            def doubled(dst, src, rows, blocks, shift):
                link(pool.tensor_tensor(dst[rows, blocks, PAD:], src[rows, blocks, PAD:],
                                        src[rows, blocks, PAD - shift:PAD + T - shift], ALU.add))

            doubled(b, a, slice(0, P), slice(0, 2), 1)
            doubled(c, b, slice(0, P), slice(0, 2), 2)
            doubled(b, c, slice(0, P), slice(1, 2), 4)
            doubled(c, b, hi, slice(1, 2), 8)
            pinv = const("pinv").rearrange("p (j t) -> p j t", j=2)
            pool.wait_ge(s_const, 16)
            for j in range(2):
                for rows, src in ((lo, b), (hi, c)):
                    link(pool.tensor_tensor(zt[rows, j, :], src[rows, j, PAD:], pinv[rows, j, :], ALU.mult))
            pool.tensor_tensor(zt[:, :, :], zt[:, :, :], a[:, :, PAD:], ALU.subtract).then_inc(s_z, 1)

            computed(pool, "km")
            computed(pool, "vm")
            for i in range(3):
                pool.dma_start(bsrc[NE * i:NE * (i + 1), :], ins["b_gate_up"][0]).then_inc(s_bias, 16)
            pool.dma_start(gffn, ins["norm_ffn"][0].partition_broadcast(P)).then_inc(s_gffn, 16)
            pool.dma_start(bdn, ins["b_down"][0]).then_inc(s_bdn, 16)
            pool.wait_ge(s_bias, 48)
            for i in range(3):
                for j in range(i, 3):
                    rows = slice(NE * j, NE * (j + 1))
                    link(pool.tensor_copy(bparts[rows, :], bsrc[rows, :]))
                    if j > i:
                        link(pool.tensor_tensor(bsrc[rows, :], bsrc[rows, :], bparts[rows, :], ALU.subtract))
            pool.wait_ge(s_part, 1)
            flat = lambda part: hpart[:, part].rearrange("p t d -> p (t d)")
            pool.tensor_tensor(bufM[:, :], bufB[:, :], flat(0), ALU.subtract).then_inc(s_rest, 1)
            pool.wait_ge(s_part, 2)
            pool.tensor_tensor(bufM[:, :], bufM[:, :], flat(1), ALU.subtract).then_inc(s_rest, 1)
            pool.wait_ge(s_rest, 2)
            pool.sem_inc(s_over, 1)

            pool.wait_ge(s_over, 4)
            pool.memset(bsel[:, :, SLOTS:P], 0.0).then_inc(s_init, 1)

            def bias_row(e, par):
                e = e if isinstance(e, int) else e % NE
                src = const("b_expert")[0:96]
                pool.wait_ge(s_init, 3)
                src = src[:, e:e + 1] if isinstance(e, int) else src[:, bass.ds(e, 1)]
                pool.tensor_copy(bsel[:, par, 0:SLOTS], src.to_broadcast([96, SLOTS])).then_inc(e_bs, 1)

            bias_row(0, 0)
            more_rounds = pool.value_load(rounds[0:1, 0:1], min_val=0, max_val=ROUNDS - 1)
            with pool.Fori(0, more_rounds * (NE // 2) + NE // 2) as i:
                for par in range(2):
                    n = i * 2 + par
                    pool.wait_ge(e_yc, n + 1)
                    bias_row(n + 1, 1 - par)


_INS = ["x", "mem", "norm_mix", "norm_mem", "w_in", "cmp_pos", "cmp_w1", "cmp_w2", "w_pool", "pool_scale", "w_mem_kv",
        "w_up_nsa", "w_up_pool", "w_up_mem", "w_out", "norm_ffn", "w_router", "b_router", "w_gate_up", "b_gate_up",
        "w_down", "b_down", "norm_final"]


def kernel(**inputs):
    import concourse.bacc as bacc
    from concourse.bass_utils import run_bass_kernel_spmd

    nc = bacc.Bacc("TRN2", target_bir_lowering=False, num_devices=1)
    arrays = {f"in_{n}": np.ascontiguousarray(inputs[n]) for n in _INS}
    arrays["in_consts"] = constants()
    ins = {n[3:]: nc.dram_tensor(n, a.shape, mybir.dt.from_np(a.dtype), kind="ExternalInput").ap()
           for n, a in arrays.items()}
    out = nc.dram_tensor("out", (1, T, D), F32, kind="ExternalOutput").ap()
    build(nc, ins, out)
    r = run_bass_kernel_spmd(nc, [arrays], core_ids=[0])
    return r.results[0]["out"]
```

```python
from contextlib import ExitStack

import numpy as np

import concourse.bass as bass
from concourse import mybir

F32 = mybir.dt.float32
F32R = mybir.dt.float32r
BF16 = mybir.dt.bfloat16
I32 = mybir.dt.int32
U32 = mybir.dt.uint32
ALU = mybir.AluOpType
ACT = mybir.ActivationFunctionType
AX = mybir.AxisListType.X

P = 128
D = 1024
T = 256
KD = D // P
NT = T // P
HD = 64
HEADS = 8
GROUPS = 2
MEM_HEADS = 4
SCALE = HD ** -0.5
CMP_BLOCK, CMP_STRIDE = 32, 16
HALF = CMP_BLOCK // 2
NC = (T - CMP_BLOCK) // CMP_STRIDE + 1
CP = 32
POOL_WINDOWS = (2, 4, 8, 16)
PAD = 16
EPS = 1e-5
NEG = -1e30
TINY = 1e-30
LIMIT, ALPHA = 7.0, 1.702
NE = 32
FF = 1024
TOPK = 4
SLOTS = 64
ROUNDS = T // SLOTS
NCOL = ROUNDS * NE

Q0, KV0, NG0, PO0, QM0, MG0 = 0, 512, 1280, 1304, 1560, 1816
NGATE = 3 * HEADS

CONSTS = {}


def _lay_out():
    at = 0
    for name, n in (("ident", P), ("cos", T), ("sin", T), ("swap", P), ("pinv", 2 * T), ("slot", P),
                    ("iota", NE), ("seen", NT * NC), ("b_ident", P), ("b_causal", P), ("b_before", P),
                    ("b_ones", P), ("b_cmp", NT * NC), ("b_expert", NE)):
        CONSTS[name] = (at, at + n)
        at += n
    return at


NCONST = _lay_out()
NF = CONSTS["b_ident"][0]


def constants():
    c = np.zeros((P, NCONST), np.float32)

    def put(name, a):
        lo, hi = CONSTS[name]
        c[:, lo:hi] = np.asarray(a, np.float32).reshape(P, hi - lo)

    p = np.arange(P)
    half = HD // 2
    inv = np.float32(10000.0) ** (-np.arange(half, dtype=np.float32) / np.float32(half))
    ang = (np.arange(T, dtype=np.float32)[None, :] * inv.astype(np.float32)[p % half][:, None]).astype(np.float32)
    put("ident", np.eye(P))
    put("b_ident", np.eye(P))
    put("cos", np.cos(ang.astype(np.float64)))
    put("sin", np.sin(ang.astype(np.float64)))
    swap = np.zeros((P, P))
    for m in range(P):
        first = m % HD < half
        swap[m + half if first else m - half, m] = -1.0 if first else 1.0
    put("swap", swap)
    pinv = np.zeros((P, 2, T))
    for j in range(2):
        for g in range(2):
            pinv[64 * g:64 * g + 64, j] = 1.0 / np.minimum(np.arange(T) + 1, POOL_WINDOWS[2 * j + g])
    put("pinv", pinv)
    put("slot", np.tile(np.arange(P) % SLOTS, (P, 1)))
    put("iota", np.tile(np.arange(NE), (P, 1)))
    tok = np.arange(NT)[None, :, None] * P + p[:, None, None]
    seen = (np.arange(NC) * CMP_STRIDE + CMP_BLOCK - 1)[None, None, :] <= tok
    put("seen", seen)
    put("b_cmp", np.where(seen, 0.0, NEG))
    put("b_causal", np.where(p[None, :] <= p[:, None], 0.0, NEG))
    put("b_before", p[:, None] < p[None, :])
    put("b_ones", np.ones((P, P)))
    put("b_expert", (p[:, None] % NE == np.arange(NE)[None, :]) & (p[:, None] < 3 * NE))
    return c


UNITS = [("nsa", h, v) for h in range(HEADS) for v in range(2)] + [("mem", h, 0) for h in range(MEM_HEADS)]
NU = len(UNITS)
NMG = 24


def fillers(u):
    return range(NMG * u // NU, NMG * (u + 1) // NU)


CHUNKS = [(w, kh) for w in ("q", "kv1", "kv2", "pq", "memkv") for kh in range(2)]
CHUNKS += [(f"mg{j}", kh) for j in range(6) for kh in range(2)]
CHUNKS += [("upn", 0), ("uppm", 0), ("upn", 1), ("uppm", 1)]
CHUNKS += [("out", i) for i in range(4)]
RAW = 6
EXPERT_CHUNKS = 12
SPLIT = 4
POOL_LO = (2, 6, 10)


def lo_step(i):
    mine = [c for c in range(EXPERT_CHUNKS) if (c in POOL_LO) == (i in POOL_LO)]
    return i in POOL_LO, mine.index(i), len(mine)


assert len(CHUNKS) % RAW == 0 and EXPERT_CHUNKS % RAW == 0 and EXPERT_CHUNKS % SPLIT == 0


def job_order():
    jobs, turn = [], [0]

    def work(*names):
        for n in names:
            jobs.append((n, 2 + turn[0] % 6))
            turn[0] += 1

    work("vec", "xT0", "xT1", "xT2", "xT3", "qA", "qB", "kcv", "ksw", "vsw", "mT0", "mT1", "mT2", "mT3",
         "ng", "swA", "swB", "swk", "pool", "qm", "hid", "km", "kcvc", "vm", "zp",
         "cs00", "cs01", "cs10", "cs11", "S0", "S1", "ct")
    for u in range(NU):
        if u + 2 < NU:
            work(f"S{u + 2}")
        work(f"T{u}")
        work(*[f"mg{j}" for j in fillers(u)])
        if u >= 1 and first_of_pair(u - 1):
            pair = pair_of(u - 1)
            jobs.append((f"o{pair}", pair % 2))
    work(*[f"up{b}{q}" for q in range(4) for b in range(3)])
    jobs.extend((f"acc{b}", b) for b in range(4))
    turn[0] = 0
    for n in ("hT00", "hT01", "hT10", "hT11", "lg0", "lg1", "cs", "cnt", "cbT"):
        jobs.append((n, 4 + turn[0] % 4))
        turn[0] += 1
    return jobs


def pair_of(u):
    kind, h, _ = UNITS[u]
    return h // 2 + (4 if kind == "mem" else 0)


def first_of_pair(u):
    return UNITS[u][1] % 2 == 0 and UNITS[u][2] == 0


def last_of_pair(u):
    return UNITS[u][1] % 2 == 1 and UNITS[u][2] == (UNITS[u][0] == "nsa")


def spans(kind):
    return [(0, T), (T, 2 * T)] if kind == "mem" else [(0, P), (P, P + T)]


def transposed(kind):
    if kind == "mem":
        return [(t * T + k * P, k * T + t * P) for k in range(2) for t in range(NT)]
    return [(0, 0), (P, P), (2 * P, 2 * P)]


LAST_USE = {"q": "qB", "kv1": "vsw", "kv2": "ng", "pq": "qm", "memkv": "vm"}


def last_use(w, i):
    if w.startswith("mg"):
        return f"mg{4 * int(w[2:]) + 3}"
    if w in ("upn", "uppm"):
        return f"up{0 if w == 'upn' else 2}{2 * i + 1}"
    if w == "out":
        return f"acc{2 + i // 2}"
    return LAST_USE[w]


def job_table():
    used, table = [0] * 8, {}
    for name, bank in job_order():
        assert name not in table
        table[name] = (bank, used[bank])
        used[bank] += 1
    return table, used


JOBS, BANK_USES = job_table()


def build(nc, ins, out):
    with ExitStack() as ctx:
        sb = lambda name, shape, dt=F32: ctx.enter_context(nc.sbuf_tensor(name, shape, dt))
        sem = lambda name: ctx.enter_context(nc.semaphore(name))

        raw = sb("raw", [P, RAW, 4, 512])
        cst = sb("cst", [P, NF])
        cb = sb("cb", [P, NCONST - NF], BF16)
        hpart = sb("hpart", [P, 3, NT, D], BF16)
        bparts = sb("bparts", [96, 2 * FF], BF16)
        pos = sb("pos", [P, NT, NCOL])
        wgt = sb("wgt", [P, NT, NCOL])
        rounds = sb("rounds", [1, 1], I32)
        stat = sb("stat", [P, 16])

        def const(name):
            lo, hi = CONSTS[name]
            return cb[:, lo - NF:hi - NF] if lo >= NF else cst[:, lo:hi]

        with ExitStack() as early:
            se = lambda name, shape, dt=F32: early.enter_context(nc.sbuf_tensor(name, shape, dt))
            sigw = se("sigw", [P, 24 * T])
            cstage = se("cstage", [P, NCONST - NF])
            prow = se("prow", [HALF, 2, P])
            vcol = se("vcol", [P, 96])
            w2 = se("w2", [HD, 2, HD])
            kswap = se("kswap", [P, 2, T])
            wpbd = se("wpbd", [P, 2, P])
            qraw = se("qraw", [P, 4, T])
            qrot = se("qrot", [P, 4, T])
            kcv = se("kcv", [P, 2, T])
            kraw = se("kraw", [P, 2, T])
            krot = se("krot", [P, 2, T])
            vnat = se("vnat", [P, NT, 2, P])
            gates = se("gates", [P, NT, NGATE])
            qm = se("qm", [P, 2, T])
            km = se("km", [P, 2, T])
            vm = se("vm", [P, NT, T])
            pb = [se(f"pb{i}", [P, 2, PAD + T]) for i in range(3)]
            zt = se("zt", [P, 2, T])
            hide = se("hide", [HD, 2, GROUPS * NC])
            hid = se("hid", [HD, 2, GROUPS * NC])
            hrep = se("hrep", [HD, GROUPS, 4, CP])
            kc = se("kc", [P, 16])
            vc = se("vc", [P, P])
            pc = se("pc", [P, NT, HEADS, CP])
            pcT = se("pcT", [P, GROUPS, T])
            sm = se("sm", [P, 4, 16])
            pbuf = se("pbuf", [P, 3, 512])
            ptb = se("ptb", [P, 2, 512])
            us = se("us", [P, 3, 8])
            onsa = se("onsa", [P, 4, T])
            opool = se("opool", [P, 2, T])
            omem = kcv
            x_sb = se("x_sb", [P, NT, D])
            bufA = se("bufA", [P, 2 * D])
            bufB = se("bufB", [P, 2 * D])
            vrow = se("vrow", [18, P])
            wrt = se("wrt", [P, KD, NE])
            brt = se("brt", [1, NE])
            lgt = se("lgt", [P, NT, NE])
            top = se("top", [P, NT, 8])
            topi = se("topi", [P, NT, 8], U32)
            topf = se("topf", [P, NT, 8])
            ex4 = se("ex4", [P, NT, 8])
            comb = se("comb", [P, NT, NE])
            rtm = se("rtm", [P, NT, NE])
            selb = se("selb", [P, NT, NE], BF16)
            cntb = se("cntb", [1, 8])
            ones1 = se("ones1", [1, P])
            cbT = se("cbT", [NE, T])
            bufM = se("bufM", [P, 2 * D])
            mem_sb = se("mem_sb", [P, NT, D])
        xn = bufA[:, :].rearrange("p (t d) -> p t d", t=NT)
        merged = bufA[:, :].rearrange("p (k t) -> p k t", k=KD)
        h2T = merged
        xT = bufB[:, :].rearrange("p (k t) -> p k t", k=KD)
        h2 = bufB[:, :].rearrange("p (t d) -> p t d", t=NT)
        memT = bufM[:, :].rearrange("p (k t) -> p k t", k=KD)
        sig = sigw[:, :].rearrange("p (k t) -> p k t", t=T)
        w1 = sigw[:, 0:2 * HALF * HD].rearrange("p (i l e) -> p i l e", i=2, l=HALF)
        blk = ptb[:, :, 0:HALF * GROUPS * NC].rearrange("p i (l g n) -> p i l g n", l=HALF, g=GROUPS)
        rtmp = pbuf
        bsrc = bufM[0:96, :]
        gffn = mem_sb[:, 0, :]
        bdn = mem_sb[0:NE, 1, :]
        
        whi = sb("whi", [P, SPLIT, 4, 512], F32R)
        wlo = sb("wlo", [P, SPLIT, 4, 512], F32R)
        xe = sb("xe", [P, 2, KD, P], F32R)
        aT = sb("aT", [P, KD, P], F32R)
        a_sb = sb("a_sb", [SLOTS, 2, 512])
        glow = sb("glow", [SLOTS, 512])
        ulow = sb("ulow", [SLOTS, 512])
        g_sb = sb("g_sb", [SLOTS, 512])
        u_sb = sb("u_sb", [SLOTS, 512])
        s_sb = sb("s_sb", [SLOTS, 512])
        y_sb = sb("y_sb", [P, D])
        scat = sb("scat", [P, 2, T])
        gw = sb("gw", [P, NT, P])
        onehot = sb("onehot", [P, NT, SLOTS], BF16)
        bsel = sb("bsel", [96, 2, P], BF16)
        gfin = sb("gfin", [P, D])

        ps = ctx.enter_context(nc.psum_tensor("ps", [P, 8, 512], F32))

        full = [sem(f"bank_full{b}") for b in range(8)]
        free = [sem(f"bank_free{b}") for b in range(8)]
        landed = [sem(f"raw_landed{i}") for i in range(RAW)]
        s_const, s_cst2, s_x, s_mem, s_vec = (sem(n) for n in ("in_const", "in_const_bf16", "in_x", "in_mem", "in_vec"))
        s_cmp, s_pw, s_rt, s_gf = (sem(n) for n in ("in_cmp", "in_pool_w", "in_router", "in_norm_final"))
        s_bias, s_bdn, s_gffn = (sem(n) for n in ("in_bias", "in_b_down", "in_norm_ffn"))
        s_zero, s_zeros, s_cb = sem("dve_zeroed"), sem("pool_zeroed"), sem("consts_cast")
        s_dve, s_pool = sem("dve_chain"), sem("pool_chain")
        s_ss, s_var, s_sd, s_xn = sem("sumsq"), sem("variance"), sem("deviation"), sem("normed")
        s_rot, s_blk, s_hexp, s_hid, s_z = (sem(n) for n in ("rotated", "blocks", "hid_exp", "hid_ready", "pooled"))
        s_cd, s_ce, s_cp = sem("cmp_diff"), sem("cmp_exp"), sem("cmp_probs")
        s_nm, s_pr = sem("unit_negmax"), sem("unit_probs")
        s_mrg, s_h2 = sem("merged_ready"), sem("h2_ready")
        s_part, s_rest = sem("part_cast"), sem("part_rest")
        s_rv, s_re, s_sel, s_rounds = sem("router_top"), sem("router_exp"), sem("selected"), sem("rounds_ready")
        s_over, s_init = sem("phase1_over"), sem("expert_memory_zeroed")
        s_fin, s_out = sem("final_rows"), sem("out_stored")
        e_hi, e_mul = sem("chunk_hi"), sem("chunk_multiplied")
        e_lo = {False: sem("chunk_lo_dve"), True: sem("chunk_lo_pool")}
        e_low, e_gur, e_gm, e_sg, e_dv = (sem(n) for n in ("low_rows_copied", "product_read", "gate_clamped", "sigmoid_done", "dve_step"))
        e_act, e_oh, e_gw, e_bs = sem("activation_ready"), sem("onehot_ready"), sem("weights_ready"), sem("bias_row_ready")
        e_ga, e_gah, e_gal = sem("gathered"), sem("tokens_hi"), sem("tokens_lo")
        e_tr, e_trh, e_trl, e_st = sem("transposed"), sem("act_hi"), sem("act_lo"), sem("scatter_weights")
        e_yc, e_sc, e_turn = sem("y_copied"), sem("scattered"), sem("turn_begun")

        def start(eng, name):
            bank, use = JOBS[name]
            if use:
                eng.wait_ge(free[bank], use)
            return ps[:, bank, :]

        def computed(eng, name):
            bank, use = JOBS[name]
            eng.wait_ge(full[bank], use + 1)
            return ps[:, bank, :]

        def taken(eng, name):
            bank, use = JOBS[name]
            eng.wait_ge(free[bank], use + 1)

        def full_of(name):
            return full[JOBS[name][0]]

        def free_of(name):
            return free[JOBS[name][0]]

        counts, chunk_at, arrived_at = [0] * RAW, {}, {}
        for c, (w, i) in enumerate(CHUNKS):
            counts[c % RAW] += 16 * {"q": 4 * GROUPS, "uppm": 2}.get(w, 1)
            chunk_at[(w, i)] = c
            arrived_at[(w, i)] = counts[c % RAW]
        LANDED0 = counts

        def arrived(eng, w, i):
            c = chunk_at[(w, i)]
            eng.wait_ge(landed[c % RAW], arrived_at[(w, i)])
            return raw[:, c % RAW]

        w_in = ins["w_in"][0].rearrange("(k p) n -> p k n", p=P)
        w_memkv = ins["w_mem_kv"][0].rearrange("(k p) n -> p k n", p=P)
        w_upn = ins["w_up_nsa"][0].rearrange("(k p) n -> p k n", p=P)
        w_upp = ins["w_up_pool"][0].rearrange("(k p) n -> p k n", p=P)
        w_upm = ins["w_up_mem"][0].rearrange("(k p) n -> p k n", p=P)
        w_o = ins["w_out"][0].rearrange("(k p) n -> p k n", p=P)
        w_gu = ins["w_gate_up"][0].rearrange("e (k p) n -> e p k n", p=P)
        w_dn = ins["w_down"][0].rearrange("e (k p) n -> e p k n", p=P)
        x_d = ins["x"][0].rearrange("(t p) d -> p t d", p=P)
        mem_d = ins["mem"][0].rearrange("(t p) d -> p t d", p=P)
        out_d = out[0].rearrange("(t p) d -> p t d", p=P)

        def expert_chunk(e, i):
            if i < 8:
                col = (0, FF, 512, FF + 512)[i // 2]
                src, k = w_gu, 4 * (i % 2)
            else:
                col = 512 * (i % 2)
                src, k = w_dn, 4 * ((i - 8) // 2)
            src = src[e] if isinstance(e, int) else src[bass.ds(e, 1)].rearrange("a p k n -> (a p) k n")
            return src[:, k:k + 4, col:col + 512]

        def split(eng, n, i):
            by_pool, at, per_expert = lo_step(i)
            eng.wait_ge(e_lo[by_pool], n * per_expert + (at + 1))

        def y_out(t):
            return raw[:, t, 0:2, :].rearrange("p a b -> p (a b)")

        block = ctx.enter_context(nc.Block())

        @block.sync
        def _(sp):
            sources = {"kv1": (KV0, 512), "kv2": (KV0 + 512, NG0 + NGATE - KV0 - 512), "pq": (PO0, 512)}
            sources.update({f"mg{j}": (MG0 + 512 * j, 512) for j in range(6)})
            for c, (w, i) in enumerate(CHUNKS):
                s = c % RAW
                if c >= RAW:
                    computed(sp, last_use(*CHUNKS[c - RAW]))
                if w in sources:
                    c0, n = sources[w]
                    sp.dma_start(raw[:, s, :, 0:n], w_in[:, 4 * i:4 * i + 4, c0:c0 + n]).then_inc(landed[s], 16)
                elif w == "q":
                    for k in range(4):
                        for g in range(GROUPS):
                            dst = raw[:, s, k].rearrange("p (h g d) -> p h g d", h=4, g=GROUPS)[:, :, g]
                            c0 = Q0 + 4 * HD * g
                            src = w_in[:, 4 * i + k, c0:c0 + 4 * HD].rearrange("p (h d) -> p h d", h=4)
                            sp.dma_start(dst, src).then_inc(landed[s], 16)
                elif w == "memkv":
                    sp.dma_start(raw[:, s], w_memkv[:, 4 * i:4 * i + 4, :]).then_inc(landed[s], 16)
                elif w == "upn":
                    sp.dma_start(raw[:, s], w_upn[:, :, 512 * i:512 * i + 512]).then_inc(landed[s], 16)
                elif w == "uppm":
                    sp.dma_start(raw[:, s, 0:2], w_upp[:, :, 512 * i:512 * i + 512]).then_inc(landed[s], 16)
                    sp.dma_start(raw[:, s, 2:4], w_upm[:, :, 512 * i:512 * i + 512]).then_inc(landed[s], 16)
                else:
                    k, col = 4 * (i % 2), 512 * (i // 2)
                    sp.dma_start(raw[:, s], w_o[:, k:k + 4, col:col + 512]).then_inc(landed[s], 16)
            for i in range(EXPERT_CHUNKS):
                if i < RAW:
                    computed(sp, last_use(*CHUNKS[len(CHUNKS) - RAW + i]))
                else:
                    split(sp, 0, i - RAW)
                sp.dma_start(raw[:, i % RAW], expert_chunk(0, i)).then_inc(landed[i % RAW], 16)
            sp.wait_ge(s_rounds, 1)
            more_rounds = sp.value_load(rounds[0:1, 0:1], min_val=0, max_val=ROUNDS - 1)
            with sp.Fori(1, more_rounds * NE + NE) as n:
                for i in range(EXPERT_CHUNKS):
                    if i < RAW:
                        by_pool, at, per_expert = lo_step(i - RAW + EXPERT_CHUNKS)
                        sp.wait_ge(e_lo[by_pool], n * per_expert + (at + 1 - per_expert))
                    else:
                        split(sp, n, i - RAW)
                    sp.dma_start(raw[:, i % RAW], expert_chunk(n % NE, i)).then_inc(landed[i % RAW], 16)
            for t in range(NT):
                sp.wait_ge(s_fin, t + 1)
                sp.dma_start(out_d[:, t, :], y_out(t)).then_inc(s_out, 16)
            sp.wait_ge(s_out, 16 * NT)

        @block.tensor
        def _(pe):
            ident = const("ident")
            b_ident = const("b_ident")
            def project(name, parts):
                o = start(pe, name)
                for j, (w, lhs) in enumerate(parts):
                    for k in range(KD):
                        m = pe.matmul(o[:, j * T:(j + 1) * T], lhs(arrived(pe, w, k // 4), k % 4), xT[:, k, :],
                                      start=(k == 0), stop=(k == KD - 1), skip_group_check=True)
                m.then_inc(full_of(name), 1)

            pe.wait_ge(s_const, 16)
            pe.wait_ge(s_vec, 16 * 4)
            o = start(pe, "vec")
            pe.transpose(o[:, 0:18], vrow[:, :], ident[0:18, 0:18])
            for i in range(2):
                m = pe.transpose(o[:, 32 + HALF * i:32 + HALF * (i + 1)], prow[:, i], ident[0:HALF, 0:HALF])
            m.then_inc(full_of("vec"), 1)

            def transposes(prefix, src, ready, count):
                pe.wait_ge(ready, count)
                for j in range(4):
                    o = start(pe, f"{prefix}{j}")
                    for kk in range(2):
                        for t in range(NT):
                            k = 2 * j + kk
                            m = pe.transpose(o[:, kk * T + t * P:kk * T + t * P + P], src[:, t, k * P:(k + 1) * P], ident)
                    m.then_inc(full_of(f"{prefix}{j}"), 1)

            transposes("xT", xn, s_xn, 2)
            for j in range(4):
                taken(pe, f"xT{j}")
            cols = lambda c: (lambda w, k: w[:, k, c:c + P])
            project("qA", [("q", cols(0)), ("q", cols(P))])
            project("qB", [("q", cols(2 * P)), ("q", cols(3 * P))])
            project("kcv", [("kv1", cols(0)), ("kv1", cols(P))])
            project("ksw", [("kv1", cols(2 * P)), ("kv2", cols(0))])
            o = start(pe, "vsw")
            for t in range(NT):
                for v, (w, c) in enumerate((("kv1", 3 * P), ("kv2", P))):
                    for k in range(KD):
                        m = pe.matmul(o[:, (2 * t + v) * P:(2 * t + v + 1) * P], xT[:, k, t * P:(t + 1) * P],
                                      arrived(pe, w, k // 4)[:, k % 4, c:c + P],
                                      start=(k == 0), stop=(k == KD - 1), skip_group_check=True)
            m.then_inc(full_of("vsw"), 1)
            transposes("mT", mem_sb, s_xn, 4)
            o = start(pe, "ng")
            for t in range(NT):
                for k in range(KD):
                    m = pe.matmul(o[:, t * NGATE:(t + 1) * NGATE], xT[:, k, t * P:(t + 1) * P],
                                  arrived(pe, "kv2", k // 4)[:, k % 4, 2 * P:2 * P + NGATE],
                                  start=(k == 0), stop=(k == KD - 1), skip_group_check=True)
            m.then_inc(full_of("ng"), 1)
            for name, src, job in (("swA", qraw[:, 0:2], "qA"), ("swB", qraw[:, 2:4], "qB"), ("swk", kraw[:, :], "ksw")):
                taken(pe, job)
                o = start(pe, name)
                m = pe.matmul(o[:, :], const("swap"), src.rearrange("p a t -> p (a t)"), start=True, stop=True)
                m.then_inc(full_of(name), 1)
            project("pool", [("pq", cols(0)), ("pq", cols(P))])
            project("qm", [("pq", cols(2 * P)), ("pq", cols(3 * P))])
            o = start(pe, "hid")
            pe.wait_ge(s_cmp, 16 * 5)
            for i in range(2):
                pe.wait_ge(s_blk, 2 * i + 2)
                for l in range(HALF):
                    m = pe.matmul(o[0:HD, GROUPS * NC * i:GROUPS * NC * (i + 1)], w1[:, i, l, :],
                                  blk[:, i, l].rearrange("p g n -> p (g n)"),
                                  start=(l == 0), stop=(l == HALF - 1), skip_group_check=True)
            m.then_inc(full_of("hid"), 1)
            for j in range(4):
                taken(pe, f"mT{j}")
            o = start(pe, "km")
            for j in range(2):
                for k in range(KD):
                    m = pe.matmul(o[:, j * T:(j + 1) * T], arrived(pe, "memkv", k // 4)[:, k % 4, j * P:(j + 1) * P],
                                  memT[:, k, :], start=(k == 0), stop=(k == KD - 1), skip_group_check=True)
            m.then_inc(full_of("km"), 1)
            pe.wait_ge(s_hid, 1)
            o = start(pe, "kcvc")
            for g in range(GROUPS):
                pe.matmul(o[HD * g:HD * (g + 1), 0:NC], w2[:, 0, :], hid[:, 0, NC * g:NC * (g + 1)],
                          start=True, stop=True, skip_group_check=True)
            for g in range(GROUPS):
                m = pe.matmul(o[:, P + HD * g:P + HD * (g + 1)], hrep[:, g].rearrange("p a n -> p (a n)"), w2[:, 1, :],
                              start=True, stop=True, skip_group_check=True)
            m.then_inc(full_of("kcvc"), 1)
            o = start(pe, "vm")
            for t in range(NT):
                for k in range(KD):
                    m = pe.matmul(o[:, t * T:(t + 1) * T], memT[:, k, t * P:(t + 1) * P],
                                  arrived(pe, "memkv", k // 4)[:, k % 4, T:2 * T],
                                  start=(k == 0), stop=(k == KD - 1), skip_group_check=True)
            m.then_inc(full_of("vm"), 1)
            pe.wait_ge(s_z, 1)
            pe.wait_ge(s_pw, 16 * 4)
            pe.wait_ge(s_zeros, 1)
            o = start(pe, "zp")
            for j in range(2):
                m = pe.matmul(o[:, j * T:(j + 1) * T], wpbd[:, j, :], zt[:, j, :], start=True, stop=True,
                              skip_group_check=True)
            m.then_inc(full_of("zp"), 1)

            taken(pe, "kcvc")
            pe.wait_ge(s_cb, 1)
            for t in range(NT):
                for g in range(GROUPS):
                    name = f"cs{t}{g}"
                    o = start(pe, name)
                    rows = slice(64 * g, 64 * g + 64)
                    for h in range(4):
                        pe.matmul(o[:, 16 * h:16 * h + NC], qraw[rows, h, t * P:(t + 1) * P], kc[rows, 0:NC],
                                  start=True, stop=False, skip_group_check=True)
                        m = pe.matmul(o[:, 16 * h:16 * h + NC], b_ident, const("b_cmp")[:, t * NC:(t + 1) * NC],
                                      start=False, stop=True, skip_group_check=True)
                    m.then_inc(full_of(name), 1)

            def scores(u):
                kind, h, v = UNITS[u]
                o = start(pe, f"S{u}")
                if kind == "mem":
                    if h == 0:
                        taken(pe, "km")
                        taken(pe, "qm")
                    rows = slice(64 * (h % 2), 64 * (h % 2) + 64)
                    for t in range(NT):
                        m = pe.matmul(o[:, t * T:(t + 1) * T], qm[rows, h // 2, t * P:(t + 1) * P], km[rows, h // 2, :],
                                      start=True, stop=True, skip_group_check=True)
                else:
                    if u == 0:
                        pe.wait_ge(s_rot, 3)
                    g = h // 4
                    rows = slice(64 * g, 64 * g + 64)
                    for t in range(NT):
                        at, n = t * P, (t + 1) * P
                        pe.matmul(o[:, at:at + n], qrot[rows, h % 4, t * P:(t + 1) * P], krot[rows, v, 0:n],
                                  start=True, stop=False, skip_group_check=True)
                        m = pe.matmul(o[:, at + t * P:at + n], b_ident, const("b_causal"),
                                      start=False, stop=True, skip_group_check=True)
                m.then_inc(full_of(f"S{u}"), 1)

            def turn(u):
                pe.wait_ge(s_pr, u + 1)
                kind = UNITS[u][0]
                o = start(pe, f"T{u}")
                for src, dst in transposed(kind):
                    m = pe.transpose(o[:, dst:dst + P], pbuf[:, u % 3, src:src + P], ident)
                m.then_inc(full_of(f"T{u}"), 1)

            def values(u):
                kind, h, v = UNITS[u]
                name = f"o{pair_of(u)}"
                rows = slice(64 * (h % 2), 64 * (h % 2) + 64)
                if h % 2 == 0 and v == 0:
                    start(pe, name)
                o = ps[:, JOBS[name][0], :]
                if kind == "nsa" and v == 0:
                    if u == 0:
                        taken(pe, "ct")
                    q = slice(CP * (h % 4), CP * (h % 4) + CP)
                    pe.matmul(o[rows, 0:T], vc[q, 64 * (h // 4):64 * (h // 4) + 64], pcT[q, h // 4, :],
                              start=True, stop=False, skip_group_check=True)
                taken(pe, f"T{u}")
                pt = ptb[:, u % 2, :]
                if kind == "nsa":
                    if u == 0:
                        taken(pe, "vsw")
                    g = h // 4
                    pe.matmul(o[rows, 0:T], vnat[:, 0, v, 64 * g:64 * g + 64], pt[:, 0:T],
                              start=False, stop=False, skip_group_check=True)
                    m = pe.matmul(o[rows, P:T], vnat[:, 1, v, 64 * g:64 * g + 64], pt[:, T:T + P],
                                  start=False, stop=(v == 1), skip_group_check=True)
                    last = h % 2 == 1 and v == 1
                else:
                    if h == 0:
                        taken(pe, "vm")
                    for k in range(2):
                        m = pe.matmul(o[rows, 0:T], vm[:, k, 64 * h:64 * h + 64], pt[:, k * T:(k + 1) * T],
                                      start=(k == 0), stop=(k == 1), skip_group_check=True)
                    last = h % 2 == 1
                if last:
                    m.then_inc(full_of(name), 1)

            scores(0)
            scores(1)
            pe.wait_ge(s_cp, 1)
            o = start(pe, "ct")
            for g in range(GROUPS):
                for t in range(NT):
                    m = pe.transpose(o[:, (2 * g + t) * P:(2 * g + t + 1) * P],
                                     pc[:, t, 4 * g:4 * g + 4, :].rearrange("p h n -> p (h n)"), ident)
            m.then_inc(full_of("ct"), 1)
            for u in range(NU):
                if u + 2 < NU:
                    scores(u + 2)
                turn(u)
                for j in fillers(u):
                    project(f"mg{j}", [(f"mg{j // 4}", cols((j % 4) * P))])
                if u:
                    values(u - 1)
            values(NU - 1)

            for q in range(4):
                for b, (w, k0, nk, src) in enumerate((("upn", 0, 4, onsa), ("uppm", 0, 2, opool), ("uppm", 2, 2, omem))):
                    if q == 0:
                        for job in (("o0", "o1", "o2", "o3"), ("zp",), ("o4", "o5"))[b]:
                            taken(pe, job)
                    name = f"up{b}{q}"
                    o = start(pe, name)
                    wt = arrived(pe, w, q // 2)
                    for j in range(2):
                        c = (2 * (q % 2) + j) * P
                        for k in range(nk):
                            m = pe.matmul(o[:, j * T:(j + 1) * T], wt[:, k0 + k, c:c + P], src[:, k, :],
                                          start=(k == 0), stop=(k == nk - 1), skip_group_check=True)
                    m.then_inc(full_of(name), 1)

            pe.wait_ge(s_mrg, 4)
            def turn_h2(t):
                pe.wait_ge(s_h2, t + 1)
                for j in range(2):
                    o = start(pe, f"hT{t}{j}")
                    for kk in range(4):
                        k = 4 * j + kk
                        m = pe.transpose(o[:, kk * P:(kk + 1) * P], h2[:, t, k * P:(k + 1) * P], ident)
                    m.then_inc(full_of(f"hT{t}{j}"), 1)

            for t in range(NT):
                for half in range(2):
                    if (t, half) == (1, 1):
                        turn_h2(0)
                    name = f"acc{2 * t + half}"
                    o = start(pe, name)
                    pe.matmul(o[:, :], ident, x_sb[:, t, 512 * half:512 * half + 512], start=True, stop=False,
                              skip_group_check=True)
                    for k in range(KD):
                        m = pe.matmul(o[:, :], merged[:, k, t * P:(t + 1) * P], arrived(pe, "out", 2 * half + k // 4)[:, k % 4, :],
                                      start=False, stop=(k == KD - 1), skip_group_check=True)
                    m.then_inc(full_of(name), 1)

            pe.wait_ge(s_rt, 32)
            for t in range(NT):
                if t == 1:
                    turn_h2(1)
                for j in range(2):
                    taken(pe, f"hT{t}{j}")
                o = start(pe, f"lg{t}")
                for k in range(KD):
                    pe.matmul(o[:, 0:NE], h2T[:, k, t * P:(t + 1) * P], wrt[:, k, :],
                              start=(k == 0), stop=False, skip_group_check=True)
                m = pe.matmul(o[:, 0:NE], ones1[0:1, :], brt[0:1, :], start=False, stop=True, skip_group_check=True)
                m.then_inc(full_of(f"lg{t}"), 1)
            pe.wait_ge(s_sel, 1)
            o = start(pe, "cs")
            pe.matmul(o[:, 0:NE], const("b_before"), selb[:, 0, :], start=True, stop=True, skip_group_check=True)
            pe.matmul(o[:, NE:2 * NE], const("b_ones"), selb[:, 0, :], start=True, stop=False, skip_group_check=True)
            m = pe.matmul(o[:, NE:2 * NE], const("b_before"), selb[:, 1, :], start=False, stop=True, skip_group_check=True)
            m.then_inc(full_of("cs"), 1)
            o = start(pe, "cnt")
            for t in range(NT):
                m = pe.matmul(o[:, 0:NE], const("b_ones"), selb[:, t, :], start=(t == 0), stop=(t == 1),
                              skip_group_check=True)
            m.then_inc(full_of("cnt"), 1)
            o = start(pe, "cbT")
            for t in range(NT):
                m = pe.matmul(o[0:NE, t * P:(t + 1) * P], comb[:, t, :], ident, start=True, stop=True,
                              skip_group_check=True)
            m.then_inc(full_of("cbT"), 1)
            pe.sem_inc(s_over, 1)

            def gather(n, xbank):
                pe.wait_ge(e_oh, n + 1)
                o = ps[:, xbank, :]
                for k in range(KD):
                    for part in range(3):
                        for t in range(NT):
                            m = pe.matmul(o[:, SLOTS * k:SLOTS * (k + 1)], hpart[:, part, t, k * P:(k + 1) * P],
                                          onehot[:, t, :], start=(part == 0 and t == 0), stop=(part == 2 and t == 1),
                                          skip_group_check=True)
                m.then_inc(e_ga, 1)

            def turn_act(n, b, bank, weights):
                pe.wait_ge(e_act, 2 * n + (b + 1))
                pe.wait_ge(e_gur, 4 * n + (2 if b == 0 else 4))
                pe.sem_inc(e_turn, 1)
                for j in range(4):
                    m = pe.transpose(ps[:, bank, SLOTS * j:SLOTS * (j + 1)], a_sb[:, b, j * P:(j + 1) * P],
                                     ident[0:SLOTS, 0:SLOTS])
                if weights:
                    pe.wait_ge(e_gw, n + 1)
                    for t in range(NT):
                        m = pe.transpose(ps[:, bank, T + t * P:T + (t + 1) * P], gw[:, t, :], ident)
                m.then_inc(e_tr, 1)

            def scatter(n, parity, t):
                pe.wait_ge(e_yc, n + 1)
                for b in (2 * t, 2 * t + 1):
                    m = pe.matmul(ps[:, b, :], scat[:, parity, t * P:(t + 1) * P],
                                  y_sb[:, 512 * (b % 2):512 * (b % 2) + 512], start=False, stop=True, skip_group_check=True)
                m.then_inc(e_sc, 1)

            def expert(n, par, last):
                X, Y = ((4, 5), (6, 7)) if par == 0 else ((6, 7), (4, 5))
                banks = (X[0], X[1], Y[0], Y[1])

                def passes(i, stationary, bank, first):
                    k0 = 4 * (i % 2) if i < 8 else 4 * ((i - 8) // 2)
                    split(pe, n, i)
                    for w in (whi, wlo):
                        for k in range(4):
                            m = pe.matmul(ps[:, bank, :], stationary[:, k0 + k, :], w[:, i % SPLIT, k, :],
                                          start=(first and w is whi and k == 0), stop=True, skip_group_check=True)
                    m.then_inc(e_mul, 1)

                for q in range(4):
                    if q == 0:
                        pe.wait_ge(e_trl, 2 * n + 1)
                        pe.wait_ge(e_bs, n + 1)
                        pe.wait_ge(e_gah, n + 1)
                        pe.wait_ge(e_gal, n + 1)
                    if q == 1:
                        pe.wait_ge(e_gur, 4 * n + 1)
                    if q == 2:
                        pe.wait_ge(e_yc, n + 1)
                    col = (0, FF, 512, FF + 512)[q]
                    pe.matmul(ps[:, banks[q], :], bsel[:, par, :], bparts[:, col:col + 512], start=True, stop=False,
                              skip_group_check=True)
                    for i in (2 * q, 2 * q + 1):
                        passes(i, xe[:, par], banks[q], False)
                    if q == 2:
                        turn_act(n, 0, X[0], True)
                        if not last:
                            pe.wait_ge(e_gur, 4 * n + 3)
                            gather(n + 1, X[1])
                scatter(n, 1 - par, 0)
                pe.wait_ge(e_trl, 2 * n + 2)
                pe.wait_ge(e_st, n + 2)
                passes(8, aT, X[0], True)
                if last:
                    pe.wait_ge(e_gur, 4 * n + 3)
                else:
                    pe.wait_ge(e_gah, n + 2)
                    pe.wait_ge(e_gal, n + 2)
                passes(9, aT, X[1], True)
                turn_act(n, 1, Y[0], False)
                scatter(n, 1 - par, 1)
                pe.wait_ge(e_trl, 2 * n + 3)
                passes(10, aT, X[0], False)
                passes(11, aT, X[1], False)

            pe.wait_ge(s_over, 4)
            gather(0, 5)
            taken(pe, "cbT")
            pe.wait_ge(s_bdn, 16)
            for b in range(4):
                pe.matmul(ps[:, b, :], cbT[:, (b // 2) * P:(b // 2 + 1) * P], bdn[:, 512 * (b % 2):512 * (b % 2) + 512],
                          start=False, stop=True, skip_group_check=True)
            pe.wait_ge(s_init, 3)
            more_rounds = pe.value_load(rounds[0:1, 0:1], min_val=0, max_val=ROUNDS - 1)
            with pe.Fori(0, more_rounds * (NE // 2) + (NE // 2 - 1)) as i:
                expert(i * 2, 0, False)
                expert(i * 2 + 1, 1, False)
            expert(more_rounds * NE + (NE - 2), 0, False)
            expert(more_rounds * NE + (NE - 1), 1, True)
            for t in range(NT):
                scatter(more_rounds * NE + NE, 1, t)

        @block.scalar
        def _(act):
            act.dma_start(x_sb[:, :, :], x_d).then_inc(s_x, 16)
            act.dma_start(cst[:, :], ins["consts"][:, 0:NF]).then_inc(s_const, 16)
            act.dma_start(vrow[0:8, :], ins["norm_mix"][0].rearrange("(k p) -> k p", p=P)).then_inc(s_vec, 16)
            act.dma_start(vrow[8:16, :], ins["norm_mem"][0].rearrange("(k p) -> k p", p=P)).then_inc(s_vec, 16)
            act.dma_start(vrow[16:18, :], ins["pool_scale"][0].rearrange("(k p) -> k p", p=P)).then_inc(s_vec, 16)
            act.dma_start(prow[:, :, :], ins["cmp_pos"][0].rearrange("i (l a) d -> l i (a d)", a=2)).then_inc(s_vec, 16)
            act.dma_start(mem_sb[:, :, :], mem_d).then_inc(s_mem, 16)

            def sumsq(src, junk, t, count):
                act.activation(junk, src, ACT.Square, accum_out=stat[:, t:t + 1]).then_inc(s_ss, 1)
                act.wait_ge(s_ss, count)

            def deviation(count, lo, cols=(0, NT)):
                act.wait_ge(s_var, count)
                a = stat[:, lo + 2 + cols[0]:lo + 2 + cols[1]]
                act.activation(a, a, ACT.Sqrt).then_inc(s_sd, 1)

            def take(name, dst, o=None, **kw):
                o = computed(act, name) if o is None else o
                act.activation(dst, o, kw.pop("func", ACT.Copy), **kw).then_inc(free_of(name), 1)

            act.wait_ge(s_x, 16)
            for t in range(NT):
                sumsq(x_sb[:, t, :], xn[:, t, :], t, t + 1)
            deviation(1, 0)
            o = computed(act, "vec")
            act.activation(vcol[:, 0:18], o[:, 0:18], ACT.Copy)
            take("vec", vcol[:, 32:32 + CMP_BLOCK], o[:, 32:32 + CMP_BLOCK])
            act.wait_ge(s_mem, 16)
            for t in range(NT):
                sumsq(mem_sb[:, t, :], bufM[:, t * D:(t + 1) * D], 4 + t, t + 3)
            deviation(2, 4)
            take("qA", qraw[:, 0:2].rearrange("p a t -> p (a t)"))
            take("qB", qraw[:, 2:4].rearrange("p a t -> p (a t)"))
            o = computed(act, "kcv")
            act.activation(kcv[:, :].rearrange("p a t -> p (a t)"), o, ACT.Copy)
            act.activation(kswap[HD:P].rearrange("p a t -> p (a t)"), o[0:HD], ACT.Copy)
            take("kcv", kswap[0:HD].rearrange("p a t -> p (a t)"), o[HD:P])
            take("ksw", kraw[:, :].rearrange("p a t -> p (a t)"))
            take("vsw", vnat[:, :].rearrange("p t v d -> p (t v d)"))
            o = computed(act, "ng")
            take("ng", gates[:, :].rearrange("p t n -> p (t n)"), o[:, 0:NT * NGATE], func=ACT.Exp, scale=-1.0)
            o = computed(act, "pool")
            take("pool", pb[0][:, :, PAD:], o[:, :].rearrange("p (a t) -> p a t", a=2))
            take("qm", qm[:, :].rearrange("p a t -> p (a t)"))
            o = computed(act, "hid")
            act.activation(hide[:, :, :].rearrange("p i n -> p (i n)"), o[0:HD, 0:2 * GROUPS * NC], ACT.Exp,
                           scale=-1.0).then_inc(s_hexp, 1)
            take("km", km[:, :].rearrange("p a t -> p (a t)"))
            take("vm", vm[:, :].rearrange("p a t -> p (a t)"))
            o = computed(act, "zp")
            act.activation(opool[:, 0, :], o[:, 0:T], ACT.Copy, scale=vcol[:, 16:17])
            take("zp", opool[:, 1, :], o[:, T:2 * T], scale=vcol[:, 17:18])
            act.wait_ge(s_cd, 4)
            pcv = pc[:, :, :, :].rearrange("p t h n -> p (t h) n")[:, :, 0:NC]
            act.activation(pcv, pcv, ACT.Exp, scale=SCALE).then_inc(s_ce, 1)

            def unit_exp(u):
                act.wait_ge(s_nm, u + 1)
                o = ps[:, JOBS[f"S{u}"][0], :]
                for t, (a, b) in enumerate(spans(UNITS[u][0])):
                    m = act.activation(pbuf[:, u % 3, a:b], o[:, a:b], ACT.Exp, bias=us[:, u % 3, 2 + t:3 + t],
                                       scale=SCALE, accum_out=us[:, u % 3, 4 + t:5 + t])
                m.then_inc(free_of(f"S{u}"), 1)

            def take_pair(u):
                pair = pair_of(u)
                o = computed(act, f"o{pair}")
                dst = onsa[:, pair, :] if pair < 4 else omem[:, pair - 4, :]
                take(f"o{pair}", dst, o[:, 0:T])

            unit_exp(0)
            unit_exp(1)
            take("ct", pcT[:, :].rearrange("p g t -> p (g t)"))
            for u in range(NU):
                if u + 2 < NU:
                    unit_exp(u + 2)
                n = 512 if UNITS[u][0] == "mem" else 3 * P
                o = computed(act, f"T{u}")
                take(f"T{u}", ptb[:, u % 2, 0:n], o[:, 0:n])
                for j in fillers(u):
                    o = computed(act, f"mg{j}")
                    take(f"mg{j}", sig[:, j, :], o[:, 0:T], func=ACT.Exp, scale=-1.0)
                if u and last_of_pair(u - 1):
                    take_pair(u - 1)
            take_pair(NU - 1)

            def first_hi(i):
                act.wait_ge(landed[i % RAW], LANDED0[i % RAW] + 16)
                act.activation(whi[:, i], raw[:, i], ACT.Copy).then_inc(e_hi, 1)

            act.wait_ge(s_mrg, 4)
            first_hi(0)
            first_hi(1)

            def next_part(part, t):
                if part:
                    act.wait_ge(s_rest, NT * (part - 1) + t + 1)
                src = bufM if part else bufB
                act.activation(hpart[:, part, t, :], src[:, t * D:(t + 1) * D], ACT.Copy).then_inc(s_part, 1)

            for t in range(NT):
                computed(act, f"acc{2 * t}")
                computed(act, f"acc{2 * t + 1}")
                sumsq(ps[:, 2 * t:2 * t + 2, :].rearrange("p b n -> p (b n)"), h2[:, t, :], 8 + t, t + 5)
                deviation(3 + t, 8, (t, t + 1))
                act.wait_ge(s_h2, t + 1)
                next_part(0, t)

            def router_exp(t):
                act.wait_ge(s_rv, t + 1)
                act.activation(ex4[:, t, 0:TOPK], top[:, t, 0:TOPK], ACT.Exp, bias=ex4[:, t, 5:6],
                               accum_out=ex4[:, t, 4:5]).then_inc(s_re, 1)

            next_part(1, 0)
            router_exp(0)
            next_part(1, 1)
            next_part(2, 0)
            router_exp(1)
            next_part(2, 1)
            first_hi(2)
            first_hi(3)
            o = computed(act, "cbT")
            take("cbT", cbT[:, :], o[0:NE, 0:T])
            taken(act, "cbT")
            act.wait_ge(s_part, 3 * NT)
            act.sem_inc(s_over, 1)

            act.wait_ge(s_over, 4)
            for signal in (e_yc, e_st):
                act.sem_inc(signal, 1)
            act.dma_start(gfin[:, :], ins["norm_final"].partition_broadcast(P)).then_inc(s_gf, 16)

            def tokens_hi(n, par, bank):
                act.wait_ge(e_ga, n + 1)
                act.activation(xe[:, par, :, 0:SLOTS], ps[:, bank, :].rearrange("p (k s) -> p k s", s=SLOTS),
                               ACT.Copy).then_inc(e_gah, 1)

            def expert(n, par, last):
                X, Y = ((4, 5), (6, 7)) if par == 0 else ((6, 7), (4, 5))
                banks = (X[0], X[1], Y[0], Y[1])
                more = lambda i: i + SPLIT < EXPERT_CHUNKS or not last

                def ahead(i):
                    if more(i):
                        act.wait_ge(e_mul, n * EXPERT_CHUNKS + (i + 1))
                        c = i + SPLIT
                        act.wait_ge(landed[c % RAW], n * 32 + (LANDED0[c % RAW] + 16 * (c // RAW + 1)))
                        act.activation(whi[:, c % SPLIT], raw[:, c % RAW], ACT.Copy).then_inc(e_hi, 1)

                def low_rows(q):
                    act.wait_ge(e_mul, n * EXPERT_CHUNKS + (2 * q + 2))
                    act.activation((glow, ulow)[q % 2][:, :], ps[SLOTS:P, banks[q], :], ACT.Copy).then_inc(e_low, 1)

                def sigmoid(b):
                    act.wait_ge(e_gm, n * 2 + (b + 1))
                    act.activation(s_sb[:, :], g_sb[:, :], ACT.Sigmoid, scale=ALPHA).then_inc(e_sg, 1)

                def act_hi(b, bank):
                    act.wait_ge(e_tr, n * 2 + (b + 1))
                    act.activation(aT[:, 4 * b:4 * b + 4, 0:SLOTS],
                                   ps[:, bank, 0:4 * SLOTS].rearrange("p (k s) -> p k s", s=SLOTS),
                                   ACT.Copy).then_inc(e_trh, 1)

                ahead(0)
                low_rows(0)
                ahead(1)
                ahead(2)
                sigmoid(0)
                low_rows(1)
                ahead(3)
                ahead(4)
                act.wait_ge(e_tr, n * 2 + 1)
                act.activation(scat[:, par, :], ps[:, X[0], T:2 * T], ACT.Copy).then_inc(e_st, 1)
                act_hi(0, X[0])
                low_rows(2)
                if not last:
                    tokens_hi(n + 1, 1 - par, X[1])
                ahead(5)
                ahead(6)
                sigmoid(1)
                low_rows(3)
                ahead(7)
                ahead(8)
                act_hi(1, Y[0])
                ahead(9)
                ahead(10)
                act.wait_ge(e_mul, n * EXPERT_CHUNKS + EXPERT_CHUNKS)
                act.activation(y_sb[:, :], ps[:, X[0]:X[0] + 2, :].rearrange("p b n -> p (b n)"), ACT.Copy).then_inc(e_yc, 1)
                ahead(11)

            tokens_hi(0, 0, 5)
            more_rounds = act.value_load(rounds[0:1, 0:1], min_val=0, max_val=ROUNDS - 1)
            with act.Fori(0, more_rounds * (NE // 2) + (NE // 2 - 1)) as i:
                expert(i * 2, 0, False)
                expert(i * 2 + 1, 1, False)
            expert(more_rounds * NE + (NE - 2), 0, False)
            expert(more_rounds * NE + (NE - 1), 1, True)

            for t in range(NT):
                act.wait_ge(e_sc, more_rounds * (2 * NE) + (2 * NE + 1 + t))
                sumsq(ps[:, 2 * t:2 * t + 2, :].rearrange("p b n -> p (b n)"), y_out(NT + t), 12 + t, t + 7)
            deviation(5, 12)

        @block.vector
        def _(dve):
            n_link = [0]

            def link(m):
                n_link[0] += 1
                m.then_inc(s_dve, 1)
                dve.wait_ge(s_dve, n_link[0])

            def variance(lo, squares, count, cols=(0, NT)):
                sums, var = stat[:, lo + cols[0]:lo + cols[1]], stat[:, lo + 2 + cols[0]:lo + 2 + cols[1]]
                dve.wait_ge(s_ss, squares)
                dve.tensor_scalar(var, sums, 1.0 / D, EPS, ALU.mult, ALU.add).then_inc(s_var, 1)
                dve.wait_ge(s_sd, count)
                link(dve.reciprocal(sums, var))

            def sigmoid_of_exp(a):
                link(dve.tensor_scalar(a, a, 1.0, None, ALU.add))
                link(dve.reciprocal(a, a))

            dve.memset(ones1[:, :], 1.0).then_inc(s_zero, 1)
            dve.memset(pc[:, :, :, :], 0.0).then_inc(s_zero, 1)
            link(dve.memset(hrep[:, :, :, :], 0.0))
            variance(0, 2, 1)
            for t in range(NT):
                dve.tensor_scalar(xn[:, t, :], x_sb[:, t, :], stat[:, t:t + 1], None, ALU.mult).then_inc(s_xn, 1)
            taken(dve, "vec")

            def scaled(name, dst, col):
                o = computed(dve, name)
                dve.tensor_tensor(dst, o[:, :].rearrange("p (k t) -> p k t", t=T),
                                  vcol[:, col:col + 2].unsqueeze(2).to_broadcast([P, 2, T]), ALU.mult).then_inc(free_of(name), 1)

            for j in range(4):
                scaled(f"xT{j}", xT[:, 2 * j:2 * j + 2, :], 2 * j)
            variance(4, 4, 2)
            for t in range(NT):
                dve.tensor_scalar(mem_sb[:, t, :], mem_sb[:, t, :], stat[:, 4 + t:5 + t], None, ALU.mult).then_inc(s_xn, 1)
            dve.wait_ge(s_cst2, 16)
            dve.tensor_copy(cb[:, :], cstage[:, :]).then_inc(s_cb, 1)
            for j in range(4):
                scaled(f"mT{j}", memT[:, 2 * j:2 * j + 2, :], 8 + 2 * j)
            taken(dve, "ng")
            sigmoid_of_exp(gates[:, :, :].rearrange("p t n -> p (t n)"))
            dve.wait_ge(s_const, 16)
            for name, job, src, dst in (("swA", "qA", qraw[:, 0:2], qrot[:, 0:2]), ("swB", "qB", qraw[:, 2:4], qrot[:, 2:4]),
                                        ("swk", "ksw", kraw[:, :], krot[:, :])):
                o = computed(dve, name)
                taken(dve, job)
                wide = lambda c: const(c).unsqueeze(1).to_broadcast([P, 2, T])
                own = rtmp[:, 0, :].rearrange("p (a t) -> p a t", a=2)
                other = rtmp[:, 1, :].rearrange("p (a t) -> p a t", a=2)
                dve.tensor_tensor(other, o[:, :].rearrange("p (a t) -> p a t", a=2), wide("sin"), ALU.mult).then_inc(free_of(name), 1)
                taken(dve, name)
                link(dve.tensor_tensor(own, src, wide("cos"), ALU.mult))
                dve.tensor_tensor(dst, own, other, ALU.add).then_inc(s_rot, 1)
                dve.wait_ge(s_rot, {"swA": 1, "swB": 2, "swk": 3}[name])
            o = computed(dve, "hid")
            dve.wait_ge(s_hexp, 1)
            sigmoid_of_exp(hide[:, :, :])
            dve.tensor_tensor(hid[:, :, :].rearrange("p i n -> p (i n)"), o[0:HD, 0:2 * GROUPS * NC],
                              hide[:, :, :].rearrange("p i n -> p (i n)"), ALU.mult).then_inc(free_of("hid"), 1)
            taken(dve, "hid")
            for g in range(GROUPS):
                m = dve.tensor_copy(hrep[:, g, :, 0:NC], hid[:, 1:2, NC * g:NC * (g + 1)].to_broadcast([HD, 4, NC]))
            m.then_inc(s_hid, 1)
            o = computed(dve, "kcvc")
            dve.tensor_copy(kc[:, 0:NC], o[:, 0:NC])
            dve.tensor_copy(vc[:, :], o[:, P:2 * P]).then_inc(free_of("kcvc"), 1)

            for t in range(NT):
                for g in range(GROUPS):
                    name = f"cs{t}{g}"
                    o = computed(dve, name)[:, 0:64].rearrange("p (h n) -> p h n", h=4)[:, :, 0:NC]
                    mx = sm[:, 0, 8 * t + 4 * g:8 * t + 4 * g + 4]
                    link(dve.tensor_reduce(mx, o, AX, ALU.max))
                    dve.tensor_tensor(pc[:, t, 4 * g:4 * g + 4, 0:NC], o, mx.unsqueeze(2).to_broadcast([P, 4, NC]),
                                      ALU.subtract).then_inc(s_cd, 1)
                    dve.wait_ge(s_cd, 2 * t + g + 1)
                    dve.sem_inc(free_of(name), 1)
            pcv = pc[:, :, :, :].rearrange("p t h n -> p (t h) n")[:, :, 0:NC]
            dve.wait_ge(s_ce, 1)
            for t in range(NT):
                seen = const("seen")[:, t * NC:(t + 1) * NC].unsqueeze(1).to_broadcast([P, HEADS, NC])
                link(dve.tensor_tensor(pc[:, t, :, 0:NC], pc[:, t, :, 0:NC], seen, ALU.mult))
            link(dve.tensor_reduce(sm[:, 1, :], pcv, AX, ALU.add))
            link(dve.tensor_scalar(sm[:, 1, :], sm[:, 1, :], TINY, None, ALU.max))
            link(dve.reciprocal(sm[:, 2, :], sm[:, 1, :]))
            link(dve.tensor_tensor(sm[:, 3, :].rearrange("p (t h) -> p t h", t=NT), sm[:, 2, :].rearrange("p (t h) -> p t h", t=NT),
                                   gates[:, :, :].rearrange("p t (h b) -> p t h b", b=3)[:, :, :, 0], ALU.mult))
            dve.tensor_tensor(pcv, pcv, sm[:, 3, :].unsqueeze(2).to_broadcast([P, 16, NC]), ALU.mult).then_inc(s_cp, 1)

            def unit_max(u):
                o = computed(dve, f"S{u}")
                for t, (a, b) in enumerate(spans(UNITS[u][0])):
                    link(dve.tensor_reduce(us[:, u % 3, t:t + 1], o[:, a:b], AX, ALU.max))
                dve.tensor_scalar(us[:, u % 3, 2:4], us[:, u % 3, 0:2], -SCALE, None, ALU.mult).then_inc(s_nm, 1)

            def unit_norm(u):
                kind, h, v = UNITS[u]
                taken(dve, f"S{u}")
                link(dve.reciprocal(us[:, u % 3, 6:8], us[:, u % 3, 4:6]))
                if kind == "nsa":
                    link(dve.tensor_tensor(us[:, u % 3, 6:8], us[:, u % 3, 6:8], gates[:, :, 3 * h + 1 + v], ALU.mult))
                for t, (a, b) in enumerate(spans(kind)):
                    m = dve.tensor_scalar(pbuf[:, u % 3, a:b], pbuf[:, u % 3, a:b], us[:, u % 3, 6 + t:7 + t], None, ALU.mult)
                m.then_inc(s_pr, 1)

            unit_max(0)
            unit_max(1)
            unit_norm(0)
            for u in range(NU):
                if u + 2 < NU:
                    unit_max(u + 2)
                if u + 1 < NU:
                    unit_norm(u + 1)
                for j in fillers(u):
                    taken(dve, f"mg{j}")
                    sigmoid_of_exp(sig[:, j, :])

            for q in range(4):
                for b in range(3):
                    name = f"up{b}{q}"
                    o = computed(dve, name)[:, :].rearrange("p (a t) -> p a t", a=2)
                    gate = sig[:, 8 * b + 2 * q:8 * b + 2 * q + 2, :]
                    part = merged[:, 2 * q:2 * q + 2, :]
                    dst = part if b == 0 else pbuf[:, b, :].rearrange("p (a t) -> p a t", a=2)
                    dve.tensor_tensor(dst, o, gate, ALU.mult).then_inc(free_of(name), 1)
                    taken(dve, name)
                    if b == 1:
                        link(dve.tensor_tensor(part, part, dst, ALU.add))
                    if b == 2:
                        dve.tensor_tensor(part, part, dst, ALU.add).then_inc(s_mrg, 1)

            def split_lo(c, i):
                if i % EXPERT_CHUNKS not in POOL_LO:
                    dve.wait_ge(e_hi, c)
                    dve.tensor_tensor(wlo[:, i % SPLIT], raw[:, i % RAW], whi[:, i % SPLIT].bitcast(F32),
                                      ALU.subtract).then_inc(e_lo[False], 1)

            split_lo(1, 0)
            split_lo(2, 1)
            dve.wait_ge(s_gffn, 16)
            for t in range(NT):
                variance(8, 5 + t, 3 + t, (t, t + 1))
                dve.scalar_tensor_tensor(h2[:, t, :], ps[:, 2 * t:2 * t + 2, :].rearrange("p b n -> p (b n)"), stat[:, 8 + t:9 + t],
                                         gffn, ALU.mult, ALU.mult).then_inc(s_h2, 1)
                for j in range(2):
                    o = computed(dve, f"hT{t}{j}")[:, :].rearrange("p (k t) -> p k t", t=P)
                    dve.tensor_copy(h2T[:, 4 * j:4 * j + 4, t * P:(t + 1) * P], o).then_inc(free_of(f"hT{t}{j}"), 1)
            for t in range(NT):
                o = computed(dve, f"lg{t}")
                dve.tensor_copy(lgt[:, t, :], o[:, 0:NE]).then_inc(free_of(f"lg{t}"), 1)
                taken(dve, f"lg{t}")
                link(dve.max(top[:, t, :], lgt[:, t, :]))
                link(dve.max_index(topi[:, t, :], top[:, t, :], lgt[:, t, :]))
                dve.tensor_scalar(ex4[:, t, 5:6], top[:, t, 0:1], -1.0, None, ALU.mult).then_inc(s_rv, 1)
                link(dve.tensor_copy(topf[:, t, :], topi[:, t, :]))
                dve.wait_ge(s_re, t + 1)
                link(dve.reciprocal(ex4[:, t, 6:7], ex4[:, t, 4:5]))
                link(dve.tensor_scalar(ex4[:, t, 0:4], ex4[:, t, 0:4], ex4[:, t, 6:7], None, ALU.mult))
                for j in range(TOPK):
                    dst = comb if j == 0 else rtm
                    link(dve.tensor_scalar(dst[:, t, :], const("iota"), topf[:, t, j:j + 1], ex4[:, t, j:j + 1],
                                           ALU.is_equal, ALU.mult))
                    if j:
                        link(dve.tensor_tensor(comb[:, t, :], comb[:, t, :], rtm[:, t, :], ALU.add))
            dve.tensor_scalar(selb[:, :, :], comb[:, :, :], 0.0, None, ALU.is_gt).then_inc(s_sel, 1)
            dve.wait_ge(s_sel, 1)
            o = computed(dve, "cs")
            dve.scalar_tensor_tensor(rtm[:, :, :].rearrange("p t e -> p (t e)"), o[:, 0:NT * NE], 1.0,
                                     selb[:, :, :].rearrange("p t e -> p (t e)"), ALU.add, ALU.mult).then_inc(free_of("cs"), 1)
            taken(dve, "cs")
            for i in range(ROUNDS):
                dve.tensor_scalar(pos[:, :, NE * i:NE * (i + 1)], rtm[:, :, :], -1.0 - SLOTS * i, None, ALU.add)
                link(dve.tensor_copy(wgt[:, :, NE * i:NE * (i + 1)], comb[:, :, :]))
            o = computed(dve, "cnt")
            dve.tensor_reduce(cntb[:, 0:1], o[0:1, 0:NE], AX, ALU.max).then_inc(free_of("cnt"), 1)
            taken(dve, "cnt")
            link(dve.tensor_scalar(cntb[:, 1:2], cntb[:, 0:1], float(SLOTS), None, ALU.is_gt))
            for i in range(2, ROUNDS):
                link(dve.tensor_scalar(cntb[:, 2:3], cntb[:, 0:1], float(SLOTS * i), None, ALU.is_gt))
                link(dve.tensor_tensor(cntb[:, 1:2], cntb[:, 1:2], cntb[:, 2:3], ALU.add))
            dve.tensor_copy(rounds[:, :], cntb[:, 1:2]).then_inc(s_rounds, 1)
            dve.wait_ge(s_rounds, 1)
            dve.sem_inc(s_over, 1)

            dve.wait_ge(s_over, 4)
            for signal in (e_trl, e_gur):
                dve.sem_inc(signal, 1)

            def make_onehot(n):
                for t in range(NT):
                    m = dve.tensor_scalar(onehot[:, t, :], const("slot")[:, 0:SLOTS], col(pos, t, n), None, ALU.is_equal)
                m.then_inc(e_oh, 1)

            def col(table, t, n):
                return table[:, t, n:n + 1] if isinstance(n, int) else table[:, t, bass.ds(n, 1)]

            def tokens_lo(n, par, bank):
                dve.wait_ge(e_gah, n + 1)
                dve.tensor_tensor(xe[:, par, :, SLOTS:P], ps[:, bank, :].rearrange("p (k s) -> p k s", s=SLOTS),
                                  xe[:, par, :, 0:SLOTS].bitcast(F32), ALU.subtract).then_inc(e_gal, 1)

            def expert(n, par, last):
                X, Y = ((4, 5), (6, 7)) if par == 0 else ((6, 7), (4, 5))
                banks = (X[0], X[1], Y[0], Y[1])

                def ahead(i):
                    if i + SPLIT < EXPERT_CHUNKS or not last:
                        split_lo(n * EXPERT_CHUNKS + (i + SPLIT + 1), i + SPLIT)

                def both_rows(q):
                    dve.wait_ge(e_low, n * 4 + (q + 1))
                    dve.tensor_tensor((g_sb, u_sb)[q % 2][:, :], ps[0:SLOTS, banks[q], :], (glow, ulow)[q % 2][:, :],
                                      ALU.add).then_inc(e_gur, 1)
                    dve.wait_ge(e_gur, n * 4 + (q + 2))

                def gate(b):
                    both_rows(2 * b)
                    dve.tensor_scalar(g_sb[:, :], g_sb[:, :], LIMIT, None, ALU.min).then_inc(e_gm, 1)

                def up(b):
                    both_rows(2 * b + 1)
                    dve.tensor_scalar(u_sb[:, :], u_sb[:, :], LIMIT, -LIMIT, ALU.min, ALU.max).then_inc(e_dv, 1)
                    dve.wait_ge(e_gm, n * 2 + (b + 1))
                    dve.wait_ge(e_dv, n * 4 + (2 * b + 1))
                    dve.scalar_tensor_tensor(u_sb[:, :], u_sb[:, :], 1.0, g_sb[:, :], ALU.add, ALU.mult).then_inc(e_dv, 1)
                    dve.wait_ge(e_dv, n * 4 + (2 * b + 2))
                    dve.wait_ge(e_sg, n * 2 + (b + 1))
                    dve.tensor_tensor(a_sb[:, b, :], u_sb[:, :], s_sb[:, :], ALU.mult).then_inc(e_act, 1)

                def act_lo(b, bank):
                    dve.wait_ge(e_trh, n * 2 + (b + 1))
                    dve.tensor_tensor(aT[:, 4 * b:4 * b + 4, SLOTS:P], ps[:, bank, 0:4 * SLOTS].rearrange("p (k s) -> p k s", s=SLOTS),
                                      aT[:, 4 * b:4 * b + 4, 0:SLOTS].bitcast(F32), ALU.subtract).then_inc(e_trl, 1)

                dve.wait_ge(e_st, n + 1)
                for t in range(NT):
                    m = dve.tensor_scalar(gw[:, t, :], const("slot"), col(pos, t, n), col(wgt, t, n), ALU.is_equal, ALU.mult)
                m.then_inc(e_gw, 1)
                if not last:
                    dve.wait_ge(e_ga, n + 1)
                    make_onehot(n + 1)
                ahead(0)
                gate(0)
                ahead(1)
                ahead(2)
                up(0)
                ahead(3)
                ahead(4)
                dve.wait_ge(e_st, n + 2)
                act_lo(0, X[0])
                gate(1)
                if not last:
                    tokens_lo(n + 1, 1 - par, X[1])
                ahead(5)
                ahead(6)
                up(1)
                ahead(7)
                ahead(8)
                act_lo(1, Y[0])
                ahead(9)
                ahead(10)
                ahead(11)

            make_onehot(0)
            dve.memset(y_sb[:, :], 0.0).then_inc(s_init, 1)
            dve.memset(scat[:, 1, :], 0.0).then_inc(s_init, 1)
            split_lo(4, 3)
            tokens_lo(0, 0, 5)
            more_rounds = dve.value_load(rounds[0:1, 0:1], min_val=0, max_val=ROUNDS - 1)
            with dve.Fori(0, more_rounds * (NE // 2) + (NE // 2 - 1)) as i:
                expert(i * 2, 0, False)
                expert(i * 2 + 1, 1, False)
            expert(more_rounds * NE + (NE - 2), 0, False)
            expert(more_rounds * NE + (NE - 1), 1, True)

            variance(12, 8, 5)
            dve.wait_ge(s_gf, 16)
            for t in range(NT):
                dve.scalar_tensor_tensor(y_out(t), ps[:, 2 * t:2 * t + 2, :].rearrange("p b n -> p (b n)"), stat[:, 12 + t:13 + t],
                                         gfin[:, :], ALU.mult, ALU.mult).then_inc(s_fin, 1)

        @block.gpsimd
        def _(pool):
            n_link = [0]

            def link(m):
                n_link[0] += 1
                m.then_inc(s_pool, 1)
                pool.wait_ge(s_pool, n_link[0])

            pool.dma_start(cstage[:, :], ins["consts"][:, NF:NCONST]).then_inc(s_cst2, 16)
            link(pool.memset(wpbd[0:HD, :, HD:P], 0.0))
            link(pool.memset(wpbd[HD:P, :, 0:HD], 0.0))
            for b in pb:
                link(pool.memset(b[:, :, 0:PAD], 0.0))
            pool.sem_inc(s_zeros, 1)
            for g in range(GROUPS):
                rows = slice(HD * g, HD * g + HD)
                for i in range(2):
                    src = ins["cmp_w1"][0, i].rearrange("(l a) d e -> a d l e", a=2)[g]
                    pool.dma_start(w1[rows, i], src).then_inc(s_cmp, 16)
                for j in range(2):
                    pool.dma_start(wpbd[rows, j, rows], ins["w_pool"][0, 2 * j + g]).then_inc(s_pw, 16)
            pool.dma_start(w2[:, :, :], ins["cmp_w2"][0].rearrange("i e f -> e i f")).then_inc(s_cmp, 16)
            pool.dma_start(wrt[:, :, :], ins["w_router"][0].rearrange("(k p) e -> p k e", p=P)).then_inc(s_rt, 16)
            pool.dma_start(brt[:, :], ins["b_router"]).then_inc(s_rt, 16)

            taken(pool, "vec")
            taken(pool, "kcv")
            for i in range(2):
                for odd in range(2):
                    rows = slice(HD * odd, HD * (odd + 1))
                    for g in range(GROUPS):
                        src = kcv if g == odd else kswap
                        tok = src[rows, i, :].rearrange("p (n l a) -> p a l n", a=2, l=CMP_STRIDE // 2)[:, odd]
                        for half in range(2):
                            l = slice(8 * half, 8 * half + 8)
                            at = 32 + HALF * i
                            posn = vcol[rows, at + 8 * half:at + 8 * half + 8].unsqueeze(2).to_broadcast([HD, 8, NC])
                            m = pool.tensor_tensor(blk[rows, i, l, g], tok[:, :, half:half + NC], posn, ALU.add)
                    m.then_inc(s_blk, 1)
                    pool.wait_ge(s_blk, 2 * i + odd + 1)

            taken(pool, "pool")
            a, b, c = pb
            lo, hi = slice(0, HD), slice(HD, P)

            def doubled(dst, src, rows, blocks, shift):
                link(pool.tensor_tensor(dst[rows, blocks, PAD:], src[rows, blocks, PAD:],
                                        src[rows, blocks, PAD - shift:PAD + T - shift], ALU.add))

            doubled(b, a, slice(0, P), slice(0, 2), 1)
            doubled(c, b, slice(0, P), slice(0, 2), 2)
            doubled(b, c, slice(0, P), slice(1, 2), 4)
            doubled(c, b, hi, slice(1, 2), 8)
            pinv = const("pinv").rearrange("p (j t) -> p j t", j=2)
            pool.wait_ge(s_const, 16)
            for j in range(2):
                for rows, src in ((lo, b), (hi, c)):
                    link(pool.tensor_tensor(zt[rows, j, :], src[rows, j, PAD:], pinv[rows, j, :], ALU.mult))
            pool.tensor_tensor(zt[:, :, :], zt[:, :, :], a[:, :, PAD:], ALU.subtract).then_inc(s_z, 1)

            computed(pool, "km")
            computed(pool, "vm")
            for i in range(3):
                pool.dma_start(bsrc[NE * i:NE * (i + 1), :], ins["b_gate_up"][0]).then_inc(s_bias, 16)
            pool.dma_start(gffn, ins["norm_ffn"][0].partition_broadcast(P)).then_inc(s_gffn, 16)
            pool.dma_start(bdn, ins["b_down"][0]).then_inc(s_bdn, 16)
            pool.wait_ge(s_bias, 48)
            for i in range(3):
                for j in range(i, 3):
                    rows = slice(NE * j, NE * (j + 1))
                    link(pool.tensor_copy(bparts[rows, :], bsrc[rows, :]))
                    if j > i:
                        link(pool.tensor_tensor(bsrc[rows, :], bsrc[rows, :], bparts[rows, :], ALU.subtract))
            def lo_part(n, i):
                pool.wait_ge(e_hi, n * EXPERT_CHUNKS + (i + 1))
                pool.tensor_tensor(wlo[:, i % SPLIT], raw[:, i % RAW], whi[:, i % SPLIT].bitcast(F32),
                                   ALU.subtract).then_inc(e_lo[True], 1)

            for part in range(2):
                for t in range(NT):
                    pool.wait_ge(s_part, NT * part + t + 1)
                    src, rest = bufM if part else bufB, bufM[:, t * D:(t + 1) * D]
                    pool.tensor_tensor(rest, src[:, t * D:(t + 1) * D], hpart[:, part, t, :], ALU.subtract).then_inc(s_rest, 1)
            lo_part(0, POOL_LO[0])
            pool.wait_ge(s_rest, 2 * NT)
            pool.sem_inc(s_over, 1)

            pool.wait_ge(s_over, 4)
            pool.memset(bsel[:, :, SLOTS:P], 0.0).then_inc(s_init, 1)

            def bias_row(e, par):
                e = e if isinstance(e, int) else e % NE
                src = const("b_expert")[0:96]
                pool.wait_ge(s_init, 3)
                src = src[:, e:e + 1] if isinstance(e, int) else src[:, bass.ds(e, 1)]
                pool.tensor_copy(bsel[:, par, 0:SLOTS], src.to_broadcast([96, SLOTS])).then_inc(e_bs, 1)

            bias_row(0, 0)
            more_rounds = pool.value_load(rounds[0:1, 0:1], min_val=0, max_val=ROUNDS - 1)

            def expert(n, par, last):
                for i in POOL_LO[1:]:
                    if not last:
                        pool.wait_ge(e_yc, n + 1)
                    lo_part(n, i)
                if not last:
                    bias_row(n + 1, 1 - par)
                    lo_part(n + 1, POOL_LO[0])

            with pool.Fori(0, more_rounds * (NE // 2) + (NE // 2 - 1)) as i:
                expert(i * 2, 0, False)
                expert(i * 2 + 1, 1, False)
            expert(more_rounds * NE + (NE - 2), 0, False)
            expert(more_rounds * NE + (NE - 1), 1, True)


_INS = ["x", "mem", "norm_mix", "norm_mem", "w_in", "cmp_pos", "cmp_w1", "cmp_w2", "w_pool", "pool_scale", "w_mem_kv",
        "w_up_nsa", "w_up_pool", "w_up_mem", "w_out", "norm_ffn", "w_router", "b_router", "w_gate_up", "b_gate_up",
        "w_down", "b_down", "norm_final"]


def kernel(**inputs):
    import concourse.bacc as bacc
    from concourse.bass_utils import run_bass_kernel_spmd

    nc = bacc.Bacc("TRN2", target_bir_lowering=False, num_devices=1)
    arrays = {f"in_{n}": np.ascontiguousarray(inputs[n]) for n in _INS}
    arrays["in_consts"] = constants()
    ins = {n[3:]: nc.dram_tensor(n, a.shape, mybir.dt.from_np(a.dtype), kind="ExternalInput").ap()
           for n, a in arrays.items()}
    out = nc.dram_tensor("out", (1, T, D), F32, kind="ExternalOutput").ap()
    build(nc, ins, out)
    r = run_bass_kernel_spmd(nc, [arrays], core_ids=[0])
    return r.results[0]["out"]
```

```python
from contextlib import ExitStack

import numpy as np

import concourse.bass as bass
from concourse import mybir

F32 = mybir.dt.float32
F32R = mybir.dt.float32r
BF16 = mybir.dt.bfloat16
I32 = mybir.dt.int32
U32 = mybir.dt.uint32
ALU = mybir.AluOpType
ACT = mybir.ActivationFunctionType
AX = mybir.AxisListType.X

P = 128
D = 1024
T = 256
KD = D // P
NT = T // P
HD = 64
HEADS = 8
GROUPS = 2
MEM_HEADS = 4
SCALE = HD ** -0.5
CMP_BLOCK, CMP_STRIDE = 32, 16
HALF = CMP_BLOCK // 2
NC = (T - CMP_BLOCK) // CMP_STRIDE + 1
CP = 32
POOL_WINDOWS = (2, 4, 8, 16)
PAD = 16
EPS = 1e-5
NEG = -1e30
TINY = 1e-30
LIMIT, ALPHA = 7.0, 1.702
NE = 32
FF = 1024
TOPK = 4
SLOTS = 64
ROUNDS = T // SLOTS
NCOL = ROUNDS * NE

Q0, KV0, NG0, PO0, MG0 = 0, 512, 1280, 1304, 1816
NGATE = 3 * HEADS

CONSTS = {}


def _lay_out():
    at = 0
    for name, n in (("ident", P), ("cos", T), ("sin", T), ("pinv", 2 * T), ("slot", P),
                    ("iota", NE), ("seen", NT * NC), ("b_ident", P), ("b_causal", P), ("b_before", P),
                    ("b_ones", P), ("b_cmp", NT * NC), ("b_expert", NE)):
        CONSTS[name] = (at, at + n)
        at += n
    return at


NCONST = _lay_out()
NF = CONSTS["b_ident"][0]


def constants():
    c = np.zeros((P, NCONST), np.float32)

    def put(name, a):
        lo, hi = CONSTS[name]
        c[:, lo:hi] = np.asarray(a, np.float32).reshape(P, hi - lo)

    p = np.arange(P)
    half = HD // 2
    inv = np.float32(10000.0) ** (-np.arange(half, dtype=np.float32) / np.float32(half))
    ang = (np.arange(T, dtype=np.float32)[None, :] * inv.astype(np.float32)[p % half][:, None]).astype(np.float32)
    put("ident", np.eye(P))
    put("b_ident", np.eye(P))
    put("cos", np.cos(ang.astype(np.float64)))
    put("sin", np.sin(ang.astype(np.float64)))
    pinv = np.zeros((P, 2, T))
    for j in range(2):
        for g in range(2):
            pinv[64 * g:64 * g + 64, j] = 1.0 / np.minimum(np.arange(T) + 1, POOL_WINDOWS[2 * j + g])
    put("pinv", pinv)
    put("slot", np.tile(np.arange(P) % SLOTS, (P, 1)))
    put("iota", np.tile(np.arange(NE), (P, 1)))
    tok = np.arange(NT)[None, :, None] * P + p[:, None, None]
    seen = (np.arange(NC) * CMP_STRIDE + CMP_BLOCK - 1)[None, None, :] <= tok
    put("seen", seen)
    put("b_cmp", np.where(seen, 0.0, NEG))
    put("b_causal", np.where(p[None, :] <= p[:, None], 0.0, NEG))
    put("b_before", p[:, None] < p[None, :])
    put("b_ones", np.ones((P, P)))
    put("b_expert", (p[:, None] % NE == np.arange(NE)[None, :]) & (p[:, None] < 3 * NE))
    return c


UNITS = [("nsa", h, v) for h in range(HEADS) for v in range(2)] + [("mem", h, 0) for h in range(MEM_HEADS)]
NU = len(UNITS)
NMG = 24


def fillers(u):
    return range(NMG * u // NU, NMG * (u + 1) // NU)


CHUNKS = [(w, kh) for w in ("q", "kv1", "kv2", "pq", "memkv") for kh in range(2)]
CHUNKS += [(f"mg{j}", kh) for j in range(6) for kh in range(2)]
CHUNKS += [("upn", 0), ("uppm", 0), ("upn", 1), ("uppm", 1)]
CHUNKS += [("out", i) for i in range(4)]
RAW = 6
EXPERT_CHUNKS = 12
DOWN = 8
SPLIT = 4
POOL_LO = (2, 5, 8, 10)


def lo_step(i):
    mine = [c for c in range(EXPERT_CHUNKS) if (c in POOL_LO) == (i in POOL_LO)]
    return i in POOL_LO, mine.index(i), len(mine)


RING = (0, 1, RAW, RAW + 1, 2, 3, 4, 5)
assert len(CHUNKS) % RAW == 0 and 2 * EXPERT_CHUNKS % len(RING) == 0 and EXPERT_CHUNKS % SPLIT == 0


def job_order():
    jobs, turn = [], [0]

    def work(*names):
        for n in names:
            jobs.append((n, 2 + turn[0] % 6))
            turn[0] += 1

    work("vec", "xT0", "xT1", "xT2", "xT3", "qA", "qB", "kcv", "ksw", "vsw", "mT0", "mT1", "mT2", "mT3",
         "ng", "pool", "qm", "hid", "km", "kcvc", "vm", "zp",
         "cs00", "cs01", "cs10", "cs11", "S0", "S1", "ct")
    for u in range(NU):
        if u + 2 < NU:
            work(f"S{u + 2}")
        work(f"T{u}")
        work(*[f"mg{j}" for j in fillers(u)])
        if u >= 1 and first_of_pair(u - 1):
            pair = pair_of(u - 1)
            jobs.append((f"o{pair}", pair % 2))
    work(*[f"up{b}{q}" for q in range(4) for b in range(3)])
    jobs.extend((f"acc{b}", b) for b in range(4))
    turn[0] = 0
    for n in ("hT00", "hT01", "hT10", "hT11", "lg0", "lg1", "cs", "cnt", "cbT"):
        jobs.append((n, 4 + turn[0] % 4))
        turn[0] += 1
    return jobs


def pair_of(u):
    kind, h, _ = UNITS[u]
    return h // 2 + (4 if kind == "mem" else 0)


def first_of_pair(u):
    return UNITS[u][1] % 2 == 0 and UNITS[u][2] == 0


def last_of_pair(u):
    return UNITS[u][1] % 2 == 1 and UNITS[u][2] == (UNITS[u][0] == "nsa")


def spans(kind):
    return [(0, T), (T, 2 * T)] if kind == "mem" else [(0, P), (P, P + T)]


def transposed(kind):
    if kind == "mem":
        return [(t * T + k * P, k * T + t * P) for k in range(2) for t in range(NT)]
    return [(0, 0), (P, P), (2 * P, 2 * P)]


LAST_USE = {"q": "qB", "kv1": "vsw", "kv2": "ng", "pq": "qm", "memkv": "vm"}


def last_use(w, i):
    if w.startswith("mg"):
        return f"mg{4 * int(w[2:]) + 3}"
    if w in ("upn", "uppm"):
        return f"up{0 if w == 'upn' else 2}{2 * i + 1}"
    if w == "out":
        return f"acc{2 + i // 2}"
    return LAST_USE[w]


def job_table():
    used, table = [0] * 8, {}
    for name, bank in job_order():
        assert name not in table
        table[name] = (bank, used[bank])
        used[bank] += 1
    return table


JOBS = job_table()


def build(nc, ins, out):
    with ExitStack() as ctx:
        sb = lambda name, shape, dt=F32: ctx.enter_context(nc.sbuf_tensor(name, shape, dt))
        sem = lambda name: ctx.enter_context(nc.semaphore(name))

        raw = sb("raw", [P, RAW, 4, 512])
        cst = sb("cst", [P, NF])
        cb = sb("cb", [P, NCONST - NF], BF16)
        hpart = sb("hpart", [P, 3, NT, D], BF16)
        cbT = sb("cbT", [NE, T])
        bdn = sb("bdn", [NE, D])
        bparts = sb("bparts", [96, 2 * FF], BF16)
        pos = sb("pos", [P, NT, NCOL])
        wgt = sb("wgt", [P, NT, NCOL])
        rounds = sb("rounds", [1, 1], I32)
        comb = sb("comb", [P, NT, NE])
        rtm = sb("rtm", [P, NT, NE])
        cntb = sb("cntb", [1, 8])
        stat = sb("stat", [P, 24])

        def const(name):
            lo, hi = CONSTS[name]
            return cb[:, lo - NF:hi - NF] if lo >= NF else cst[:, lo:hi]

        with ExitStack() as early:
            se = lambda name, shape, dt=F32: early.enter_context(nc.sbuf_tensor(name, shape, dt))
            sigw = se("sigw", [P, 24 * T])
            cstage = se("cstage", [P, NCONST - NF])
            prow = se("prow", [HALF, 2, P])
            vcol = se("vcol", [P, 96])
            w2 = se("w2", [HD, 2, HD])
            kswap = se("kswap", [P, 2, T])
            wpbd = se("wpbd", [P, 2, P])
            qraw = se("qraw", [P, 4, T])
            qrot = se("qrot", [P, 4, T])
            kcv = se("kcv", [P, 2, T])
            kraw = se("kraw", [P, 2, T])
            krot = se("krot", [P, 2, T])
            vnat = se("vnat", [P, NT, 2, P])
            gates = se("gates", [P, NT, NGATE])
            qm = se("qm", [P, 2, T])
            km = se("km", [P, 2, T])
            vm = se("vm", [P, NT, T])
            pb = [se(f"pb{i}", [P, 2, PAD + T]) for i in range(3)]
            zt = se("zt", [P, 2, T])
            hide = se("hide", [HD, 2, GROUPS * NC])
            hid = se("hid", [HD, 2, GROUPS * NC])
            hrep = se("hrep", [HD, GROUPS, 4, CP])
            kc = se("kc", [P, 16])
            vc = se("vc", [P, P])
            pc = se("pc", [P, NT, HEADS, CP])
            pcT = se("pcT", [P, GROUPS, T])
            sm = se("sm", [P, 4, 16])
            pbuf = se("pbuf", [P, 3, 512])
            ptb = se("ptb", [P, 2, 512])
            us = se("us", [P, 3, 8])
            onsa = se("onsa", [P, 4, T])
            opool = se("opool", [P, 2, T])
            omem = kcv
            x_sb = se("x_sb", [P, NT, D])
            bufA = se("bufA", [P, 2 * D])
            bufB = se("bufB", [P, 2 * D])
            vrow = se("vrow", [18, P])
            wrt = se("wrt", [P, KD, NE])
            brt = se("brt", [1, NE])
            lgt = se("lgt", [P, NT, NE])
            top = se("top", [P, NT, 8])
            topi = se("topi", [P, NT, 8], U32)
            topf = se("topf", [P, NT, 8])
            ex4 = se("ex4", [P, NT, 8])
            selb = se("selb", [P, NT, NE], BF16)
            rt4 = se("rt4", [P, NT, TOPK, NE])
            ones1 = se("ones1", [1, P])
            bufM = se("bufM", [P, 2 * D])
            mem_sb = se("mem_sb", [P, NT, D])
        xn = bufA[:, :].rearrange("p (t d) -> p t d", t=NT)
        merged = bufA[:, :].rearrange("p (k t) -> p k t", k=KD)
        h2T = merged
        xT = bufB[:, :].rearrange("p (k t) -> p k t", k=KD)
        h2 = bufB[:, :].rearrange("p (t d) -> p t d", t=NT)
        memT = bufM[:, :].rearrange("p (k t) -> p k t", k=KD)
        sig = sigw[:, :].rearrange("p (k t) -> p k t", t=T)
        turned = sigw[:, 4096:4096 + 6 * T].rearrange("p (j n) -> p j n", j=3)
        w1 = sigw[:, 0:2 * HALF * HD].rearrange("p (i l e) -> p i l e", i=2, l=HALF)
        blk = ptb[:, :, 0:HALF * GROUPS * NC].rearrange("p i (l g n) -> p i l g n", l=HALF, g=GROUPS)
        rtmp = pbuf
        bsrc = bufM[0:96, :]
        gffn = mem_sb[:, 0, :]
        whi = sb("whi", [P, SPLIT, 4, 512], F32R)
        wlo = sb("wlo", [P, SPLIT, 4, 512], F32R)
        raw2 = sb("raw2", [P, len(RING) - RAW, 4, 512])
        xe = sb("xe", [P, 2, KD, P], F32R)
        aT = sb("aT", [P, KD, P], F32R)
        a_sb = sb("a_sb", [SLOTS, 2, 512])
        glow = sb("glow", [SLOTS, 512])
        ulow = sb("ulow", [SLOTS, 512])
        g_sb = sb("g_sb", [SLOTS, 512])
        u_sb = sb("u_sb", [SLOTS, 512])
        s_sb = sb("s_sb", [SLOTS, 512])
        y_sb = sb("y_sb", [P, D])
        scat = sb("scat", [P, 2, T])
        gw = sb("gw", [P, NT, P])
        onehot = sb("onehot", [P, NT, SLOTS], BF16)
        bsel = sb("bsel", [96, 2, P], BF16)
        gfin = sb("gfin", [P, D])

        ps = ctx.enter_context(nc.psum_tensor("ps", [P, 8, 512], F32))

        full = [sem(f"bank_full{b}") for b in range(8)]
        free = [sem(f"bank_free{b}") for b in range(8)]
        landed = [sem(f"raw_landed{i}") for i in range(len(RING))]
        s_const, s_cst2, s_mem, s_vec = (sem(n) for n in ("in_const", "in_const_bf16", "in_mem", "in_vec"))
        s_x = [sem(f"in_x{t}") for t in range(NT)]
        s_cmp, s_pw, s_rt, s_gf = (sem(n) for n in ("in_cmp", "in_pool_w", "in_router", "in_norm_final"))
        s_bias, s_bdn, s_gffn = (sem(n) for n in ("in_bias", "in_b_down", "in_norm_ffn"))
        s_zero, s_zeros, s_cb = sem("dve_zeroed"), sem("pool_zeroed"), sem("consts_cast")
        s_dve, s_pool = sem("dve_chain"), sem("pool_chain")
        s_ss, s_var, s_sd, s_xn = sem("sumsq"), sem("variance"), sem("deviation"), sem("normed")
        s_rot, s_blk, s_hexp, s_hid, s_z = (sem(n) for n in ("rotated", "blocks", "hid_exp", "hid_ready", "pooled"))
        s_cd, s_ce, s_cp = sem("cmp_diff"), sem("cmp_exp"), sem("cmp_probs")
        s_nm, s_pr = sem("unit_negmax"), sem("unit_probs")
        s_mrg, s_h2 = sem("merged_ready"), sem("h2_ready")
        s_part, s_rest = sem("part_cast"), sem("part_rest")
        s_rv, s_re, s_sel, s_rounds = sem("router_top"), sem("router_exp"), sem("selected"), sem("rounds_ready")
        s_over, s_init = sem("phase1_over"), sem("expert_memory_zeroed")
        s_fin, s_out = sem("final_rows"), sem("out_stored")
        e_hi, e_mul = sem("chunk_hi"), sem("chunk_multiplied")
        e_lo = {False: sem("chunk_lo_dve"), True: sem("chunk_lo_pool")}
        e_low, e_gur, e_gm, e_sg, e_dv = (sem(n) for n in ("low_rows_copied", "product_read", "gate_clamped", "sigmoid_done", "dve_step"))
        e_act, e_oh, e_gw, e_bs = sem("activation_ready"), sem("onehot_ready"), sem("weights_ready"), sem("bias_row_ready")
        e_ga, e_gah, e_gal = sem("gathered"), sem("tokens_hi"), sem("tokens_lo")
        e_tr, e_trh, e_trl, e_st = sem("transposed"), sem("act_hi"), sem("act_lo"), sem("scatter_weights")
        e_yc, e_sc, e_turn = sem("y_copied"), sem("scattered"), sem("turn_begun")

        def start(eng, name):
            bank, use = JOBS[name]
            if use:
                eng.wait_ge(free[bank], use)
            return ps[:, bank, :]

        def computed(eng, name):
            bank, use = JOBS[name]
            eng.wait_ge(full[bank], use + 1)
            return ps[:, bank, :]

        def taken(eng, name):
            bank, use = JOBS[name]
            eng.wait_ge(free[bank], use + 1)

        def full_of(name):
            return full[JOBS[name][0]]

        def free_of(name):
            return free[JOBS[name][0]]

        counts, chunk_at, arrived_at = [0] * RAW, {}, {}
        for c, (w, i) in enumerate(CHUNKS):
            counts[c % RAW] += 16 * {"q": 4 * GROUPS, "uppm": 2}.get(w, 1)
            chunk_at[(w, i)] = c
            arrived_at[(w, i)] = counts[c % RAW]
        landed_before = counts + [0] * (len(RING) - RAW)

        def arrived(eng, w, i):
            c = chunk_at[(w, i)]
            eng.wait_ge(landed[c % RAW], arrived_at[(w, i)])
            return raw[:, c % RAW]

        w_in = ins["w_in"][0].rearrange("(k p) n -> p k n", p=P)
        w_memkv = ins["w_mem_kv"][0].rearrange("(k p) n -> p k n", p=P)
        w_upn = ins["w_up_nsa"][0].rearrange("(k p) n -> p k n", p=P)
        w_upp = ins["w_up_pool"][0].rearrange("(k p) n -> p k n", p=P)
        w_upm = ins["w_up_mem"][0].rearrange("(k p) n -> p k n", p=P)
        w_o = ins["w_out"][0].rearrange("(k p) n -> p k n", p=P)
        w_gu = ins["w_gate_up"][0].rearrange("e (k p) n -> e p k n", p=P)
        w_dn = ins["w_down"][0].rearrange("e (k p) n -> e p k n", p=P)
        x_d = ins["x"][0].rearrange("(t p) d -> p t d", p=P)
        mem_d = ins["mem"][0].rearrange("(t p) d -> p t d", p=P)
        out_d = out[0].rearrange("(t p) d -> p t d", p=P)

        def load_chunk(eng, e, i, dst):
            down = i >= DOWN
            src = w_dn if down else w_gu
            src = src[e] if isinstance(e, int) else src[bass.ds(e, 1)].rearrange("a p k n -> (a p) k n")
            if down:
                k = 2 * (i - DOWN)
                return eng.dma_start(dst.rearrange("p (k h) n -> p k (h n)", h=2), src[:, k:k + 2, :])
            k, col = 4 * (i % 2), (0, FF, 512, FF + 512)[i // 2]
            return eng.dma_start(dst, src[:, k:k + 4, col:col + 512])

        def ring_slot(par, i):
            s = RING[(EXPERT_CHUNKS * par + i) % len(RING)]
            return s, raw[:, s] if s < RAW else raw2[:, s - RAW]

        def chunk_landed(eng, n, par, i):
            j = EXPERT_CHUNKS * par + i
            s = RING[j % len(RING)]
            per_expert = 16 * EXPERT_CHUNKS // len(RING)
            eng.wait_ge(landed[s], n * per_expert + (landed_before[s] + 16 * (j // len(RING) + 1) - par * per_expert))

        def split(eng, n, i):
            by_pool, at, per_expert = lo_step(i)
            eng.wait_ge(e_lo[by_pool], n * per_expert + (at + 1))

        def y_out(t):
            return raw[:, t, 0:2, :].rearrange("p a b -> p (a b)")

        block = ctx.enter_context(nc.Block())

        @block.sync
        def _(sp):
            sources = {"kv1": (KV0, 512), "kv2": (KV0 + 512, NG0 + NGATE - KV0 - 512), "pq": (PO0, 512)}
            sources.update({f"mg{j}": (MG0 + 512 * j, 512) for j in range(6)})
            for t in range(NT):
                sp.dma_start(x_sb[:, t, :], x_d[:, t, :]).then_inc(s_x[t], 16)
            sp.dma_start(cst[:, :], ins["consts"][:, 0:NF]).then_inc(s_const, 16)
            for c, (w, i) in enumerate(CHUNKS):
                s = c % RAW
                if (w, i) == ("kv1", 0):
                    sp.dma_start(mem_sb[:, :, :], mem_d).then_inc(s_mem, 16)
                if c >= RAW:
                    computed(sp, last_use(*CHUNKS[c - RAW]))
                if w in sources:
                    c0, n = sources[w]
                    sp.dma_start(raw[:, s, :, 0:n], w_in[:, 4 * i:4 * i + 4, c0:c0 + n]).then_inc(landed[s], 16)
                elif w == "q":
                    for k in range(4):
                        for g in range(GROUPS):
                            dst = raw[:, s, k].rearrange("p (h g d) -> p h g d", h=4, g=GROUPS)[:, :, g]
                            c0 = Q0 + 4 * HD * g
                            src = w_in[:, 4 * i + k, c0:c0 + 4 * HD].rearrange("p (h d) -> p h d", h=4)
                            sp.dma_start(dst, src).then_inc(landed[s], 16)
                elif w == "memkv":
                    sp.dma_start(raw[:, s], w_memkv[:, 4 * i:4 * i + 4, :]).then_inc(landed[s], 16)
                elif w == "upn":
                    sp.dma_start(raw[:, s], w_upn[:, :, 512 * i:512 * i + 512]).then_inc(landed[s], 16)
                elif w == "uppm":
                    sp.dma_start(raw[:, s, 0:2], w_upp[:, :, 512 * i:512 * i + 512]).then_inc(landed[s], 16)
                    sp.dma_start(raw[:, s, 2:4], w_upm[:, :, 512 * i:512 * i + 512]).then_inc(landed[s], 16)
                else:
                    k, col = 4 * (i % 2), 512 * (i // 2)
                    sp.dma_start(raw[:, s], w_o[:, k:k + 4, col:col + 512]).then_inc(landed[s], 16)
            def load(n, par, i):
                s, dst = ring_slot(par, i)
                load_chunk(sp, n if isinstance(n, int) else n % NE, i, dst).then_inc(landed[s], 16)

            def load_expert(n, par):
                for i in range(EXPERT_CHUNKS):
                    if i < len(RING):
                        by_pool, at, per_expert = lo_step(i - len(RING) + EXPERT_CHUNKS)
                        sp.wait_ge(e_lo[by_pool], n * per_expert + (at + 1 - per_expert))
                    else:
                        split(sp, n, i - len(RING))
                    load(n, par, i)

            for i in range(EXPERT_CHUNKS):
                s, _ = ring_slot(0, i)
                if i >= len(RING):
                    split(sp, 0, i - len(RING))
                elif s < RAW:
                    computed(sp, last_use(*CHUNKS[len(CHUNKS) - RAW + s]))
                else:
                    sp.wait_ge(s_mrg, 4)
                load(0, 0, i)
            sp.wait_ge(s_rounds, 1)
            more_rounds = sp.value_load(rounds[0:1, 0:1], min_val=0, max_val=ROUNDS - 1)
            with sp.Fori(0, more_rounds * (NE // 2) + (NE // 2 - 1)) as i:
                load_expert(i * 2 + 1, 1)
                load_expert(i * 2 + 2, 0)
            load_expert(more_rounds * NE + (NE - 1), 1)
            for t in range(NT):
                sp.wait_ge(s_fin, t + 1)
                sp.dma_start(out_d[:, t, :], y_out(t)).then_inc(s_out, 16)
            sp.wait_ge(s_out, 16 * NT)

        @block.tensor
        def _(pe):
            ident = const("ident")
            b_ident = const("b_ident")
            def project(name, parts):
                o = start(pe, name)
                for j, (w, lhs) in enumerate(parts):
                    for k in range(KD):
                        m = pe.matmul(o[:, j * T:(j + 1) * T], lhs(arrived(pe, w, k // 4), k % 4), xT[:, k, :],
                                      start=(k == 0), stop=(k == KD - 1), skip_group_check=True)
                m.then_inc(full_of(name), 1)

            pe.wait_ge(s_const, 16)
            pe.wait_ge(s_vec, 16 * 4)
            o = start(pe, "vec")
            pe.transpose(o[:, 0:18], vrow[:, :], ident[0:18, 0:18])
            for i in range(2):
                m = pe.transpose(o[:, 32 + HALF * i:32 + HALF * (i + 1)], prow[:, i], ident[0:HALF, 0:HALF])
            m.then_inc(full_of("vec"), 1)

            def transposes(prefix, src, ready, before):
                for t in range(NT):
                    pe.wait_ge(ready, before + t + 1)
                    for j in range(4):
                        o = start(pe, f"{prefix}{j}") if t == 0 else ps[:, JOBS[f"{prefix}{j}"][0], :]
                        for kk in range(2):
                            k = 2 * j + kk
                            m = pe.transpose(o[:, kk * T + t * P:kk * T + t * P + P], src[:, t, k * P:(k + 1) * P], ident)
                        if t == NT - 1:
                            m.then_inc(full_of(f"{prefix}{j}"), 1)

            transposes("xT", xn, s_xn, 0)
            cols = lambda c: (lambda w, k: w[:, k, c:c + P])
            jobs = {"qA": start(pe, "qA"), "qB": start(pe, "qB")}
            for j in range(2):
                for kh in range(2):
                    w = arrived(pe, "q", kh)
                    for n, (name, o) in enumerate(jobs.items()):
                        for k in range(4 * kh, 4 * kh + 4):
                            if j == n == 0 and k % 2 == 0:
                                taken(pe, f"xT{k // 2}")
                            m = pe.matmul(o[:, j * T:(j + 1) * T], cols((2 * n + j) * P)(w, k % 4), xT[:, k, :],
                                          start=(k == 0), stop=(k == KD - 1), skip_group_check=True)
                        if j and kh:
                            m.then_inc(full_of(name), 1)
            project("kcv", [("kv1", cols(0)), ("kv1", cols(P))])
            project("ksw", [("kv1", cols(2 * P)), ("kv2", cols(0))])
            o = start(pe, "vsw")
            for t in range(NT):
                for v, (w, c) in enumerate((("kv1", 3 * P), ("kv2", P))):
                    for k in range(KD):
                        m = pe.matmul(o[:, (2 * t + v) * P:(2 * t + v + 1) * P], xT[:, k, t * P:(t + 1) * P],
                                      arrived(pe, w, k // 4)[:, k % 4, c:c + P],
                                      start=(k == 0), stop=(k == KD - 1), skip_group_check=True)
            m.then_inc(full_of("vsw"), 1)
            transposes("mT", mem_sb, s_xn, NT)
            o = start(pe, "ng")
            for t in range(NT):
                for k in range(KD):
                    m = pe.matmul(o[:, t * NGATE:(t + 1) * NGATE], xT[:, k, t * P:(t + 1) * P],
                                  arrived(pe, "kv2", k // 4)[:, k % 4, 2 * P:2 * P + NGATE],
                                  start=(k == 0), stop=(k == KD - 1), skip_group_check=True)
            m.then_inc(full_of("ng"), 1)
            project("pool", [("pq", cols(0)), ("pq", cols(P))])
            project("qm", [("pq", cols(2 * P)), ("pq", cols(3 * P))])
            o = start(pe, "hid")
            pe.wait_ge(s_cmp, 16 * 5)
            for i in range(2):
                pe.wait_ge(s_blk, 2 * i + 2)
                for l in range(HALF):
                    m = pe.matmul(o[0:HD, GROUPS * NC * i:GROUPS * NC * (i + 1)], w1[:, i, l, :],
                                  blk[:, i, l].rearrange("p g n -> p (g n)"),
                                  start=(l == 0), stop=(l == HALF - 1), skip_group_check=True)
            m.then_inc(full_of("hid"), 1)
            for j in range(4):
                taken(pe, f"mT{j}")
            o = start(pe, "km")
            for j in range(2):
                for k in range(KD):
                    m = pe.matmul(o[:, j * T:(j + 1) * T], arrived(pe, "memkv", k // 4)[:, k % 4, j * P:(j + 1) * P],
                                  memT[:, k, :], start=(k == 0), stop=(k == KD - 1), skip_group_check=True)
            m.then_inc(full_of("km"), 1)
            pe.wait_ge(s_hid, 1)
            o = start(pe, "kcvc")
            for g in range(GROUPS):
                pe.matmul(o[HD * g:HD * (g + 1), 0:NC], w2[:, 0, :], hid[:, 0, NC * g:NC * (g + 1)],
                          start=True, stop=True, skip_group_check=True)
            for g in range(GROUPS):
                m = pe.matmul(o[:, P + HD * g:P + HD * (g + 1)], hrep[:, g].rearrange("p a n -> p (a n)"), w2[:, 1, :],
                              start=True, stop=True, skip_group_check=True)
            m.then_inc(full_of("kcvc"), 1)
            o = start(pe, "vm")
            for t in range(NT):
                for k in range(KD):
                    m = pe.matmul(o[:, t * T:(t + 1) * T], memT[:, k, t * P:(t + 1) * P],
                                  arrived(pe, "memkv", k // 4)[:, k % 4, T:2 * T],
                                  start=(k == 0), stop=(k == KD - 1), skip_group_check=True)
            m.then_inc(full_of("vm"), 1)
            pe.wait_ge(s_z, 1)
            pe.wait_ge(s_pw, 16 * 4)
            pe.wait_ge(s_zeros, 1)
            o = start(pe, "zp")
            for j in range(2):
                m = pe.matmul(o[:, j * T:(j + 1) * T], wpbd[:, j, :], zt[:, j, :], start=True, stop=True,
                              skip_group_check=True)
            m.then_inc(full_of("zp"), 1)

            taken(pe, "kcvc")
            pe.wait_ge(s_cb, 1)
            for t in range(NT):
                for g in range(GROUPS):
                    name = f"cs{t}{g}"
                    o = start(pe, name)
                    rows = slice(64 * g, 64 * g + 64)
                    for h in range(4):
                        pe.matmul(o[:, 16 * h:16 * h + NC], qraw[rows, h, t * P:(t + 1) * P], kc[rows, 0:NC],
                                  start=True, stop=False, skip_group_check=True)
                        m = pe.matmul(o[:, 16 * h:16 * h + NC], b_ident, const("b_cmp")[:, t * NC:(t + 1) * NC],
                                      start=False, stop=True, skip_group_check=True)
                    m.then_inc(full_of(name), 1)

            def scores(u):
                kind, h, v = UNITS[u]
                o = start(pe, f"S{u}")
                if kind == "mem":
                    if h == 0:
                        taken(pe, "km")
                        taken(pe, "qm")
                    rows = slice(64 * (h % 2), 64 * (h % 2) + 64)
                    for t in range(NT):
                        m = pe.matmul(o[:, t * T:(t + 1) * T], qm[rows, h // 2, t * P:(t + 1) * P], km[rows, h // 2, :],
                                      start=True, stop=True, skip_group_check=True)
                else:
                    if u == 0:
                        pe.wait_ge(s_rot, 3)
                    g = h // 4
                    rows = slice(64 * g, 64 * g + 64)
                    for t in range(NT):
                        at, n = t * P, (t + 1) * P
                        pe.matmul(o[:, at:at + n], qrot[rows, h % 4, t * P:(t + 1) * P], krot[rows, v, 0:n],
                                  start=True, stop=False, skip_group_check=True)
                        m = pe.matmul(o[:, at + t * P:at + n], b_ident, const("b_causal"),
                                      start=False, stop=True, skip_group_check=True)
                m.then_inc(full_of(f"S{u}"), 1)

            def turn(u):
                pe.wait_ge(s_pr, u + 1)
                kind = UNITS[u][0]
                o = start(pe, f"T{u}")
                for src, dst in transposed(kind):
                    m = pe.transpose(o[:, dst:dst + P], pbuf[:, u % 3, src:src + P], ident)
                m.then_inc(full_of(f"T{u}"), 1)

            def values(u):
                kind, h, v = UNITS[u]
                name = f"o{pair_of(u)}"
                rows = slice(64 * (h % 2), 64 * (h % 2) + 64)
                if h % 2 == 0 and v == 0:
                    start(pe, name)
                o = ps[:, JOBS[name][0], :]
                if kind == "nsa" and v == 0:
                    if u == 0:
                        taken(pe, "ct")
                    q = slice(CP * (h % 4), CP * (h % 4) + CP)
                    pe.matmul(o[rows, 0:T], vc[q, 64 * (h // 4):64 * (h // 4) + 64], pcT[q, h // 4, :],
                              start=True, stop=False, skip_group_check=True)
                taken(pe, f"T{u}")
                pt = ptb[:, u % 2, :]
                if kind == "nsa":
                    if u == 0:
                        taken(pe, "vsw")
                    g = h // 4
                    pe.matmul(o[rows, 0:T], vnat[:, 0, v, 64 * g:64 * g + 64], pt[:, 0:T],
                              start=False, stop=False, skip_group_check=True)
                    m = pe.matmul(o[rows, P:T], vnat[:, 1, v, 64 * g:64 * g + 64], pt[:, T:T + P],
                                  start=False, stop=(v == 1), skip_group_check=True)
                    last = h % 2 == 1 and v == 1
                else:
                    if h == 0:
                        taken(pe, "vm")
                    for k in range(2):
                        m = pe.matmul(o[rows, 0:T], vm[:, k, 64 * h:64 * h + 64], pt[:, k * T:(k + 1) * T],
                                      start=(k == 0), stop=(k == 1), skip_group_check=True)
                    last = h % 2 == 1
                if last:
                    m.then_inc(full_of(name), 1)

            scores(0)
            scores(1)
            pe.wait_ge(s_cp, 1)
            o = start(pe, "ct")
            for g in range(GROUPS):
                for t in range(NT):
                    m = pe.transpose(o[:, (2 * g + t) * P:(2 * g + t + 1) * P],
                                     pc[:, t, 4 * g:4 * g + 4, :].rearrange("p h n -> p (h n)"), ident)
            m.then_inc(full_of("ct"), 1)
            for u in range(NU):
                if u + 2 < NU:
                    scores(u + 2)
                turn(u)
                for j in fillers(u):
                    project(f"mg{j}", [(f"mg{j // 4}", cols((j % 4) * P))])
                if u:
                    values(u - 1)
            values(NU - 1)

            for q in range(4):
                for b, (w, k0, nk, src) in enumerate((("upn", 0, 4, onsa), ("uppm", 0, 2, opool), ("uppm", 2, 2, omem))):
                    if q == 0:
                        for job in (("o0", "o1", "o2", "o3"), ("zp",), ("o4", "o5"))[b]:
                            taken(pe, job)
                    name = f"up{b}{q}"
                    o = start(pe, name)
                    wt = arrived(pe, w, q // 2)
                    for j in range(2):
                        c = (2 * (q % 2) + j) * P
                        for k in range(nk):
                            m = pe.matmul(o[:, j * T:(j + 1) * T], wt[:, k0 + k, c:c + P], src[:, k, :],
                                          start=(k == 0), stop=(k == nk - 1), skip_group_check=True)
                    m.then_inc(full_of(name), 1)

            pe.wait_ge(s_mrg, 4)
            def turn_h2(t):
                pe.wait_ge(s_h2, t + 1)
                for j in range(2):
                    o = start(pe, f"hT{t}{j}")
                    for kk in range(4):
                        k = 4 * j + kk
                        m = pe.transpose(o[:, kk * P:(kk + 1) * P], h2[:, t, k * P:(k + 1) * P], ident)
                    m.then_inc(full_of(f"hT{t}{j}"), 1)

            for t in range(NT):
                for half in range(2):
                    if (t, half) == (1, 1):
                        turn_h2(0)
                    name = f"acc{2 * t + half}"
                    o = start(pe, name)
                    pe.matmul(o[:, :], ident, x_sb[:, t, 512 * half:512 * half + 512], start=True, stop=False,
                              skip_group_check=True)
                    for k in range(KD):
                        m = pe.matmul(o[:, :], merged[:, k, t * P:(t + 1) * P], arrived(pe, "out", 2 * half + k // 4)[:, k % 4, :],
                                      start=False, stop=(k == KD - 1), skip_group_check=True)
                    m.then_inc(full_of(name), 1)

            pe.wait_ge(s_rt, 32)
            for t in range(NT):
                if t == 1:
                    turn_h2(1)
                for j in range(2):
                    taken(pe, f"hT{t}{j}")
                o = start(pe, f"lg{t}")
                for k in range(KD):
                    pe.matmul(o[:, 0:NE], h2T[:, k, t * P:(t + 1) * P], wrt[:, k, :],
                              start=(k == 0), stop=False, skip_group_check=True)
                m = pe.matmul(o[:, 0:NE], ones1[0:1, :], brt[0:1, :], start=False, stop=True, skip_group_check=True)
                m.then_inc(full_of(f"lg{t}"), 1)
            pe.wait_ge(s_sel, 1)
            o = start(pe, "cs")
            pe.matmul(o[:, 0:NE], const("b_before"), selb[:, 0, :], start=True, stop=True, skip_group_check=True)
            pe.matmul(o[:, NE:2 * NE], const("b_ones"), selb[:, 0, :], start=True, stop=False, skip_group_check=True)
            m = pe.matmul(o[:, NE:2 * NE], const("b_before"), selb[:, 1, :], start=False, stop=True, skip_group_check=True)
            m.then_inc(full_of("cs"), 1)
            o = start(pe, "cnt")
            for t in range(NT):
                m = pe.matmul(o[:, 0:NE], const("b_ones"), selb[:, t, :], start=(t == 0), stop=(t == 1),
                              skip_group_check=True)
            m.then_inc(full_of("cnt"), 1)
            o = start(pe, "cbT")
            for t in range(NT):
                m = pe.matmul(o[0:NE, t * P:(t + 1) * P], comb[:, t, :], ident, start=True, stop=True,
                              skip_group_check=True)
            m.then_inc(full_of("cbT"), 1)
            pe.sem_inc(s_over, 1)

            def gather(n, xbank):
                pe.wait_ge(e_oh, n + 1)
                o = ps[:, xbank, :]
                for k in range(KD):
                    for part in range(3):
                        for t in range(NT):
                            m = pe.matmul(o[:, SLOTS * k:SLOTS * (k + 1)], hpart[:, part, t, k * P:(k + 1) * P],
                                          onehot[:, t, :], start=(part == 0 and t == 0), stop=(part == 2 and t == 1),
                                          skip_group_check=True)
                m.then_inc(e_ga, 1)

            def turn_act(n, b, bank, weights):
                pe.wait_ge(e_act, 2 * n + (b + 1))
                pe.wait_ge(e_gur, 4 * n + (2 if b == 0 else 4))
                pe.sem_inc(e_turn, 1)
                for j in range(4):
                    m = pe.transpose(ps[:, bank, SLOTS * j:SLOTS * (j + 1)], a_sb[:, b, j * P:(j + 1) * P],
                                     ident[0:SLOTS, 0:SLOTS])
                if weights:
                    pe.wait_ge(e_gw, n + 1)
                    for t in range(NT):
                        m = pe.transpose(ps[:, bank, T + t * P:T + (t + 1) * P], gw[:, t, :], ident)
                m.then_inc(e_tr, 1)

            def scatter(n, parity, t):
                pe.wait_ge(e_yc, n + 1)
                for b in (2 * t, 2 * t + 1):
                    m = pe.matmul(ps[:, b, :], scat[:, parity, t * P:(t + 1) * P],
                                  y_sb[:, 512 * (b % 2):512 * (b % 2) + 512], start=False, stop=True, skip_group_check=True)
                m.then_inc(e_sc, 1)

            def expert(n, par, last):
                X, Y = ((4, 5), (6, 7)) if par == 0 else ((6, 7), (4, 5))
                banks = (X[0], X[1], Y[0], Y[1])

                def passes(i):
                    split(pe, n, i)
                    for w in (whi, wlo):
                        for b in range(4):
                            if i < DOWN:
                                k, bank, first = 4 * (i % 2) + b, banks[i // 2], False
                                stationary = xe[:, par, k, :]
                            else:
                                k, bank = 2 * (i - DOWN) + b // 2, X[b % 2]
                                first = k == 0 and w is whi
                                stationary = aT[:, k, :]
                            m = pe.matmul(ps[:, bank, :], stationary, w[:, i % SPLIT, b, :],
                                          start=first, stop=True, skip_group_check=True)
                    m.then_inc(e_mul, 1)

                for q in range(4):
                    if q == 0:
                        pe.wait_ge(e_trl, 2 * n + 1)
                        pe.wait_ge(e_bs, n + 1)
                        pe.wait_ge(e_gah, n + 1)
                        pe.wait_ge(e_gal, n + 1)
                    if q == 1:
                        pe.wait_ge(e_gur, 4 * n + 1)
                    if q == 2:
                        pe.wait_ge(e_yc, n + 1)
                    col = (0, FF, 512, FF + 512)[q]
                    pe.matmul(ps[:, banks[q], :], bsel[:, par, :], bparts[:, col:col + 512], start=True, stop=False,
                              skip_group_check=True)
                    for i in (2 * q, 2 * q + 1):
                        passes(i)
                    if q == 2:
                        turn_act(n, 0, X[0], True)
                        if not last:
                            pe.wait_ge(e_gur, 4 * n + 3)
                            gather(n + 1, X[1])
                scatter(n, 1 - par, 0)
                pe.wait_ge(e_trl, 2 * n + 2)
                pe.wait_ge(e_st, n + 2)
                if last:
                    pe.wait_ge(e_gur, 4 * n + 3)
                else:
                    pe.wait_ge(e_gah, n + 2)
                    pe.wait_ge(e_gal, n + 2)
                passes(8)
                passes(9)
                if last:
                    scatter(n, 1 - par, 1)
                turn_act(n, 1, Y[0], False)
                if not last:
                    scatter(n, 1 - par, 1)
                pe.wait_ge(e_trl, 2 * n + 3)
                passes(10)
                passes(11)

            pe.wait_ge(s_over, 4)
            gather(0, 5)
            pe.wait_ge(s_init, 3)
            pe.wait_ge(s_rounds, 1)
            more_rounds = pe.value_load(rounds[0:1, 0:1], min_val=0, max_val=ROUNDS - 1)
            with pe.Fori(0, more_rounds * (NE // 2) + (NE // 2 - 1)) as i:
                expert(i * 2, 0, False)
                expert(i * 2 + 1, 1, False)
            taken(pe, "cbT")
            pe.wait_ge(s_bdn, 16)
            for b in range(4):
                pe.matmul(ps[:, b, :], cbT[:, (b // 2) * P:(b // 2 + 1) * P], bdn[:, 512 * (b % 2):512 * (b % 2) + 512],
                          start=False, stop=True, skip_group_check=True)
            expert(more_rounds * NE + (NE - 2), 0, False)
            expert(more_rounds * NE + (NE - 1), 1, True)
            for t in range(NT):
                scatter(more_rounds * NE + NE, 1, t)

        @block.scalar
        def _(act):
            act.dma_start(vrow[0:8, :], ins["norm_mix"][0].rearrange("(k p) -> k p", p=P)).then_inc(s_vec, 16)
            act.dma_start(vrow[8:16, :], ins["norm_mem"][0].rearrange("(k p) -> k p", p=P)).then_inc(s_vec, 16)
            act.dma_start(vrow[16:18, :], ins["pool_scale"][0].rearrange("(k p) -> k p", p=P)).then_inc(s_vec, 16)
            act.dma_start(prow[:, :, :], ins["cmp_pos"][0].rearrange("i (l a) d -> l i (a d)", a=2)).then_inc(s_vec, 16)

            def sumsq(src, junk, t, count):
                act.activation(junk, src, ACT.Square, accum_out=stat[:, t:t + 1]).then_inc(s_ss, 1)
                act.wait_ge(s_ss, count)

            def deviation(count, lo, cols=(0, NT)):
                act.wait_ge(s_var, count)
                a = stat[:, lo + 2 + cols[0]:lo + 2 + cols[1]]
                act.activation(a, a, ACT.Sqrt).then_inc(s_sd, 1)

            def take(name, dst, o=None, **kw):
                o = computed(act, name) if o is None else o
                act.activation(dst, o, kw.pop("func", ACT.Copy), **kw).then_inc(free_of(name), 1)

            act.wait_ge(s_zero, 1)
            act.activation(stat[:, 17:18], stat[:, 16:17], ACT.Sqrt)
            for t in range(NT):
                act.wait_ge(s_x[t], 16)
                sumsq(x_sb[:, t, :], xn[:, t, :], t, t + 1)
                deviation(1 + t, 0, (t, t + 1))
            o = computed(act, "vec")
            act.activation(vcol[:, 0:18], o[:, 0:18], ACT.Copy)
            take("vec", vcol[:, 32:32 + CMP_BLOCK], o[:, 32:32 + CMP_BLOCK])
            taken(act, "vec")
            for j in (1, 3):
                o = computed(act, f"xT{j}")
                for k in (2 * j, 2 * j + 1):
                    m = act.activation(xT[:, k, :], o[:, (k % 2) * T:(k % 2 + 1) * T], ACT.Copy, scale=vcol[:, k:k + 1])
                m.then_inc(free_of(f"xT{j}"), 1)
            act.wait_ge(s_mem, 16)
            for t in range(NT):
                sumsq(mem_sb[:, t, :], bufM[:, t * D:(t + 1) * D], 4 + t, t + 3)
            deviation(3, 4)
            def take_and_turn(name, dst, j):
                o = computed(act, name)
                act.activation(dst.rearrange("p a t -> p (a t)"), o, ACT.Copy)
                for lo in range(0, P, HD // 2):
                    first = lo % HD == 0
                    other = lo + HD // 2 if first else lo - HD // 2
                    m = act.activation(turned[lo:lo + HD // 2, j], o[other:other + HD // 2, :], ACT.Copy,
                                       scale=-1.0 if first else 1.0)
                m.then_inc(free_of(name), 1)

            take_and_turn("qA", qraw[:, 0:2], 0)
            take_and_turn("qB", qraw[:, 2:4], 1)
            o = computed(act, "kcv")
            act.activation(kcv[:, :].rearrange("p a t -> p (a t)"), o, ACT.Copy)
            act.activation(kswap[HD:P].rearrange("p a t -> p (a t)"), o[0:HD], ACT.Copy)
            take("kcv", kswap[0:HD].rearrange("p a t -> p (a t)"), o[HD:P])
            take_and_turn("ksw", kraw[:, :], 2)
            take("vsw", vnat[:, :].rearrange("p t v d -> p (t v d)"))
            o = computed(act, "ng")
            take("ng", gates[:, :].rearrange("p t n -> p (t n)"), o[:, 0:NT * NGATE], func=ACT.Exp, scale=-1.0)
            o = computed(act, "pool")
            take("pool", pb[0][:, :, PAD:], o[:, :].rearrange("p (a t) -> p a t", a=2))
            take("qm", qm[:, :].rearrange("p a t -> p (a t)"))
            o = computed(act, "hid")
            act.activation(hide[:, :, :].rearrange("p i n -> p (i n)"), o[0:HD, 0:2 * GROUPS * NC], ACT.Exp,
                           scale=-1.0).then_inc(s_hexp, 1)
            take("km", km[:, :].rearrange("p a t -> p (a t)"))
            take("vm", vm[:, :].rearrange("p a t -> p (a t)"))
            o = computed(act, "zp")
            act.activation(opool[:, 0, :], o[:, 0:T], ACT.Copy, scale=vcol[:, 16:17])
            take("zp", opool[:, 1, :], o[:, T:2 * T], scale=vcol[:, 17:18])
            act.wait_ge(s_cd, 4)
            pcv = pc[:, :, :, :].rearrange("p t h n -> p (t h) n")[:, :, 0:NC]
            act.activation(pcv, pcv, ACT.Exp, scale=SCALE).then_inc(s_ce, 1)

            def unit_exp(u):
                act.wait_ge(s_nm, u + 1)
                o = ps[:, JOBS[f"S{u}"][0], :]
                for t, (a, b) in enumerate(spans(UNITS[u][0])):
                    m = act.activation(pbuf[:, u % 3, a:b], o[:, a:b], ACT.Exp, bias=us[:, u % 3, 2 + t:3 + t],
                                       scale=SCALE, accum_out=us[:, u % 3, 4 + t:5 + t])
                m.then_inc(free_of(f"S{u}"), 1)

            def take_pair(u):
                pair = pair_of(u)
                o = computed(act, f"o{pair}")
                dst = onsa[:, pair, :] if pair < 4 else omem[:, pair - 4, :]
                take(f"o{pair}", dst, o[:, 0:T])

            unit_exp(0)
            unit_exp(1)
            take("ct", pcT[:, :].rearrange("p g t -> p (g t)"))
            for u in range(NU):
                if u + 2 < NU:
                    unit_exp(u + 2)
                n = 512 if UNITS[u][0] == "mem" else 3 * P
                o = computed(act, f"T{u}")
                take(f"T{u}", ptb[:, u % 2, 0:n], o[:, 0:n])
                for j in fillers(u):
                    o = computed(act, f"mg{j}")
                    take(f"mg{j}", sig[:, j, :], o[:, 0:T], func=ACT.Exp, scale=-1.0)
                if u and last_of_pair(u - 1):
                    take_pair(u - 1)
            take_pair(NU - 1)

            def first_hi(i):
                chunk_landed(act, 0, 0, i)
                act.activation(whi[:, i], ring_slot(0, i)[1], ACT.Copy).then_inc(e_hi, 1)

            act.wait_ge(s_mrg, 4)
            for i in range(SPLIT):
                first_hi(i)

            def next_part(part, t):
                if part:
                    act.wait_ge(s_rest, NT * (part - 1) + t + 1)
                src = bufM if part else bufB
                act.activation(hpart[:, part, t, :], src[:, t * D:(t + 1) * D], ACT.Copy).then_inc(s_part, 1)

            for t in range(NT):
                computed(act, f"acc{2 * t}")
                computed(act, f"acc{2 * t + 1}")
                sumsq(ps[:, 2 * t:2 * t + 2, :].rearrange("p b n -> p (b n)"), h2[:, t, :], 8 + t, t + 5)
                deviation(4 + t, 8, (t, t + 1))
                act.wait_ge(s_h2, t + 1)
                next_part(0, t)

            def router_exp(t):
                act.wait_ge(s_rv, t + 1)
                act.activation(ex4[:, t, 0:TOPK], top[:, t, 0:TOPK], ACT.Exp, bias=ex4[:, t, 5:6],
                               accum_out=ex4[:, t, 4:5]).then_inc(s_re, 1)

            next_part(1, 0)
            router_exp(0)
            next_part(1, 1)
            next_part(2, 0)
            router_exp(1)
            next_part(2, 1)
            o = computed(act, "cbT")
            take("cbT", cbT[:, :], o[0:NE, 0:T])
            act.wait_ge(s_part, 3 * NT)
            act.sem_inc(s_over, 1)

            act.wait_ge(s_over, 4)
            for signal in (e_yc, e_st):
                act.sem_inc(signal, 1)
            act.dma_start(gfin[:, :], ins["norm_final"].partition_broadcast(P)).then_inc(s_gf, 16)

            def tokens_hi(n, par, bank):
                act.wait_ge(e_ga, n + 1)
                act.activation(xe[:, par, :, 0:SLOTS], ps[:, bank, :].rearrange("p (k s) -> p k s", s=SLOTS),
                               ACT.Copy).then_inc(e_gah, 1)

            def expert(n, par, last):
                X, Y = ((4, 5), (6, 7)) if par == 0 else ((6, 7), (4, 5))
                banks = (X[0], X[1], Y[0], Y[1])
                more = lambda i: i + SPLIT < EXPERT_CHUNKS or not last

                def ahead(i):
                    if more(i):
                        act.wait_ge(e_mul, n * EXPERT_CHUNKS + (i + 1))
                        c = i + SPLIT
                        chunk_landed(act, n, par, c)
                        act.activation(whi[:, c % SPLIT], ring_slot(par, c)[1], ACT.Copy).then_inc(e_hi, 1)

                def low_rows(q):
                    act.wait_ge(e_mul, n * EXPERT_CHUNKS + (2 * q + 2))
                    act.activation((glow, ulow)[q % 2][:, :], ps[SLOTS:P, banks[q], :], ACT.Copy).then_inc(e_low, 1)

                def sigmoid(b):
                    act.wait_ge(e_gm, n * 2 + (b + 1))
                    act.activation(s_sb[:, :], g_sb[:, :], ACT.Sigmoid, scale=ALPHA).then_inc(e_sg, 1)

                def act_hi(b, bank):
                    act.wait_ge(e_tr, n * 2 + (b + 1))
                    act.activation(aT[:, 4 * b:4 * b + 4, 0:SLOTS],
                                   ps[:, bank, 0:4 * SLOTS].rearrange("p (k s) -> p k s", s=SLOTS),
                                   ACT.Copy).then_inc(e_trh, 1)

                ahead(0)
                low_rows(0)
                ahead(1)
                ahead(2)
                sigmoid(0)
                low_rows(1)
                ahead(3)
                ahead(4)
                act.wait_ge(e_tr, n * 2 + 1)
                act.activation(scat[:, par, :], ps[:, X[0], T:2 * T], ACT.Copy).then_inc(e_st, 1)
                act_hi(0, X[0])
                low_rows(2)
                if not last:
                    tokens_hi(n + 1, 1 - par, X[1])
                ahead(5)
                ahead(6)
                sigmoid(1)
                low_rows(3)
                ahead(7)
                ahead(8)
                act_hi(1, Y[0])
                ahead(9)
                ahead(10)
                act.wait_ge(e_mul, n * EXPERT_CHUNKS + EXPERT_CHUNKS)
                act.activation(y_sb[:, :], ps[:, X[0]:X[0] + 2, :].rearrange("p b n -> p (b n)"), ACT.Copy).then_inc(e_yc, 1)
                ahead(11)

            tokens_hi(0, 0, 5)
            act.wait_ge(s_rounds, 1)
            more_rounds = act.value_load(rounds[0:1, 0:1], min_val=0, max_val=ROUNDS - 1)
            with act.Fori(0, more_rounds * (NE // 2) + (NE // 2 - 1)) as i:
                expert(i * 2, 0, False)
                expert(i * 2 + 1, 1, False)
            expert(more_rounds * NE + (NE - 2), 0, False)
            expert(more_rounds * NE + (NE - 1), 1, True)

            act.activation(stat[:, 18:19], stat[:, 16:17], ACT.Sqrt)
            for t in range(NT):
                act.wait_ge(e_sc, more_rounds * (2 * NE) + (2 * NE + 1 + t))
                sumsq(ps[:, 2 * t:2 * t + 2, :].rearrange("p b n -> p (b n)"), y_out(NT + t), 12 + t, t + 7)
                deviation(6 + t, 12, (t, t + 1))

        @block.vector
        def _(dve):
            n_link = [0]

            def link(m):
                n_link[0] += 1
                m.then_inc(s_dve, 1)
                dve.wait_ge(s_dve, n_link[0])

            def variance(lo, squares, count, cols=(0, NT)):
                sums, var = stat[:, lo + cols[0]:lo + cols[1]], stat[:, lo + 2 + cols[0]:lo + 2 + cols[1]]
                dve.wait_ge(s_ss, squares)
                dve.tensor_scalar(var, sums, 1.0 / D, EPS, ALU.mult, ALU.add).then_inc(s_var, 1)
                dve.wait_ge(s_sd, count)
                link(dve.reciprocal(sums, var))

            def sigmoid_of_exp(a):
                link(dve.tensor_scalar(a, a, 1.0, None, ALU.add))
                link(dve.reciprocal(a, a))

            dve.memset(stat[:, 16:17], 0.0).then_inc(s_zero, 1)
            dve.memset(ones1[:, :], 1.0).then_inc(s_zero, 1)
            dve.memset(pc[:, :, :, :], 0.0).then_inc(s_zero, 1)
            link(dve.memset(hrep[:, :, :, :], 0.0))
            for t in range(NT):
                variance(0, 1 + t, 1 + t, (t, t + 1))
                dve.tensor_scalar(xn[:, t, :], x_sb[:, t, :], stat[:, t:t + 1], None, ALU.mult).then_inc(s_xn, 1)
            taken(dve, "vec")

            def scaled(name, dst, col):
                o = computed(dve, name)
                dve.tensor_tensor(dst, o[:, :].rearrange("p (k t) -> p k t", t=T),
                                  vcol[:, col:col + 2].unsqueeze(2).to_broadcast([P, 2, T]), ALU.mult).then_inc(free_of(name), 1)

            for j in (0, 2):
                scaled(f"xT{j}", xT[:, 2 * j:2 * j + 2, :], 2 * j)
            variance(4, 4, 3)
            for t in range(NT):
                dve.tensor_scalar(mem_sb[:, t, :], mem_sb[:, t, :], stat[:, 4 + t:5 + t], None, ALU.mult).then_inc(s_xn, 1)
            dve.wait_ge(s_cst2, 16)
            dve.tensor_copy(cb[:, :], cstage[:, :]).then_inc(s_cb, 1)
            for j in range(4):
                scaled(f"mT{j}", memT[:, 2 * j:2 * j + 2, :], 8 + 2 * j)
            taken(dve, "ng")
            sigmoid_of_exp(gates[:, :, :].rearrange("p t n -> p (t n)"))
            dve.wait_ge(s_const, 16)
            for j, (job, src, dst) in enumerate((("qA", qraw[:, 0:2], qrot[:, 0:2]), ("qB", qraw[:, 2:4], qrot[:, 2:4]),
                                                 ("ksw", kraw[:, :], krot[:, :]))):
                taken(dve, job)
                wide = lambda c: const(c).unsqueeze(1).to_broadcast([P, 2, T])
                own, other = (rtmp[:, i, :].rearrange("p (a t) -> p a t", a=2) for i in range(2))
                dve.tensor_tensor(own, src, wide("cos"), ALU.mult)
                link(dve.tensor_tensor(other, turned[:, j, :].rearrange("p (a t) -> p a t", a=2), wide("sin"), ALU.mult))
                dve.tensor_tensor(dst, own, other, ALU.add).then_inc(s_rot, 1)
                dve.wait_ge(s_rot, j + 1)
            o = computed(dve, "hid")
            dve.wait_ge(s_hexp, 1)
            sigmoid_of_exp(hide[:, :, :])
            dve.tensor_tensor(hid[:, :, :].rearrange("p i n -> p (i n)"), o[0:HD, 0:2 * GROUPS * NC],
                              hide[:, :, :].rearrange("p i n -> p (i n)"), ALU.mult).then_inc(free_of("hid"), 1)
            taken(dve, "hid")
            for g in range(GROUPS):
                m = dve.tensor_copy(hrep[:, g, :, 0:NC], hid[:, 1:2, NC * g:NC * (g + 1)].to_broadcast([HD, 4, NC]))
            m.then_inc(s_hid, 1)
            o = computed(dve, "kcvc")
            dve.tensor_copy(kc[:, 0:NC], o[:, 0:NC])
            dve.tensor_copy(vc[:, :], o[:, P:2 * P]).then_inc(free_of("kcvc"), 1)

            for t in range(NT):
                for g in range(GROUPS):
                    name = f"cs{t}{g}"
                    o = computed(dve, name)[:, 0:64].rearrange("p (h n) -> p h n", h=4)[:, :, 0:NC]
                    mx = sm[:, 0, 8 * t + 4 * g:8 * t + 4 * g + 4]
                    link(dve.tensor_reduce(mx, o, AX, ALU.max))
                    dve.tensor_tensor(pc[:, t, 4 * g:4 * g + 4, 0:NC], o, mx.unsqueeze(2).to_broadcast([P, 4, NC]),
                                      ALU.subtract).then_inc(s_cd, 1)
                    dve.wait_ge(s_cd, 2 * t + g + 1)
                    dve.sem_inc(free_of(name), 1)
            pcv = pc[:, :, :, :].rearrange("p t h n -> p (t h) n")[:, :, 0:NC]
            dve.wait_ge(s_ce, 1)
            for t in range(NT):
                seen = const("seen")[:, t * NC:(t + 1) * NC].unsqueeze(1).to_broadcast([P, HEADS, NC])
                link(dve.tensor_tensor(pc[:, t, :, 0:NC], pc[:, t, :, 0:NC], seen, ALU.mult))
            link(dve.tensor_reduce(sm[:, 1, :], pcv, AX, ALU.add))
            link(dve.tensor_scalar(sm[:, 1, :], sm[:, 1, :], TINY, None, ALU.max))
            link(dve.reciprocal(sm[:, 2, :], sm[:, 1, :]))
            link(dve.tensor_tensor(sm[:, 3, :].rearrange("p (t h) -> p t h", t=NT), sm[:, 2, :].rearrange("p (t h) -> p t h", t=NT),
                                   gates[:, :, :].rearrange("p t (h b) -> p t h b", b=3)[:, :, :, 0], ALU.mult))
            dve.tensor_tensor(pcv, pcv, sm[:, 3, :].unsqueeze(2).to_broadcast([P, 16, NC]), ALU.mult).then_inc(s_cp, 1)

            def unit_max(u):
                o = computed(dve, f"S{u}")
                for t, (a, b) in enumerate(spans(UNITS[u][0])):
                    link(dve.tensor_reduce(us[:, u % 3, t:t + 1], o[:, a:b], AX, ALU.max))
                dve.tensor_scalar(us[:, u % 3, 2:4], us[:, u % 3, 0:2], -SCALE, None, ALU.mult).then_inc(s_nm, 1)

            def unit_norm(u):
                kind, h, v = UNITS[u]
                taken(dve, f"S{u}")
                link(dve.reciprocal(us[:, u % 3, 6:8], us[:, u % 3, 4:6]))
                if kind == "nsa":
                    link(dve.tensor_tensor(us[:, u % 3, 6:8], us[:, u % 3, 6:8], gates[:, :, 3 * h + 1 + v], ALU.mult))
                for t, (a, b) in enumerate(spans(kind)):
                    m = dve.tensor_scalar(pbuf[:, u % 3, a:b], pbuf[:, u % 3, a:b], us[:, u % 3, 6 + t:7 + t], None, ALU.mult)
                m.then_inc(s_pr, 1)

            unit_max(0)
            unit_max(1)
            unit_norm(0)
            for u in range(NU):
                if u + 2 < NU:
                    unit_max(u + 2)
                if u + 1 < NU:
                    unit_norm(u + 1)
                for j in fillers(u):
                    taken(dve, f"mg{j}")
                    sigmoid_of_exp(sig[:, j, :])

            for q in range(4):
                for b in range(3):
                    name = f"up{b}{q}"
                    o = computed(dve, name)[:, :].rearrange("p (a t) -> p a t", a=2)
                    gate = sig[:, 8 * b + 2 * q:8 * b + 2 * q + 2, :]
                    part = merged[:, 2 * q:2 * q + 2, :]
                    dst = part if b == 0 else pbuf[:, b, :].rearrange("p (a t) -> p a t", a=2)
                    dve.tensor_tensor(dst, o, gate, ALU.mult).then_inc(free_of(name), 1)
                    taken(dve, name)
                    if b == 1:
                        link(dve.tensor_tensor(part, part, dst, ALU.add))
                    if b == 2:
                        dve.tensor_tensor(part, part, dst, ALU.add).then_inc(s_mrg, 1)

            def split_lo(n, par, i):
                if i % EXPERT_CHUNKS not in POOL_LO:
                    dve.wait_ge(e_hi, n * EXPERT_CHUNKS + (i + 1))
                    dve.tensor_tensor(wlo[:, i % SPLIT], ring_slot(par, i)[1], whi[:, i % SPLIT].bitcast(F32),
                                      ALU.subtract).then_inc(e_lo[False], 1)

            for i in range(SPLIT):
                split_lo(0, 0, i)
            dve.wait_ge(s_gffn, 16)
            for t in range(NT):
                variance(8, 5 + t, 4 + t, (t, t + 1))
                dve.scalar_tensor_tensor(h2[:, t, :], ps[:, 2 * t:2 * t + 2, :].rearrange("p b n -> p (b n)"), stat[:, 8 + t:9 + t],
                                         gffn, ALU.mult, ALU.mult).then_inc(s_h2, 1)
                for j in range(2):
                    o = computed(dve, f"hT{t}{j}")[:, :].rearrange("p (k t) -> p k t", t=P)
                    dve.tensor_copy(h2T[:, 4 * j:4 * j + 4, t * P:(t + 1) * P], o).then_inc(free_of(f"hT{t}{j}"), 1)
            for t in range(NT):
                o = computed(dve, f"lg{t}")
                dve.tensor_copy(lgt[:, t, :], o[:, 0:NE]).then_inc(free_of(f"lg{t}"), 1)
                taken(dve, f"lg{t}")
                link(dve.max(top[:, t, :], lgt[:, t, :]))
                link(dve.max_index(topi[:, t, :], top[:, t, :], lgt[:, t, :]))
                dve.tensor_scalar(ex4[:, t, 5:6], top[:, t, 0:1], -1.0, None, ALU.mult).then_inc(s_rv, 1)
                link(dve.tensor_copy(topf[:, t, :], topi[:, t, :]))
                dve.wait_ge(s_re, t + 1)
                link(dve.reciprocal(ex4[:, t, 6:7], ex4[:, t, 4:5]))
                link(dve.tensor_scalar(ex4[:, t, 0:4], ex4[:, t, 0:4], ex4[:, t, 6:7], None, ALU.mult))
                for j in range(TOPK):
                    m = dve.tensor_scalar(rt4[:, t, j, :], const("iota"), topf[:, t, j:j + 1], ex4[:, t, j:j + 1],
                                          ALU.is_equal, ALU.mult)
                link(m)
                link(dve.tensor_reduce(comb[:, t, :], rt4[:, t].rearrange("p j e -> p e j"), AX, ALU.add))
            dve.tensor_scalar(selb[:, :, :], comb[:, :, :], 0.0, None, ALU.is_gt).then_inc(s_sel, 1)
            dve.wait_ge(s_sel, 1)
            o = computed(dve, "cs")
            dve.scalar_tensor_tensor(rtm[:, :, :].rearrange("p t e -> p (t e)"), o[:, 0:NT * NE], 1.0,
                                     selb[:, :, :].rearrange("p t e -> p (t e)"), ALU.add, ALU.mult).then_inc(free_of("cs"), 1)
            taken(dve, "cs")

            def table_columns(i):
                dve.tensor_scalar(pos[:, :, NE * i:NE * (i + 1)], rtm[:, :, :], -1.0 - SLOTS * i, None, ALU.add)
                link(dve.tensor_copy(wgt[:, :, NE * i:NE * (i + 1)], comb[:, :, :]))

            table_columns(0)
            dve.sem_inc(s_over, 1)

            dve.wait_ge(s_over, 4)
            for signal in (e_trl, e_gur):
                dve.sem_inc(signal, 1)

            def make_onehot(n):
                for t in range(NT):
                    m = dve.tensor_scalar(onehot[:, t, :], const("slot")[:, 0:SLOTS], col(pos, t, n), None, ALU.is_equal)
                m.then_inc(e_oh, 1)

            def col(table, t, n):
                return table[:, t, n:n + 1] if isinstance(n, int) else table[:, t, bass.ds(n, 1)]

            def tokens_lo(n, par, bank):
                dve.wait_ge(e_gah, n + 1)
                dve.tensor_tensor(xe[:, par, :, SLOTS:P], ps[:, bank, :].rearrange("p (k s) -> p k s", s=SLOTS),
                                  xe[:, par, :, 0:SLOTS].bitcast(F32), ALU.subtract).then_inc(e_gal, 1)

            def expert(n, par, last):
                X, Y = ((4, 5), (6, 7)) if par == 0 else ((6, 7), (4, 5))
                banks = (X[0], X[1], Y[0], Y[1])

                def ahead(i):
                    if i + SPLIT < EXPERT_CHUNKS or not last:
                        split_lo(n, par, i + SPLIT)

                def both_rows(q):
                    dve.wait_ge(e_low, n * 4 + (q + 1))
                    dve.tensor_tensor((g_sb, u_sb)[q % 2][:, :], ps[0:SLOTS, banks[q], :], (glow, ulow)[q % 2][:, :],
                                      ALU.add).then_inc(e_gur, 1)
                    dve.wait_ge(e_gur, n * 4 + (q + 2))

                def gate(b):
                    both_rows(2 * b)
                    dve.tensor_scalar(g_sb[:, :], g_sb[:, :], LIMIT, None, ALU.min).then_inc(e_gm, 1)

                def up(b):
                    both_rows(2 * b + 1)
                    dve.tensor_scalar(u_sb[:, :], u_sb[:, :], LIMIT, -LIMIT, ALU.min, ALU.max).then_inc(e_dv, 1)
                    dve.wait_ge(e_gm, n * 2 + (b + 1))
                    dve.wait_ge(e_dv, n * 4 + (2 * b + 1))
                    dve.scalar_tensor_tensor(u_sb[:, :], u_sb[:, :], 1.0, g_sb[:, :], ALU.add, ALU.mult).then_inc(e_dv, 1)
                    dve.wait_ge(e_dv, n * 4 + (2 * b + 2))
                    dve.wait_ge(e_sg, n * 2 + (b + 1))
                    dve.tensor_tensor(a_sb[:, b, :], u_sb[:, :], s_sb[:, :], ALU.mult).then_inc(e_act, 1)

                def act_lo(b, bank):
                    dve.wait_ge(e_trh, n * 2 + (b + 1))
                    dve.tensor_tensor(aT[:, 4 * b:4 * b + 4, SLOTS:P], ps[:, bank, 0:4 * SLOTS].rearrange("p (k s) -> p k s", s=SLOTS),
                                      aT[:, 4 * b:4 * b + 4, 0:SLOTS].bitcast(F32), ALU.subtract).then_inc(e_trl, 1)

                dve.wait_ge(e_st, n + 1)
                for t in range(NT):
                    m = dve.tensor_scalar(gw[:, t, :], const("slot"), col(pos, t, n), col(wgt, t, n), ALU.is_equal, ALU.mult)
                m.then_inc(e_gw, 1)
                if not last:
                    dve.wait_ge(e_ga, n + 1)
                    make_onehot(n + 1)
                ahead(0)
                gate(0)
                ahead(1)
                ahead(2)
                up(0)
                ahead(3)
                ahead(4)
                dve.wait_ge(e_st, n + 2)
                act_lo(0, X[0])
                gate(1)
                if not last:
                    tokens_lo(n + 1, 1 - par, X[1])
                ahead(5)
                ahead(6)
                up(1)
                ahead(7)
                act_lo(1, Y[0])
                ahead(8)
                ahead(9)
                ahead(10)
                ahead(11)

            make_onehot(0)
            dve.memset(y_sb[:, :], 0.0).then_inc(s_init, 1)
            dve.memset(scat[:, 1, :], 0.0).then_inc(s_init, 1)
            for i in range(1, ROUNDS):
                table_columns(i)
            o = computed(dve, "cnt")
            dve.tensor_reduce(cntb[:, 0:1], o[0:1, 0:NE], AX, ALU.max).then_inc(free_of("cnt"), 1)
            taken(dve, "cnt")
            link(dve.tensor_scalar(cntb[:, 1:2], cntb[:, 0:1], float(SLOTS), None, ALU.is_gt))
            for i in range(2, ROUNDS):
                link(dve.tensor_scalar(cntb[:, 2:3], cntb[:, 0:1], float(SLOTS * i), None, ALU.is_gt))
                link(dve.tensor_tensor(cntb[:, 1:2], cntb[:, 1:2], cntb[:, 2:3], ALU.add))
            dve.tensor_copy(rounds[:, :], cntb[:, 1:2]).then_inc(s_rounds, 1)
            dve.wait_ge(s_rounds, 1)
            tokens_lo(0, 0, 5)
            more_rounds = dve.value_load(rounds[0:1, 0:1], min_val=0, max_val=ROUNDS - 1)
            with dve.Fori(0, more_rounds * (NE // 2) + (NE // 2 - 1)) as i:
                expert(i * 2, 0, False)
                expert(i * 2 + 1, 1, False)
            expert(more_rounds * NE + (NE - 2), 0, False)
            expert(more_rounds * NE + (NE - 1), 1, True)

            dve.wait_ge(s_gf, 16)
            for t in range(NT):
                variance(12, 7 + t, 6 + t, (t, t + 1))
                dve.scalar_tensor_tensor(y_out(t), ps[:, 2 * t:2 * t + 2, :].rearrange("p b n -> p (b n)"), stat[:, 12 + t:13 + t],
                                         gfin[:, :], ALU.mult, ALU.mult).then_inc(s_fin, 1)

        @block.gpsimd
        def _(pool):
            n_link = [0]

            def link(m):
                n_link[0] += 1
                m.then_inc(s_pool, 1)
                pool.wait_ge(s_pool, n_link[0])

            link(pool.memset(wpbd[0:HD, :, HD:P], 0.0))
            link(pool.memset(wpbd[HD:P, :, 0:HD], 0.0))
            for b in pb:
                link(pool.memset(b[:, :, 0:PAD], 0.0))
            pool.sem_inc(s_zeros, 1)
            arrived(pool, "q", 1)
            pool.dma_start(cstage[:, :], ins["consts"][:, NF:NCONST]).then_inc(s_cst2, 16)
            for g in range(GROUPS):
                rows = slice(HD * g, HD * g + HD)
                for i in range(2):
                    src = ins["cmp_w1"][0, i].rearrange("(l a) d e -> a d l e", a=2)[g]
                    pool.dma_start(w1[rows, i], src).then_inc(s_cmp, 16)
                for j in range(2):
                    pool.dma_start(wpbd[rows, j, rows], ins["w_pool"][0, 2 * j + g]).then_inc(s_pw, 16)
            pool.dma_start(w2[:, :, :], ins["cmp_w2"][0].rearrange("i e f -> e i f")).then_inc(s_cmp, 16)
            pool.dma_start(wrt[:, :, :], ins["w_router"][0].rearrange("(k p) e -> p k e", p=P)).then_inc(s_rt, 16)
            pool.dma_start(brt[:, :], ins["b_router"]).then_inc(s_rt, 16)

            taken(pool, "vec")
            taken(pool, "kcv")
            for i in range(2):
                for odd in range(2):
                    rows = slice(HD * odd, HD * (odd + 1))
                    for g in range(GROUPS):
                        src = kcv if g == odd else kswap
                        tok = src[rows, i, :].rearrange("p (n l a) -> p a l n", a=2, l=CMP_STRIDE // 2)[:, odd]
                        for half in range(2):
                            l = slice(8 * half, 8 * half + 8)
                            at = 32 + HALF * i
                            posn = vcol[rows, at + 8 * half:at + 8 * half + 8].unsqueeze(2).to_broadcast([HD, 8, NC])
                            m = pool.tensor_tensor(blk[rows, i, l, g], tok[:, :, half:half + NC], posn, ALU.add)
                    m.then_inc(s_blk, 1)
                    pool.wait_ge(s_blk, 2 * i + odd + 1)

            taken(pool, "pool")
            a, b, c = pb
            lo, hi = slice(0, HD), slice(HD, P)

            def doubled(dst, src, rows, blocks, shift):
                link(pool.tensor_tensor(dst[rows, blocks, PAD:], src[rows, blocks, PAD:],
                                        src[rows, blocks, PAD - shift:PAD + T - shift], ALU.add))

            doubled(b, a, slice(0, P), slice(0, 2), 1)
            doubled(c, b, slice(0, P), slice(0, 2), 2)
            doubled(b, c, slice(0, P), slice(1, 2), 4)
            doubled(c, b, hi, slice(1, 2), 8)
            pinv = const("pinv").rearrange("p (j t) -> p j t", j=2)
            pool.wait_ge(s_const, 16)
            for j in range(2):
                for rows, src in ((lo, b), (hi, c)):
                    link(pool.tensor_tensor(zt[rows, j, :], src[rows, j, PAD:], pinv[rows, j, :], ALU.mult))
            pool.tensor_tensor(zt[:, :, :], zt[:, :, :], a[:, :, PAD:], ALU.subtract).then_inc(s_z, 1)

            computed(pool, "km")
            computed(pool, "vm")
            for i in range(3):
                pool.dma_start(bsrc[NE * i:NE * (i + 1), :], ins["b_gate_up"][0]).then_inc(s_bias, 16)
            pool.dma_start(gffn, ins["norm_ffn"][0].partition_broadcast(P)).then_inc(s_gffn, 16)
            pool.dma_start(bdn[:, :], ins["b_down"][0]).then_inc(s_bdn, 16)
            pool.wait_ge(s_bias, 48)
            for i in range(3):
                for j in range(i, 3):
                    rows = slice(NE * j, NE * (j + 1))
                    link(pool.tensor_copy(bparts[rows, :], bsrc[rows, :]))
                    if j > i:
                        link(pool.tensor_tensor(bsrc[rows, :], bsrc[rows, :], bparts[rows, :], ALU.subtract))
            def lo_part(n, par, i):
                pool.wait_ge(e_hi, n * EXPERT_CHUNKS + (i + 1))
                pool.tensor_tensor(wlo[:, i % SPLIT], ring_slot(par, i)[1], whi[:, i % SPLIT].bitcast(F32),
                                   ALU.subtract).then_inc(e_lo[True], 1)

            lo_part(0, 0, POOL_LO[0])
            for part in range(2):
                for t in range(NT):
                    pool.wait_ge(s_part, NT * part + t + 1)
                    src, rest = bufM if part else bufB, bufM[:, t * D:(t + 1) * D]
                    pool.tensor_tensor(rest, src[:, t * D:(t + 1) * D], hpart[:, part, t, :], ALU.subtract).then_inc(s_rest, 1)
            pool.wait_ge(s_rest, 2 * NT)
            pool.sem_inc(s_over, 1)

            pool.wait_ge(s_over, 4)
            pool.memset(bsel[:, :, SLOTS:P], 0.0).then_inc(s_init, 1)

            def bias_row(e, par):
                e = e if isinstance(e, int) else e % NE
                src = const("b_expert")[0:96]
                pool.wait_ge(s_init, 3)
                src = src[:, e:e + 1] if isinstance(e, int) else src[:, bass.ds(e, 1)]
                pool.tensor_copy(bsel[:, par, 0:SLOTS], src.to_broadcast([96, SLOTS])).then_inc(e_bs, 1)

            bias_row(0, 0)
            pool.wait_ge(s_rounds, 1)
            more_rounds = pool.value_load(rounds[0:1, 0:1], min_val=0, max_val=ROUNDS - 1)

            def expert(n, par, last):
                for i in POOL_LO[1:]:
                    if not last:
                        pool.wait_ge(e_yc, n + 1)
                    lo_part(n, par, i)
                if not last:
                    bias_row(n + 1, 1 - par)
                    lo_part(n + 1, 1 - par, POOL_LO[0])

            with pool.Fori(0, more_rounds * (NE // 2) + (NE // 2 - 1)) as i:
                expert(i * 2, 0, False)
                expert(i * 2 + 1, 1, False)
            expert(more_rounds * NE + (NE - 2), 0, False)
            expert(more_rounds * NE + (NE - 1), 1, True)


_INS = ["x", "mem", "norm_mix", "norm_mem", "w_in", "cmp_pos", "cmp_w1", "cmp_w2", "w_pool", "pool_scale", "w_mem_kv",
        "w_up_nsa", "w_up_pool", "w_up_mem", "w_out", "norm_ffn", "w_router", "b_router", "w_gate_up", "b_gate_up",
        "w_down", "b_down", "norm_final"]


def kernel(**inputs):
    import concourse.bacc as bacc
    from concourse.bass_utils import run_bass_kernel_spmd

    nc = bacc.Bacc("TRN2", target_bir_lowering=False, num_devices=1)
    arrays = {f"in_{n}": np.ascontiguousarray(inputs[n]) for n in _INS}
    arrays["in_consts"] = constants()
    ins = {n[3:]: nc.dram_tensor(n, a.shape, mybir.dt.from_np(a.dtype), kind="ExternalInput").ap()
           for n, a in arrays.items()}
    out = nc.dram_tensor("out", (1, T, D), F32, kind="ExternalOutput").ap()
    build(nc, ins, out)
    r = run_bass_kernel_spmd(nc, [arrays], core_ids=[0])
    return r.results[0]["out"]
```
